# Optimizing a Trainium2 kernel written in Bass

```python
import math
import jax, jax.numpy as jnp
from jax import lax
import numpy as np

D_MODEL = 1024
BATCH = 1
SEQ = 256
DEPTH = 2

CHUNK = 64
DN_HEADS = 8
DN_DK = 128
DN_DV = 128
DN_WIDTH = DN_HEADS * DN_DK
CONV_K = 4
SA_HEADS = 8
SA_HD = 128
SA_WIDTH = SA_HEADS * SA_HD
IDX_HEADS = 8
IDX_HD = 64
TOPK_MAX = 256
Q_BLOCK = 128
XA_HEADS = 4
XA_HD = 256
XA_WIDTH = XA_HEADS * XA_HD
N_MEM = 256
ROPE_THETA = 500000.0
ROPE_DIV = 4
D_FF = ((8 * D_MODEL // 3 + 255) // 256) * 256
N_BRANCH = 3
NORM_EPS = 1e-6

IN_SIZES = (DN_WIDTH, DN_WIDTH, DN_HEADS * DN_DV, DN_HEADS * DN_DV, DN_HEADS, DN_HEADS,
            SA_WIDTH, SA_WIDTH, SA_WIDTH, IDX_HEADS * IDX_HD, IDX_HD, IDX_HEADS,
            XA_WIDTH, N_BRANCH * D_MODEL)
N_IN = sum(IN_SIZES)


def rmsnorm(x, g):
    xf = x.astype(jnp.float32)
    y = xf * lax.rsqrt(jnp.mean(xf * xf, axis=-1, keepdims=True) + NORM_EPS)
    return (y * g.astype(jnp.float32)).astype(x.dtype)

def l2norm(x):
    return x * lax.rsqrt(jnp.sum(x * x, axis=-1, keepdims=True) + NORM_EPS)

def rope_partial(x, positions):
    rd = x.shape[-1] // ROPE_DIV
    half = rd // 2
    inv_freq = ROPE_THETA ** (-(jnp.arange(half, dtype=jnp.float32) * 2.0 / rd))
    ang = positions.astype(jnp.float32)[..., None] * inv_freq
    cos = jnp.cos(ang)[:, :, None, :]
    sin = jnp.sin(ang)[:, :, None, :]
    xr = x[..., :rd].astype(jnp.float32)
    x1, x2 = xr[..., :half], xr[..., half:]
    rot = jnp.concatenate([x1 * cos - x2 * sin, x2 * cos + x1 * sin], axis=-1)
    return jnp.concatenate([rot.astype(x.dtype), x[..., rd:]], axis=-1)

def causal_conv(x, w):
    c = x.shape[-1]
    return lax.conv_general_dilated(x, w[:, None, :], window_strides=(1,),
                                    padding=[(CONV_K - 1, 0)],
                                    dimension_numbers=('NWC', 'WIO', 'NWC'),
                                    feature_group_count=c)

def gated_delta_rule(q, k, v, beta, g):
    b, s, h, dk = q.shape
    dv = v.shape[-1]
    n = s // CHUNK

    def chunks(t):
        return jnp.moveaxis(t.reshape((b, n, CHUNK) + t.shape[2:]), 2, 3)

    qc, kc, vc, bc, gc = (chunks(t) for t in (q, k, v, beta, g))
    gc = jnp.cumsum(gc, axis=-1)
    pos = jnp.arange(CHUNK)
    incl = pos[:, None] >= pos[None, :]
    strict = pos[:, None] > pos[None, :]
    diff = gc[..., :, None] - gc[..., None, :]
    decay = jnp.where(incl, jnp.exp(jnp.where(incl, diff, 0.0)), 0.0)
    kb = kc * bc[..., None]
    m = jnp.where(strict, jnp.einsum('bnhid,bnhjd->bnhij', kb, kc) * decay, 0.0)
    rhs = jnp.concatenate([vc * bc[..., None], kb * jnp.exp(gc)[..., None]], axis=-1)
    sol = lax.linalg.triangular_solve(m, rhs, left_side=True, lower=True, unit_diagonal=True)
    u, w = sol[..., :dv], sol[..., dv:]
    a_qk = jnp.einsum('bnhid,bnhjd->bnhij', qc, kc) * decay
    q_dec = qc * jnp.exp(gc)[..., None]
    g_last = gc[..., -1]
    k_dec = kc * jnp.exp(g_last[..., None] - gc)[..., None]
    c_dec = jnp.exp(g_last)

    def step(state, xs):
        qd, kd, a, uu, ww, cd = xs
        v_new = uu - jnp.einsum('bhck,bhkv->bhcv', ww, state)
        o = jnp.einsum('bhck,bhkv->bhcv', qd, state) + jnp.einsum('bhij,bhjv->bhiv', a, v_new)
        state = state * cd[..., None, None] + jnp.einsum('bhck,bhcv->bhkv', kd, v_new)
        return state, o

    xs = tuple(jnp.moveaxis(t, 1, 0) for t in (q_dec, k_dec, a_qk, u, w, c_dec))
    s0 = jnp.zeros((b, h, dk, dv), jnp.float32)
    _, o = lax.scan(step, s0, xs)
    return jnp.swapaxes(jnp.moveaxis(o, 0, 1), 2, 3).reshape(b, s, h, dv)

def deltanet_branch(q_in, k_in, v_in, z_in, b_in, a_in, conv_w, a_log, dt_bias, dn_norm):
    b, s, _ = q_in.shape
    f32 = jnp.float32
    qkv = jax.nn.silu(causal_conv(jnp.concatenate([q_in, k_in, v_in], axis=-1), conv_w))
    q, k, v = jnp.split(qkv, [DN_WIDTH, 2 * DN_WIDTH], axis=-1)
    q = l2norm(q.reshape(b, s, DN_HEADS, DN_DK).astype(f32)) * DN_DK ** -0.5
    k = l2norm(k.reshape(b, s, DN_HEADS, DN_DK).astype(f32))
    v = v.reshape(b, s, DN_HEADS, DN_DV).astype(f32)
    beta = jax.nn.sigmoid(b_in.astype(f32))
    g = -jnp.exp(a_log.astype(f32)) * jax.nn.softplus(a_in.astype(f32) + dt_bias.astype(f32))
    o = gated_delta_rule(q, k, v, beta, g)
    z = z_in.reshape(b, s, DN_HEADS, DN_DV).astype(f32)
    o = rmsnorm(o, dn_norm) * jax.nn.silu(z)
    return o.reshape(b, s, DN_WIDTH).astype(q_in.dtype)

def dsa_branch(q_in, k_in, v_in, iq_in, ik_in, iw_in, positions):
    b, s, _ = q_in.shape
    f32 = jnp.float32
    q = rope_partial(q_in.reshape(b, s, SA_HEADS, SA_HD), positions)
    k = rope_partial(k_in.reshape(b, s, SA_HEADS, SA_HD), positions)
    v = v_in.reshape(b, s, SA_HEADS, SA_HD)
    iq = rope_partial(iq_in.reshape(b, s, IDX_HEADS, IDX_HD), positions).astype(f32)
    ik = rope_partial(ik_in.reshape(b, s, 1, IDX_HD), positions)[:, :, 0].astype(f32)
    iw = iw_in.astype(f32) * (IDX_HEADS ** -0.5 * IDX_HD ** -0.5)
    k_sel = min(TOPK_MAX, s // 4)
    nb = s // Q_BLOCK
    key_chunk = jnp.arange(s) // CHUNK

    def blocks(t):
        return jnp.moveaxis(t.reshape((b, nb, Q_BLOCK) + t.shape[2:]), 1, 0)

    def attend(xs):
        qb, iqb, iwb, blk = xs
        q_chunk = (blk * Q_BLOCK + jnp.arange(Q_BLOCK)) // CHUNK
        score = jax.nn.relu(jnp.einsum('bthd,bsd->bths', iqb, ik))
        score = jnp.einsum('bths,bth->bts', score, iwb)
        admissible = key_chunk[None, :] <= q_chunk[:, None]
        score = jnp.where(admissible[None], score, -jnp.inf)
        _, sel = lax.top_k(score, k_sel)
        valid = (sel // CHUNK) <= q_chunk[None, :, None]
        kg = jax.vmap(lambda a, i: a[i])(k, sel)
        vg = jax.vmap(lambda a, i: a[i])(v, sel)
        logits = jnp.einsum('bthd,btkhd->bthk', qb, kg).astype(f32) * SA_HD ** -0.5
        logits = jnp.where(valid[:, :, None, :], logits, -jnp.inf)
        p = jax.nn.softmax(logits, axis=-1).astype(vg.dtype)
        return jnp.einsum('bthk,btkhd->bthd', p, vg)

    o = lax.map(attend, (blocks(q), blocks(iq), blocks(iw), jnp.arange(nb, dtype=jnp.int32)))
    return jnp.moveaxis(o, 0, 1).reshape(b, s, SA_WIDTH)

def memory_branch(q_in, mem_n, w_mem_kv):
    b, s, _ = q_in.shape
    m = mem_n.shape[1]
    mk, mv = jnp.split(mem_n @ w_mem_kv, 2, axis=-1)
    q = q_in.reshape(b, s, XA_HEADS, XA_HD)
    mk = mk.reshape(b, m, XA_HEADS, XA_HD)
    mv = mv.reshape(b, m, XA_HEADS, XA_HD)
    logits = jnp.einsum('bshd,bmhd->bhsm', q, mk).astype(jnp.float32) * XA_HD ** -0.5
    p = jax.nn.softmax(logits, axis=-1).astype(mv.dtype)
    return jnp.einsum('bhsm,bmhd->bshd', p, mv).reshape(b, s, XA_WIDTH)

def first_inputs(seed: int = 0) -> dict:
    key = jax.random.key(seed)
    ks = jax.random.split(key, 20)
    f32 = jnp.float32

    def nrm(k, shape, fan_in):
        return jax.random.normal(k, shape, f32) * fan_in ** -0.5

    def gain(k, shape):
        return 1.0 + 0.02 * jax.random.normal(k, shape, f32)

    x = jax.random.normal(ks[0], (BATCH, SEQ, D_MODEL), f32)
    mem = jax.random.normal(ks[1], (BATCH, N_MEM, D_MODEL), f32)
    offset = jax.random.randint(ks[2], (BATCH, 1), 0, 64, dtype=jnp.int32) * CHUNK
    positions = (offset + jnp.arange(SEQ, dtype=jnp.int32)[None, :]).astype(jnp.int32)
    dt = jnp.exp(jax.random.uniform(ks[3], (DEPTH, DN_HEADS), f32, math.log(1e-3), math.log(1e-1)))
    return {
        'x': x,
        'mem': mem,
        'positions': positions,
        'norm_mix': gain(ks[4], (DEPTH, D_MODEL)),
        'norm_mem': gain(ks[5], (DEPTH, D_MODEL)),
        'w_in': nrm(ks[6], (DEPTH, D_MODEL, N_IN), D_MODEL),
        'b_gate': 0.1 * jax.random.normal(ks[7], (DEPTH, N_BRANCH, D_MODEL), f32),
        'conv_w': nrm(ks[8], (DEPTH, CONV_K, 3 * DN_WIDTH), CONV_K),
        'a_log': jnp.log(jax.random.uniform(ks[9], (DEPTH, DN_HEADS), f32, 1.0, 16.0)),
        'dt_bias': jnp.log(jnp.expm1(dt)),
        'dn_norm': gain(ks[10], (DEPTH, DN_DV)),
        'w_mem_kv': nrm(ks[11], (DEPTH, D_MODEL, 2 * XA_WIDTH), D_MODEL),
        'w_branch': nrm(ks[12], (DEPTH, N_BRANCH, DN_WIDTH, D_MODEL), DN_WIDTH),
        'w_out': nrm(ks[13], (DEPTH, D_MODEL, D_MODEL), D_MODEL),
        'norm_ffn': gain(ks[14], (DEPTH, D_MODEL)),
        'w_ffn_in': nrm(ks[15], (DEPTH, D_MODEL, 2 * D_FF), D_MODEL),
        'w_ffn_out': nrm(ks[16], (DEPTH, D_FF, D_MODEL), D_FF),
        'norm_final': gain(ks[17], (D_MODEL,)),
    }

def first_block(x, mem, positions, norm_mix, norm_mem, w_in, b_gate, conv_w, a_log, dt_bias,
              dn_norm, w_mem_kv, w_branch, w_out, norm_ffn, w_ffn_in, w_ffn_out, norm_final):
    b, s, d = x.shape
    split_pts = []
    acc = 0
    for size in IN_SIZES[:-1]:
        acc += size
        split_pts.append(acc)
    for l in range(DEPTH):
        h = rmsnorm(x, norm_mix[l])
        (dq, dk, dv, dz, db, da, sq, sk, sv, iq, ik, iw, xq, gl) = jnp.split(h @ w_in[l], split_pts, axis=-1)
        o_dn = deltanet_branch(dq, dk, dv, dz, db, da, conv_w[l], a_log[l], dt_bias[l], dn_norm[l])
        o_sa = dsa_branch(sq, sk, sv, iq, ik, iw, positions)
        o_xa = memory_branch(xq, rmsnorm(mem, norm_mem[l]), w_mem_kv[l])
        gates = jax.nn.sigmoid((gl.reshape(b, s, N_BRANCH, d) + b_gate[l]).astype(jnp.float32)).astype(x.dtype)
        merged = (gates[:, :, 0] * (o_dn @ w_branch[l, 0])
                  + gates[:, :, 1] * (o_sa @ w_branch[l, 1])
                  + gates[:, :, 2] * (o_xa @ w_branch[l, 2]))
        x = x + merged @ w_out[l]
        h = rmsnorm(x, norm_ffn[l])
        gt, up = jnp.split(h @ w_ffn_in[l], 2, axis=-1)
        x = x + (jax.nn.silu(gt) * up) @ w_ffn_out[l]
    return rmsnorm(x, norm_final)


GRID_W = 64
CTX_LEN = 256
N_EVEN = (DEPTH + 1) // 2
N_ODD = DEPTH // 2
N_MOD = 6
EPS = 1e-6
ROPE_BASE = 10000.0

POOL_WINDOWS = (2, 4, 8, 16)
POOL_GROUP = D_MODEL // 16
POOL_WIDTH = POOL_GROUP * len(POOL_WINDOWS)
DIFF_HEAD_DIM = 64
DIFF_V_DIM = 2 * DIFF_HEAD_DIM
DIFF_HEADS = (D_MODEL - POOL_WIDTH) // DIFF_V_DIM
DIFF_QK_WIDTH = DIFF_HEADS * 2 * DIFF_HEAD_DIM
DIFF_V_WIDTH = DIFF_HEADS * DIFF_V_DIM
EVEN_IN_WIDTH = POOL_WIDTH + 2 * DIFF_QK_WIDTH + DIFF_V_WIDTH
EVEN_MIX_WIDTH = POOL_WIDTH + DIFF_V_WIDTH
MLA_HEADS = D_MODEL // 128
MLA_NOPE = 128
MLA_ROPE = 64
MLA_V = 128
MLA_Q_RANK = D_MODEL // 2
MLA_KV_RANK = D_MODEL // 4
ODD_IN_WIDTH = MLA_Q_RANK + MLA_KV_RANK + MLA_ROPE
MLA_MIX_WIDTH = MLA_HEADS * MLA_V
FFN_HIDDEN = ((8 * D_MODEL // 3 + 255) // 256) * 256
N_EXPERTS = 8
TOP_K = 2


F32 = jnp.float32

def rmsnorm_2(h, g=None):
    hf = h.astype(F32)
    y = hf * lax.rsqrt(jnp.mean(hf * hf, axis=-1, keepdims=True) + EPS)
    if g is not None:
        y = y * g.astype(F32)
    return y.astype(h.dtype)

def adaln(cond, w, b):
    return jax.nn.silu(cond) @ w + b

def modulate(h, shift, scale):
    return h * (1.0 + scale) + shift

def axial_rope_tables(rows, dim):
    t = jnp.arange(rows * GRID_W, dtype=jnp.int32)
    row = (t // GRID_W).astype(F32)
    col = (t % GRID_W).astype(F32)
    quarter = dim // 4
    inv = ROPE_BASE ** (-jnp.arange(quarter, dtype=F32) / quarter)
    ar = row[:, None] * inv[None, :]
    ac = col[:, None] * inv[None, :]
    cos = jnp.concatenate([jnp.cos(ar), jnp.cos(ar), jnp.cos(ac), jnp.cos(ac)], axis=-1)
    sin = jnp.concatenate([jnp.sin(ar), jnp.sin(ar), jnp.sin(ac), jnp.sin(ac)], axis=-1)
    return cos, sin

def apply_axial_rope(u, cos, sin):
    u1, u2, u3, u4 = jnp.split(u, 4, axis=-1)
    rot = jnp.concatenate([-u2, u1, -u4, u3], axis=-1)
    return (u.astype(F32) * cos + rot.astype(F32) * sin).astype(u.dtype)

def sweep_query_blocks(fn, qs):
    b, l = qs[0].shape[:2]
    nb = l // Q_BLOCK
    blocked = tuple(jnp.moveaxis(q.reshape((b, nb, Q_BLOCK) + q.shape[2:]), 1, 0) for q in qs)
    out = lax.map(lambda qb: fn(*qb), blocked)
    return jnp.moveaxis(out, 0, 1).reshape((b, l) + out.shape[3:])

def softmax_attn_block(q, k, v, scale):
    s = jnp.einsum('bqhd,bkhd->bhqk', q, k).astype(F32) * scale
    p = jax.nn.softmax(s, axis=-1)
    return jnp.einsum('bhqk,bkhe->bqhe', p.astype(v.dtype), v)

def diff_attn_block(q1, q2, k1, k2, v, lam):
    scale = DIFF_HEAD_DIM ** -0.5
    s1 = jnp.einsum('bqhd,bkhd->bhqk', q1, k1).astype(F32) * scale
    s2 = jnp.einsum('bqhd,bkhd->bhqk', q2, k2).astype(F32) * scale
    a = jax.nn.softmax(s1, axis=-1) - lam * jax.nn.softmax(s2, axis=-1)
    return jnp.einsum('bhqk,bkhe->bqhe', a.astype(v.dtype), v)

def multiscale_pool(u, pool_w, pool_scale):
    b, l, _ = u.shape
    uf = u.astype(F32)
    cs = jnp.concatenate([jnp.zeros((b, 1, POOL_WIDTH), F32), jnp.cumsum(uf, axis=1)], axis=1)
    t = jnp.arange(l)
    outs = []
    for g, w in enumerate(POOL_WINDOWS):
        lo = jnp.clip(t - w // 2, 0, l)
        hi = jnp.clip(t + w // 2, 0, l)
        sl = slice(g * POOL_GROUP, (g + 1) * POOL_GROUP)
        csg = cs[:, :, sl]
        s = jnp.take(csg, hi, axis=1) - jnp.take(csg, lo, axis=1)
        cnt = (hi - lo).astype(F32)[None, :, None]
        outs.append(s / cnt - uf[:, :, sl])
    p = jnp.stack(outs, axis=2).astype(u.dtype)
    y = jnp.einsum('blgc,gcd->blgd', p, pool_w).reshape(b, l, POOL_WIDTH)
    return y * pool_scale

def split_even(z):
    n = z.shape[:2]
    o = POOL_WIDTH
    p = z[..., :o]
    q = z[..., o:o + DIFF_QK_WIDTH].reshape(n + (DIFF_HEADS, 2, DIFF_HEAD_DIM))
    k = z[..., o + DIFF_QK_WIDTH:o + 2 * DIFF_QK_WIDTH].reshape(n + (DIFF_HEADS, 2, DIFF_HEAD_DIM))
    v = z[..., o + 2 * DIFF_QK_WIDTH:].reshape(n + (DIFF_HEADS, DIFF_V_DIM))
    return p, q, k, v

def even_merge(p, attn, pool_w, pool_scale, w_out, lam_init):
    b, l = p.shape[:2]
    pooled = multiscale_pool(p, pool_w, pool_scale)
    heads = (rmsnorm_2(attn) * (1.0 - lam_init)).reshape(b, l, DIFF_V_WIDTH)
    return jnp.concatenate([pooled, heads], axis=-1) @ w_out

def even_mixer(a_lat, a_ctx, w_in, pool_w, pool_scale, lq1, lk1, lq2, lk2, w_out,
               cos, sin, lam_init, need_ctx):
    p_lat, q_lat, k_lat, v_lat = split_even(a_lat @ w_in)
    p_ctx, q_ctx, k_ctx, v_ctx = split_even(a_ctx @ w_in)
    cs, sn = cos[None, :, None, None, :], sin[None, :, None, None, :]
    q_lat = apply_axial_rope(q_lat, cs, sn)
    k_lat = apply_axial_rope(k_lat, cs, sn)
    lam = (jnp.exp(jnp.sum(lq1.astype(F32) * lk1.astype(F32)))
           - jnp.exp(jnp.sum(lq2.astype(F32) * lk2.astype(F32))) + lam_init)
    k_all = jnp.concatenate([k_lat, k_ctx], axis=1)
    v_all = jnp.concatenate([v_lat, v_ctx], axis=1)
    k1, k2 = k_all[..., 0, :], k_all[..., 1, :]
    attn_lat = sweep_query_blocks(
        lambda b1, b2: diff_attn_block(b1, b2, k1, k2, v_all, lam),
        (q_lat[..., 0, :], q_lat[..., 1, :]))
    y_lat = even_merge(p_lat, attn_lat, pool_w, pool_scale, w_out, lam_init)
    y_ctx = None
    if need_ctx:
        attn_ctx = diff_attn_block(q_ctx[..., 0, :], q_ctx[..., 1, :],
                                   k_ctx[..., 0, :], k_ctx[..., 1, :], v_ctx, lam)
        y_ctx = even_merge(p_ctx, attn_ctx, pool_w, pool_scale, w_out, lam_init)
    return y_lat, y_ctx

def odd_mixer(a_lat, a_ctx, w_in, q_norm_g, kv_norm_g, w_uq, w_ukv, w_out, cos, sin, need_ctx):
    z_lat = a_lat @ w_in
    z_ctx = a_ctx @ w_in

    def queries(z):
        cq = rmsnorm_2(z[..., :MLA_Q_RANK], q_norm_g)
        return (cq @ w_uq).reshape(z.shape[:2] + (MLA_HEADS, MLA_NOPE + MLA_ROPE))

    def keys_values(z):
        ckv = rmsnorm_2(z[..., MLA_Q_RANK:MLA_Q_RANK + MLA_KV_RANK], kv_norm_g)
        kv = (ckv @ w_ukv).reshape(z.shape[:2] + (MLA_HEADS, MLA_NOPE + MLA_V))
        return kv[..., :MLA_NOPE], kv[..., MLA_NOPE:], z[..., MLA_Q_RANK + MLA_KV_RANK:]

    def full_keys(k_nope, k_rope):
        shared = jnp.broadcast_to(k_rope[:, :, None, :], k_nope.shape[:3] + (MLA_ROPE,))
        return jnp.concatenate([k_nope, shared], axis=-1)

    q_lat = queries(z_lat)
    q_lat = jnp.concatenate(
        [q_lat[..., :MLA_NOPE],
         apply_axial_rope(q_lat[..., MLA_NOPE:], cos[None, :, None, :], sin[None, :, None, :])],
        axis=-1)
    kn_lat, v_lat, kr_lat = keys_values(z_lat)
    kr_lat = apply_axial_rope(kr_lat, cos[None], sin[None])
    kn_ctx, v_ctx, kr_ctx = keys_values(z_ctx)
    k_ctx = full_keys(kn_ctx, kr_ctx)
    k_all = jnp.concatenate([full_keys(kn_lat, kr_lat), k_ctx], axis=1)
    v_all = jnp.concatenate([v_lat, v_ctx], axis=1)
    scale = (MLA_NOPE + MLA_ROPE) ** -0.5
    b, l = a_lat.shape[:2]
    o_lat = sweep_query_blocks(lambda qb: softmax_attn_block(qb, k_all, v_all, scale), (q_lat,))
    y_lat = o_lat.reshape(b, l, MLA_MIX_WIDTH) @ w_out
    y_ctx = None
    if need_ctx:
        o_ctx = softmax_attn_block(queries(z_ctx), k_ctx, v_ctx, scale)
        y_ctx = o_ctx.reshape(a_ctx.shape[:2] + (MLA_MIX_WIDTH,)) @ w_out
    return y_lat, y_ctx

def swiglu(h, w_gate, w_up, w_down):
    return (jax.nn.silu(h @ w_gate) * (h @ w_up)) @ w_down

def moe_swiglu(h, router_w, w_gate, w_up, w_down):
    b, l, d = h.shape
    tok = h.reshape(-1, d)
    n = tok.shape[0]
    probs = jax.nn.softmax((tok @ router_w).astype(F32), axis=-1)
    top_p, top_e = lax.top_k(probs, TOP_K)
    top_p = top_p / jnp.sum(top_p, axis=-1, keepdims=True)
    flat_e = top_e.reshape(-1)
    order = jnp.argsort(flat_e)
    tok_idx = order // TOP_K
    xs = tok[tok_idx]
    group_sizes = jnp.bincount(flat_e, length=N_EXPERTS).astype(jnp.int32)
    hg = lax.ragged_dot(xs, w_gate, group_sizes)
    hu = lax.ragged_dot(xs, w_up, group_sizes)
    ys = lax.ragged_dot(jax.nn.silu(hg) * hu, w_down, group_sizes)
    wts = top_p.reshape(-1)[order].astype(ys.dtype)
    out = jax.ops.segment_sum(ys * wts[:, None], tok_idx, num_segments=n)
    return out.reshape(b, l, d)

def second_inputs(seed: int = 0) -> dict:
    key = jax.random.key(seed)
    ks = iter(jax.random.split(key, 48))
    D = D_MODEL
    F = FFN_HIDDEN

    def nrm(shape, s):
        return jax.random.normal(next(ks), shape, jnp.float32) * s

    return {
        "x": nrm((BATCH, SEQ, D), 1.0),
        "c": nrm((BATCH, D), 1.0),
        "ctx": nrm((BATCH, CTX_LEN, D), 1.0),
        "c_ctx": nrm((D,), 1.0),
        "norm1_g": 1.0 + nrm((DEPTH, D), 0.1),
        "norm2_g": 1.0 + nrm((DEPTH, D), 0.1),
        "mod_w": nrm((DEPTH, D, N_MOD * D), 0.5 * D ** -0.5),
        "mod_b": nrm((DEPTH, N_MOD * D), 0.01),
        "even_w_in": nrm((N_EVEN, D, EVEN_IN_WIDTH), D ** -0.5),
        "pool_w": nrm((N_EVEN, len(POOL_WINDOWS), POOL_GROUP, POOL_GROUP), POOL_GROUP ** -0.5),
        "pool_scale": 1.0 + nrm((N_EVEN, POOL_WIDTH), 0.1),
        "lambda_q1": nrm((N_EVEN, DIFF_HEAD_DIM), 0.1),
        "lambda_k1": nrm((N_EVEN, DIFF_HEAD_DIM), 0.1),
        "lambda_q2": nrm((N_EVEN, DIFF_HEAD_DIM), 0.1),
        "lambda_k2": nrm((N_EVEN, DIFF_HEAD_DIM), 0.1),
        "even_w_out": nrm((N_EVEN, EVEN_MIX_WIDTH, D), EVEN_MIX_WIDTH ** -0.5),
        "ffn_w_gate": nrm((N_EVEN, D, F), D ** -0.5),
        "ffn_w_up": nrm((N_EVEN, D, F), D ** -0.5),
        "ffn_w_down": nrm((N_EVEN, F, D), F ** -0.5),
        "odd_w_in": nrm((N_ODD, D, ODD_IN_WIDTH), D ** -0.5),
        "q_norm_g": 1.0 + nrm((N_ODD, MLA_Q_RANK), 0.1),
        "kv_norm_g": 1.0 + nrm((N_ODD, MLA_KV_RANK), 0.1),
        "w_uq": nrm((N_ODD, MLA_Q_RANK, MLA_HEADS * (MLA_NOPE + MLA_ROPE)), MLA_Q_RANK ** -0.5),
        "w_ukv": nrm((N_ODD, MLA_KV_RANK, MLA_HEADS * (MLA_NOPE + MLA_V)), MLA_KV_RANK ** -0.5),
        "odd_w_out": nrm((N_ODD, MLA_MIX_WIDTH, D), MLA_MIX_WIDTH ** -0.5),
        "router_w": nrm((N_ODD, D, N_EXPERTS), D ** -0.5),
        "moe_w_gate": nrm((N_ODD, N_EXPERTS, D, F), D ** -0.5),
        "moe_w_up": nrm((N_ODD, N_EXPERTS, D, F), D ** -0.5),
        "moe_w_down": nrm((N_ODD, N_EXPERTS, F, D), F ** -0.5),
        "final_norm_g": 1.0 + nrm((D,), 0.1),
    }

def second_block(x, c, ctx, c_ctx, norm1_g, norm2_g, mod_w, mod_b, even_w_in, pool_w, pool_scale,
              lambda_q1, lambda_k1, lambda_q2, lambda_k2, even_w_out, ffn_w_gate, ffn_w_up,
              ffn_w_down, odd_w_in, q_norm_g, kv_norm_g, w_uq, w_ukv, odd_w_out, router_w,
              moe_w_gate, moe_w_up, moe_w_down, final_norm_g):
    rows = x.shape[1] // GRID_W
    cos_d, sin_d = axial_rope_tables(rows, DIFF_HEAD_DIM)
    cos_m, sin_m = axial_rope_tables(rows, MLA_ROPE)
    h_lat, h_ctx = x, ctx
    for i in range(DEPTH):
        need_ctx = i < DEPTH - 1
        j = i // 2
        mod_lat = adaln(c, mod_w[i], mod_b[i])[:, None, :]
        mod_ctx = adaln(c_ctx, mod_w[i], mod_b[i])[None, None, :]
        sh1, sc1, g1, sh2, sc2, g2 = jnp.split(mod_lat, N_MOD, axis=-1)
        csh1, csc1, cg1, csh2, csc2, cg2 = jnp.split(mod_ctx, N_MOD, axis=-1)
        a_lat = modulate(rmsnorm_2(h_lat, norm1_g[i]), sh1, sc1)
        a_ctx = modulate(rmsnorm_2(h_ctx, norm1_g[i]), csh1, csc1)
        if i % 2 == 0:
            lam_init = 0.8 - 0.6 * math.exp(-0.3 * i)
            y_lat, y_ctx = even_mixer(a_lat, a_ctx, even_w_in[j], pool_w[j], pool_scale[j],
                                      lambda_q1[j], lambda_k1[j], lambda_q2[j], lambda_k2[j],
                                      even_w_out[j], cos_d, sin_d, lam_init, need_ctx)
            ffn = lambda h: swiglu(h, ffn_w_gate[j], ffn_w_up[j], ffn_w_down[j])
        else:
            y_lat, y_ctx = odd_mixer(a_lat, a_ctx, odd_w_in[j], q_norm_g[j], kv_norm_g[j],
                                     w_uq[j], w_ukv[j], odd_w_out[j], cos_m, sin_m, need_ctx)
            ffn = lambda h: moe_swiglu(h, router_w[j], moe_w_gate[j], moe_w_up[j], moe_w_down[j])
        h_lat = h_lat + g1 * y_lat
        h_lat = h_lat + g2 * ffn(modulate(rmsnorm_2(h_lat, norm2_g[i]), sh2, sc2))
        if need_ctx:
            h_ctx = h_ctx + cg1 * y_ctx
            h_ctx = h_ctx + cg2 * ffn(modulate(rmsnorm_2(h_ctx, norm2_g[i]), csh2, csc2))
    return rmsnorm_2(h_lat, final_norm_g)


def setup_inputs(seed=0):
    out = dict(first_inputs(seed))
    for name, value in second_inputs(seed + 1).items():
        if name != "x":
            out[name + "_2"] = value
    return out


def reference(
    x, mem, positions, norm_mix, norm_mem, w_in, b_gate, conv_w, a_log, dt_bias, dn_norm,
    w_mem_kv, w_branch, w_out, norm_ffn, w_ffn_in, w_ffn_out, norm_final, c_2, ctx_2, c_ctx_2,
    norm1_g_2, norm2_g_2, mod_w_2, mod_b_2, even_w_in_2, pool_w_2, pool_scale_2, lambda_q1_2,
    lambda_k1_2, lambda_q2_2, lambda_k2_2, even_w_out_2, ffn_w_gate_2, ffn_w_up_2, ffn_w_down_2,
    odd_w_in_2, q_norm_g_2, kv_norm_g_2, w_uq_2, w_ukv_2, odd_w_out_2, router_w_2, moe_w_gate_2,
    moe_w_up_2, moe_w_down_2, final_norm_g_2,
):
    x = first_block(
        x, mem, positions, norm_mix, norm_mem, w_in, b_gate, conv_w, a_log, dt_bias, dn_norm,
        w_mem_kv, w_branch, w_out, norm_ffn, w_ffn_in, w_ffn_out, norm_final,
    )
    return second_block(
        x, c_2, ctx_2, c_ctx_2, norm1_g_2, norm2_g_2, mod_w_2, mod_b_2, even_w_in_2, pool_w_2,
        pool_scale_2, lambda_q1_2, lambda_k1_2, lambda_q2_2, lambda_k2_2, even_w_out_2,
        ffn_w_gate_2, ffn_w_up_2, ffn_w_down_2, odd_w_in_2, q_norm_g_2, kv_norm_g_2, w_uq_2,
        w_ukv_2, odd_w_out_2, router_w_2, moe_w_gate_2, moe_w_up_2, moe_w_down_2,
        final_norm_g_2,
    )


_drawn_inputs = setup_inputs


def setup_inputs(seed=0):
    import zlib

    import numpy as np

    out = dict(_drawn_inputs(seed))
    spreads = {}
    factors = {'norm_mem': 5.749,
     'dn_norm': 3.416,
     'mod_b_2': 2.856,
     'pool_scale_2': 2.674,
     'q_norm_g_2': 5.73,
     'kv_norm_g_2': 4.273}
    for name, (base, spread) in spreads.items():
        noise = np.random.default_rng([zlib.crc32(name.encode()), seed]).standard_normal(out[name].shape)
        drawn = base * np.exp(spread * noise) if base else spread * noise
        out[name] = __import__('jax').numpy.asarray(drawn.astype(out[name].dtype))
    for name, factor in factors.items():
        out[name] = (out[name] * factor).astype(out[name].dtype)
    return out
```

```python
import math
from contextlib import ExitStack

import numpy as np
import concourse.bass as bass
from concourse import mybir

F32 = mybir.dt.float32
I32 = mybir.dt.int32
ACT = mybir.ActivationFunctionType
ALU = mybir.AluOpType
AXX = mybir.AxisListType.X

P = 128
D = 1024
KT = D // P
T = 256
NP2 = T // P
DEPTH = 2
CHUNK = 64
NCH = T // CHUNK
DNH = 8
SAH = 8
XAH = 4
TOPK = T // 4
F_HID = 2816
FT = F_HID // P
NE = 8
DH = 6
MH = 8
EPS = 1e-6
NEG = -1e30
TAKEN = -3e38
RING = 6
BANKS = 8
SLAB = KT * P
TWO_PI_PARTS = (6.28125, 0.0019350051879882812, 3.019916e-07)
ROUND = 12582912.0
LAM_INIT = 0.8 - 0.6 * math.exp(0.0)


def rotation(pairs):
    r = np.zeros((P, P), np.float32)
    for out_row, in_row, sign in pairs:
        r[in_row, out_row] = sign
    return r


def make_consts():
    i = np.arange(P)
    same = (i[:, None] // CHUNK) == (i[None, :] // CHUNK)
    c = {}
    c["ident"] = np.eye(P, dtype=np.float32)
    c["ones"] = np.ones((P, P), np.float32)
    c["upto"] = ((i[:, None] <= i[None, :]) & same).astype(np.float32)
    c["after"] = ((i[:, None] > i[None, :]) & same).astype(np.float32)
    for n in range(2):
        c[f"chunk{n}"] = np.repeat((i // CHUNK == n).astype(np.float32)[:, None], P, 1)
    c["strict"] = ((i[:, None] > i[None, :]) & same).astype(np.float32)
    c["incl"] = ((i[:, None] <= i[None, :]) & same).astype(np.float32)
    for k in range(6):
        b = 1 << k
        c[f"merge{k}"] = ((i[:, None] // (2 * b) == i[None, :] // (2 * b))
                          & (i[:, None] % (2 * b) >= b) & (i[None, :] % (2 * b) < b)).astype(np.float32)
    c["rot_sa"] = rotation([(r, r + 16, -1.0) for r in range(16)] + [(r + 16, r, 1.0) for r in range(16)])
    ri = rotation([(b + r, b + r + 8, -1.0) for b in (0, 64) for r in range(8)]
                  + [(b + r + 8, b + r, 1.0) for b in (0, 64) for r in range(8)])
    c["rot_ix"] = ri
    dup = np.zeros((P, P), np.float32)
    for m in range(P):
        dup[m % 64, m] = 1.0
    c["dup"] = dup
    duprot = np.zeros((P, P), np.float32)
    for m in range(P):
        duprot[:64, m] = ri[:64, m % 64]
    c["dup_rot"] = duprot
    invf = np.zeros((P, 2), np.float32)
    for r in range(32):
        invf[r, 0] = 500000.0 ** (-((r % 16) * 2.0 / 32))
    for r in range(P):
        if r % 64 < 16:
            invf[r, 1] = 500000.0 ** (-(((r % 64) % 8) * 2.0 / 16))
    c["invf"] = invf
    adm = np.zeros((P, P + 2 * P), np.float32)
    for p in range(2):
        key = np.arange(P * (p + 1)) // CHUNK
        query = (P * p + i) // CHUNK
        adm[:, P * p:P * p + P * (p + 1)] = np.where(key[None, :] <= query[:, None], 0.0, NEG)
    c["admit"] = adm
    return c


def pack(parts):
    at, off = {}, 0
    for name, a in parts.items():
        at[name] = (off, a.shape[1])
        off += a.shape[1]
    return np.ascontiguousarray(np.concatenate(list(parts.values()), axis=1)), at


def make_consts_2():
    i, t = np.arange(P), np.arange(T)
    rot = rotation([(b + h + r, b + h + r + 16, -1.0) for b in (0, 64) for h in (0, 32) for r in range(16)]
                   + [(b + h + r + 16, b + h + r, 1.0) for b in (0, 64) for h in (0, 32) for r in range(16)])
    row, col = (t // 64).astype(np.float32), (t % 64).astype(np.float32)
    inv = (np.float32(10000.0) ** (-np.arange(16, dtype=np.float32) / 16)).astype(np.float32)
    ang = np.zeros((P, T), np.float32)
    for r in range(P):
        ang[r] = (row if r % 64 < 32 else col) * inv[r % 16]
    count = np.zeros((P, 2, T), np.float32)
    for r in range(P):
        for s in range(2):
            w = (2, 4, 8, 16)[2 * s + r // 64]
            count[r, s] = 1.0 / (np.clip(t + w // 2, 0, T) - np.clip(t - w // 2, 0, T))
    return rot, np.concatenate([np.cos(ang), np.sin(ang), count.reshape(P, 2 * T)], axis=1).astype(np.float32)


CONSTS, CAT = pack(make_consts())
ROT_AX, TABLES_2 = make_consts_2()
VEC_WIDTHS = dict(norm_mix=16, norm_mem=16, norm_ffn=16, norm_final=8, dn_norm=2, conv=192, b_gate=48,
                  a_log=16, dt_bias=16, cond=16, norm1=16, norm2=16, mod_b=96, pool_scale=2, lam=4,
                  q_norm=4, kv_norm=2, final_2=8, router=64)
VAT, _o = {}, 0
for _n, _w in VEC_WIDTHS.items():
    VAT[_n] = (_o, _w)
    _o += _w
VEC_W = _o


class Counts:

    def __init__(self, nc, ctx, known):
        self.nc, self.ctx, self.known, self.found = nc, ctx, known, {}
        self.sems, self.counted = {}, {}
        self.banks = [ctx.enter_context(nc.psum_tensor(f"bank{b}", [P, 512], F32)) for b in range(BANKS)]

    def sem(self, stage):
        if stage not in self.sems:
            self.sems[stage] = self.ctx.enter_context(self.nc.semaphore(stage))
            self.counted[stage] = 0
        return self.sems[stage]

    def advance(self, stage, n):
        self.sem(stage)
        self.counted[stage] += n
        return self.counted[stage]

    def value(self, stage, tag):
        return self.known.get((stage, tag), 1)

    def at(self, stage, tag):
        return self.sem(stage), self.value(stage, tag)

    def place(self, tag):
        return self.known.get(("bank", tag), (0, 1))

    def bank(self, tag):
        return self.banks[self.place(tag)[0]]

    def full(self, tag):
        return self.at(f"bank_full{self.place(tag)[0]}", tag)

    def empty(self, tag):
        b, n = self.place(tag)
        return self.sem(f"bank_read{b}"), n

    def summed(self, tag):
        slot, n = self.place((tag, "summed"))
        return self.sem(f"slab_done{slot}"), n


class Engine:

    def __init__(self, counts, eng, name):
        self.c, self.eng, self.name = counts, eng, name
        self.latest = None

    def count(self, stage=None, tag=None, by=1):
        stage = stage or f"{self.name}_step"
        n = self.c.advance(stage, by)
        if tag is not None:
            self.c.found[(stage, tag)] = n
        self.latest = (stage, n)
        return self.c.sem(stage), by

    def emptied(self, tag):
        b, n = self.c.place(tag)
        self.latest = (f"bank_read{b}", n)
        return self.c.sem(f"bank_read{b}"), 1

    def last(self):
        stage, n = self.latest
        return self.c.sem(stage), n


class Tensor(Engine):

    def __init__(self, counts, eng):
        super().__init__(counts, eng, "tensor")
        self.fills, self.turn, self.bank = [1] * BANKS, 0, None

    def take(self, tag, bank=None):
        if bank is None:
            bank, self.turn = self.turn, (self.turn + 1) % BANKS
        held = self.fills[bank]
        self.fills[bank] += 1
        self.c.found[("bank", tag)] = (bank, self.fills[bank])
        self.bank = self.c.banks[bank]
        return self.c.sem(f"bank_read{bank}"), held

    def filled(self, tag):
        return self.count(f"bank_full{self.c.found[('bank', tag)][0]}", tag)

class Stream:

    def __init__(self):
        self.phases, self.total = {}, 0

    def add(self, name, source, n, width=SLAB, first=0):
        self.phases[name] = (source, self.total, n, width, first)
        self.total += n


def loops(n):
    turns = n // RING
    return (turns if turns >= 3 else 0)


def load_stream(sync, stream, ring, c):
    for source, g0, n, width, first in stream.phases.values():
        def load(i, slot, before):
            if before is not None:
                sync.wait_ge(c.sem(f"slab_done{slot}"), before)
            index = bass.ds(i, 1)
            sync.dma_start(ring[:, slot, 0:width], source[index].rearrange("a p n -> p (a n)"))\
                .then_inc(c.sem(f"slab_loaded{slot}"), 16)
        turns = loops(n)
        peeled = 1 if turns and g0 < RING else 0
        for i in range(peeled * RING):
            g = g0 + i
            load(first + i, g % RING, g // RING if g >= RING else None)
        if turns:
            with sync.Fori(peeled, turns) as turn:
                for u in range(RING):
                    g = g0 + u
                    load(turn * RING + (first + u), g % RING, turn + g // RING)
        for i in range(turns * RING, n):
            g = g0 + i
            load(first + i, g % RING, g // RING if g >= RING else None)


def gemm_tensor(te, stream, name, ring, tag, rhs, cols, tiles=KT):
    _, g0, n, _, _ = stream.phases[name]
    nc, c = te.c.nc, te.c

    def slab(slot, ps):
        for k in range(tiles):
            last = nc.tensor.matmul(ps[:, 0:cols], ring[:, slot, k * P:(k + 1) * P], rhs(k),
                                    start=k == 0, stop=k == tiles - 1)
        last.then_inc(c.sem(f"slab_done{slot}"), 1)

    turns = loops(n)
    if turns:
        base = list(te.fills)
        with te.eng.Fori(0, turns) as turn:
            for u in range(RING):
                slot = (g0 + u) % RING
                te.eng.wait_ge(c.sem(f"slab_loaded{slot}"), (turn + ((g0 + u) // RING + 1)) * 16)
                te.eng.wait_ge(c.sem(f"bank_read{slot}"), turn + base[slot])
                slab(slot, c.banks[slot])
        for u in range(RING):
            slot = (g0 + u) % RING
            for t in range(turns):
                c.found[("bank", (name, tag, t * RING + u))] = (slot, base[slot] + t + 1)
            te.fills[slot] += turns
    for i in range(turns * RING, n):
        g = g0 + i
        te.eng.wait_ge(c.sem(f"slab_loaded{g % RING}"), 16 * (g // RING + 1))
        te.eng.wait_ge(*te.take((name, tag, i), bank=g % RING))
        slab(g % RING, te.bank)


def gemm_read(rd, stream, name, tag, read):
    _, g0, n, _, _ = stream.phases[name]
    c = rd.c
    turns = loops(n)
    if turns:
        with rd.eng.Fori(0, turns) as turn:
            for u in range(RING):
                slot = (g0 + u) % RING
                rd.eng.wait_ge(c.sem(f"slab_done{slot}"), turn + ((g0 + u) // RING + 1))
                read(turn * RING + u, c.banks[slot]).then_inc(c.sem(f"bank_read{slot}"), 1)
        rd.emptied((name, tag, turns * RING - 1))
    for i in range(turns * RING, n):
        g = g0 + i
        rd.eng.wait_ge(c.sem(f"slab_done{g % RING}"), g // RING + 1)
        read(i, c.banks[g % RING]).then_inc(*rd.emptied((name, tag, i)))


def norm_tensor(te, k, tag, squares, tiles, cols):
    te.eng.wait_ge(*te.c.at("squared", tag))
    te.eng.wait_ge(*te.take(tag))
    ps = te.bank
    for i in range(tiles):
        last = te.c.nc.tensor.matmul(ps[:, 0:cols], k["ones"], squares[:, i, 0:cols],
                                     start=i == 0, stop=i == tiles - 1)
    last.then_inc(*te.filled(tag))


def norm_scalar(sc, tag, src, squares, root, tiles, cols):
    nc = sc.c.nc
    if sc.last_norm is not None:
        sc.eng.wait_ge(*sc.c.full(sc.last_norm))
        sc.eng.wait_ge(*sc.c.at("normed", sc.last_norm))
    nc.scalar.activation(squares[:, 0:tiles, 0:cols], src, ACT.Square).then_inc(*sc.count("squared", tag))
    sc.eng.wait_ge(*sc.c.full(tag))
    ps = sc.c.bank(tag)
    nc.scalar.activation(root[:, 0:cols], ps[:, 0:cols], ACT.Sqrt, bias=sc.eps[:, 0:1], scale=1.0 / (tiles * P)).then_inc(*sc.emptied(tag))
    sc.last_norm = tag


def norm_vector(ve, tag, src, gain, root, out, tiles, cols, streams=None):
    nc = ve.c.nc
    ve.eng.wait_ge(*ve.c.empty(tag))
    nc.vector.reciprocal(root[:, 0:cols], root[:, 0:cols]).then_inc(*ve.count())
    ve.eng.wait_ge(*ve.last())
    parts = [(slice(0, cols), gain, None)] if streams is None else streams
    for at, g, _ in parts:
        for i in range(tiles):
            ins = nc.vector.scalar_tensor_tensor(out=out[:, i, at], in0=src[:, i, at], scalar=g[:, i:i + 1],
                                                 in1=root[:, at], op0=ALU.mult, op1=ALU.mult)
    if streams is not None:
        ins.then_inc(*ve.count())
        ve.eng.wait_ge(*ve.last())
        for at, _, shift in parts:
            for i in range(tiles):
                ins = nc.vector.tensor_scalar(out[:, i, at], out[:, i, at], shift[:, i:i + 1], None, ALU.add)
    ins.then_inc(*ve.count("normed", tag))


def att_tensor(te, k, tag, units, P_of, PT_of, ident):
    nc = te.c.nc
    n = len(units)

    def logits(u):
        x = units[u]
        for b, bank in enumerate(x["logits"]):
            te.eng.wait_ge(*te.take((tag, "logits", u, b)))
            ps = te.bank
            for col, width, pairs in bank:
                for j, (lhsT, rhs) in enumerate(pairs):
                    last = nc.tensor.matmul(ps[:, col:col + width], lhsT, rhs, start=j == 0,
                                            stop=j == len(pairs) - 1)
            last.then_inc(*te.filled((tag, "logits", u, b)))

    def turned(u):
        x = units[u]
        te.eng.wait_ge(*te.c.at("probs", (tag, u)))
        tiles = x["turn"]
        te.eng.wait_ge(*te.take((tag, "turned", u)))
        ps = te.bank
        for j, (sub, kt) in enumerate(tiles):
            last = nc.tensor.transpose(ps[:, j * P:(j + 1) * P], P_of(u)[:, sub, kt * P:(kt + 1) * P], ident)
        last.then_inc(*te.filled((tag, "turned", u)))

    def out(u):
        x = units[u]
        te.eng.wait_ge(*te.c.empty((tag, "turned", u)))
        te.eng.wait_ge(*te.take((tag, "mixed", u)))
        ps = te.bank
        for col, pairs in x["out"](PT_of(u)):
            for j, (lhsT, rhs) in enumerate(pairs):
                last = nc.tensor.matmul(ps[:, col:col + P], lhsT, rhs, start=j == 0, stop=j == len(pairs) - 1)
        last.then_inc(*te.filled((tag, "mixed", u)))

    for u in range(n + 3):
        if u < n:
            logits(u)
        if 0 <= u - 2 < n:
            turned(u - 2)
        if 0 <= u - 3 < n:
            out(u - 3)


ATT_BUF = 3


def att_vector(ve, tag, units, P_of, mx, sm, scale, combine=None):
    nc = ve.c.nc
    n = len(units)

    def front(u):
        x = units[u]
        if u >= ATT_BUF:
            ve.eng.wait_ge(*ve.c.full((tag, "turned", u - ATT_BUF)))
        s, nk, subs = P_of(u), x["nk"], x["subs"]
        at = 0
        for b, bank in enumerate(x["logits"]):
            ve.eng.wait_ge(*ve.c.full((tag, "logits", u, b)))
            ps = ve.c.bank((tag, "logits", u, b))
            m = len(bank)
            src = ps[:, 0:512].rearrange("p (s k) -> p s k", s=m)[:, :, 0:nk]
            if x["mask"] is None:
                ins = nc.vector.tensor_scalar(s[:, at:at + m, 0:nk], src, scale, None, ALU.mult)
            else:
                ins = nc.vector.scalar_tensor_tensor(out=s[:, at:at + m, 0:nk], in0=src, scalar=scale,
                                                     in1=x["mask"].unsqueeze(1).to_broadcast([P, m, nk]),
                                                     op0=ALU.mult, op1=ALU.add)
            ins.then_inc(*ve.emptied((tag, "logits", u, b)))
            at += m
        ve.eng.wait_ge(*ve.last())
        nc.vector.tensor_reduce(mx[:, u % ATT_BUF, 0:subs], s[:, 0:subs, 0:nk], AXX, ALU.max).then_inc(*ve.count())
        ve.eng.wait_ge(*ve.last())
        nc.vector.tensor_scalar(mx[:, u % ATT_BUF, 0:subs], mx[:, u % ATT_BUF, 0:subs], -1.0, None,
                                        ALU.mult).then_inc(*ve.count("maxed", (tag, u)))

    def back(u):
        x = units[u]
        s, nk, subs = P_of(u), x["nk"], x["subs"]
        ve.eng.wait_ge(*ve.c.at("exped", (tag, u)))
        r = sm[:, u % ATT_BUF, 0:subs]
        nc.vector.reciprocal(r, r).then_inc(*ve.count())
        ve.eng.wait_ge(*ve.last())
        if combine is None:
            for j in range(subs):
                ins = nc.vector.tensor_scalar(s[:, j, 0:nk], s[:, j, 0:nk], r[:, j:j + 1], None, ALU.mult)
        else:
            nc.vector.tensor_scalar(r[:, 1:2], r[:, 1:2], combine, None, ALU.mult).then_inc(*ve.count())
            ve.eng.wait_ge(*ve.last())
            nc.vector.tensor_scalar(s[:, 1, 0:nk], s[:, 1, 0:nk], r[:, 1:2], None, ALU.mult).then_inc(*ve.count())
            ve.eng.wait_ge(*ve.last())
            ins = nc.vector.scalar_tensor_tensor(out=s[:, 0, 0:nk], in0=s[:, 0, 0:nk], scalar=r[:, 0:1],
                                                 in1=s[:, 1, 0:nk], op0=ALU.mult, op1=ALU.subtract)
        ins.then_inc(*ve.count("probs", (tag, u)))

    for u in range(n + 1):
        if u < n:
            front(u)
        if u >= 1:
            back(u - 1)


def att_scalar(sc, tag, units, P_of, PT_of, mx, sm):
    nc = sc.c.nc
    n = len(units)

    def exps(u):
        x = units[u]
        sc.eng.wait_ge(*sc.c.at("maxed", (tag, u)))
        for j in range(x["subs"]):
            ins = nc.scalar.activation(P_of(u)[:, j, 0:x["nk"]], P_of(u)[:, j, 0:x["nk"]], ACT.Exp,
                                       bias=mx[:, u % ATT_BUF, j:j + 1], accum_out=sm[:, u % ATT_BUF, j:j + 1])
        ins.then_inc(*sc.count("exped", (tag, u)))

    def turned(u):
        x = units[u]
        sc.eng.wait_ge(*sc.c.full((tag, "turned", u)))
        ps = sc.c.bank((tag, "turned", u))
        if u >= ATT_BUF:
            sc.eng.wait_ge(*sc.c.full((tag, "mixed", u - ATT_BUF)))
        w = len(x["turn"]) * P
        nc.scalar.activation(PT_of(u)[:, 0:w], ps[:, 0:w], ACT.Copy).then_inc(*sc.emptied((tag, "turned", u)))

    def out(u):
        sc.eng.wait_ge(*sc.c.full((tag, "mixed", u)))
        ps = sc.c.bank((tag, "mixed", u))
        dst, cols = units[u]["dst"]
        src = ps[:, 0:cols] if dst.ndim == 2 else ps[:, 0:cols].rearrange("p (a b) -> p a b", b=P)
        nc.scalar.activation(dst, src, ACT.Copy).then_inc(*sc.emptied((tag, "mixed", u)))

    for u in range(n + 3):
        if u < n:
            exps(u)
        if 0 <= u - 2 < n:
            turned(u - 2)
        if 0 <= u - 3 < n:
            out(u - 3)

def ffn_tensor(te, stream, name, ring, tag, act, steps):
    _, g0, n, _, _ = stream.phases[name]
    nc, c = te.c.nc, te.c
    x, hidden = act
    for b in range(6):
        te.eng.wait_ge(*te.take((tag, "ffn", b), bank=b))
    te.eng.wait_ge(*te.c.at("hidden_ready", ("cleared", tag)))
    h0 = te.c.value("hidden0", tag)

    def loaded(j, turn=0):
        slot = (g0 + j) % RING
        te.eng.wait_ge(c.sem(f"slab_loaded{slot}"), (turn + ((g0 + j) // RING + 1)) * 16)
        return slot

    def gate_up(f, bank, used):
        if used is not None:
            te.eng.wait_ge(c.sem("hidden_ready"), used)
        for part in range(2):
            slot = loaded(3 * f[0] + part, f[1])
            for k in range(KT):
                last = nc.tensor.matmul(c.banks[bank][:, part * T:(part + 1) * T], ring[:, slot, k * P:(k + 1) * P],
                                        x[:, k, 0:T], start=k == 0, stop=k == KT - 1)
            last.then_inc(c.sem(f"slab_done{slot}"), 1)

    def down(f, parity, ready):
        te.eng.wait_ge(c.sem("hidden_ready"), ready)
        slot = loaded(3 * f[0] + 2, f[1])
        for m in range(KT):
            last = nc.tensor.matmul(c.banks[m // 2][:, (m % 2) * T:(m % 2 + 1) * T],
                                    ring[:, slot, m * P:(m + 1) * P], hidden[:, parity, :],
                                    start=False, stop=True, skip_group_check=True)
        last.then_inc(c.sem(f"slab_done{slot}"), 1)

    pairs = (steps - 2) // 2
    gate_up((0, 0), 4, None)
    with te.eng.Fori(0, pairs) as turn:
        gate_up((1, turn), 5, turn * 2 + h0)
        down((0, turn), 0, turn * 2 + (h0 + 1))
        gate_up((2, turn), 4, turn * 2 + (h0 + 1))
        down((1, turn), 1, turn * 2 + (h0 + 2))
    f = 2 * pairs
    gate_up((f + 1, 0), 5, h0 + f)
    down((f, 0), 0, h0 + f + 1)
    down((f + 1, 0), 1, h0 + f + 2)
    g = g0 + n - 1
    c.found[("bank", (tag, "summed"))] = (g % RING, g // RING + 1)


def ffn_scalar(sc, stream, name, tag, silu, steps):
    _, g0, n, _, _ = stream.phases[name]
    nc, c = sc.c.nc, sc.c
    s0 = c.advance("silu_ready", 0)
    h0 = c.value("hidden0", tag)
    c.found[("silu0", tag)] = s0

    def one(u, turn):
        slot = (g0 + 3 * u + 1) % RING
        sc.eng.wait_ge(c.sem(f"slab_done{slot}"), turn + ((g0 + 3 * u + 1) // RING + 1))
        if u >= 2:
            sc.eng.wait_ge(c.sem("hidden_ready"), turn * 2 + (h0 + u - 1))
        nc.scalar.activation(silu[:, u % 2, :], c.banks[4 + u % 2][:, 0:T], ACT.Silu)\
            .then_inc(c.sem("silu_ready"), 1)

    for u in range(2):
        one(u, 0)
    with sc.eng.Fori(0, steps // 2 - 1) as turn:
        for u in range(2):
            one(2 + u, turn)
    c.advance("silu_ready", steps)
    sc.latest = ("silu_ready", s0 + steps)


def ffn_vector(ve, stream, name, tag, silu, hidden, tick, steps, weight=None):
    _, g0, n, _, _ = stream.phases[name]
    nc, c = ve.c.nc, ve.c
    s0 = c.value("silu0", tag)
    for b in range(4):
        n_before = c.place((tag, "ffn", b))[1]
        ve.eng.wait_ge(c.sem(f"bank_read{b}"), n_before - 1)
        ins = nc.vector.memset(c.banks[b][:, :], 0.0)
    ins.then_inc(*ve.count("hidden_ready", ("cleared", tag)))
    h0 = c.advance("hidden_ready", 0)
    c.found[("hidden0", tag)] = h0
    w0 = c.advance("weighed", 0)

    def one(u, turn, expert, past):
        up = (g0 + 3 * u + 1) % RING
        ve.eng.wait_ge(c.sem(f"slab_done{up}"), turn + ((g0 + 3 * u + 1) // RING + 1))
        ve.eng.wait_ge(c.sem("silu_ready"), turn * 2 + (s0 + u + 1))
        if past:
            d = (g0 + 3 * (u - 2) + 2) % RING
            ve.eng.wait_ge(c.sem(f"slab_done{d}"), turn + ((g0 + 3 * (u - 2) + 2) // RING + 1))
        b = 4 + u % 2
        s = silu[:, u % 2, :]
        if weight is None:
            nc.vector.tensor_tensor(hidden[:, u % 2, :], s, c.banks[b][:, T:2 * T], ALU.mult)\
                .then_inc(c.sem("hidden_ready"), 1)
        else:
            nc.vector.tensor_tensor(s, s, weight(expert), ALU.mult).then_inc(c.sem("weighed"), 1)
            ve.eng.wait_ge(c.sem("weighed"), turn * 2 + (w0 + u + 1))
            nc.vector.tensor_tensor(hidden[:, u % 2, :], s, c.banks[b][:, T:2 * T], ALU.mult)\
                .then_inc(c.sem("hidden_ready"), 1)

    if weight is None:
        for u in range(2):
            one(u, 0, None, False)
        with ve.eng.Fori(0, steps // 2 - 1) as turn:
            for u in range(2):
                one(2 + u, turn, None, True)
    else:
        for u in range(2):
            one(u, 0, 0, False)
        with ve.eng.Fori(0, FT // 2 - 1) as turn:
            for u in range(2):
                one(2 + u, turn, 0, True)
        with ve.eng.Fori(0, NE - 1) as e:
            with ve.eng.Fori(0, FT // 2) as turn:
                for u in range(2):
                    one(FT + u, turn + e * (FT // 2), e + 1, True)
        c.advance("weighed", steps)
    c.advance("hidden_ready", steps)
    ve.latest = ("hidden_ready", h0 + steps)
    ve.eng.wait_ge(*ve.last())
    for b in (4, 5):
        nc.vector.memset(tick[:, b:b + 1], 0.0).then_inc(*ve.emptied((tag, "ffn", b)))


def even_ffn_read(rd, stream, part, read):
    _, g0, n, _, _ = stream.phases["even_ffn"]
    c = rd.c
    first = lambda i: c.place(("even_ffn", 0, i))

    def one(i, turn, f):
        slot = (g0 + i) % RING
        rd.eng.wait_ge(c.sem(f"slab_done{slot}"), turn + ((g0 + i) // RING + 1))
        b, m = first(i + 1 if part == 0 else i - 1)
        if part == 0:
            rd.eng.wait_ge(c.sem(f"bank_read{b}"), turn + (m - 1))
        else:
            rd.eng.wait_ge(c.sem(f"bank_read{b}"), turn + m)
        return read(f, (i // 2) % 3, c.banks[slot])

    turns = loops(n)
    with rd.eng.Fori(0, turns) as turn:
        for u in range(part, RING, 2):
            one(u, turn, turn * 3 + u // 2).then_inc(c.sem(f"bank_read{(g0 + u) % RING}"), 1)
    for i in range(turns * RING + part, n, 2):
        slot = (g0 + i) % RING
        rd.eng.wait_ge(c.sem(f"slab_done{slot}"), (g0 + i) // RING + 1)
        b, m = first(i + 1 if part == 0 else i - 1)
        rd.eng.wait_ge(c.sem(f"bank_read{b}"), m - 1 if part == 0 else m)
        read(i // 2, (i // 2) % 3, c.banks[slot]).then_inc(*rd.emptied(("even_ffn", 0, i)))

def tile_of(a, i):
    return a[:, bass.ds(i, 1), :].rearrange("p a t -> p (a t)")


def program(nc, dram, known):
    ctx = ExitStack()
    c = Counts(nc, ctx, known)

    with ctx:

        def sb(name, shape, dt=F32):
            return ctx.enter_context(nc.sbuf_tensor(name, shape, dt))

        ring = sb("ring", [P, RING, SLAB])
        consts = sb("consts", [P, CONSTS.shape[1]])
        vecs = sb("vecs", [P, VEC_W])
        x = sb("x", [P, KT, T])
        hn = sb("hn", [P, KT, T])
        squares = sb("squares", [P, KT * T])
        root = sb("root", [P, 512])
        rope = sb("rope", [P, 4, T])
        small = sb("small", [P, 640])
        tick = sb("tick", [P, 8])
        eps = sb("eps", [P, 4])
        mods = sb("mods", [P, DEPTH, 48, 2])
        cond = sb("cond", [P, KT, 2])
        arena = sb("arena", [P, 33 * T + 28 * T + 8 * 2048 + 1536])
        A = arena[:, 0:33 * T].rearrange("p (k t) -> p k t", t=T)
        Bq = arena[:, 33 * T:61 * T].rearrange("p (k t) -> p k t", t=T)
        W = arena[:, 61 * T:]

        k = {n: consts[:, o:o + w] for n, (o, w) in CAT.items()}
        v = {n: vecs[:, o:o + w] for n, (o, w) in VAT.items()}

        def area(i, n=2048, off=0):
            return W[:, i * 2048 + off:i * 2048 + off + n]

        sq8 = squares[:, :].rearrange("p (k t) -> p k t", t=T)
        KB, KD, VB, M, X, Pl, Y, AT = [area(i).rearrange("p (a b) -> p a b", b=P) for i in range(8)]
        MK = squares[:, :].rearrange("p (a b) -> p a b", b=P)
        DEC, DECT, EGB = [area(8, 512, 512 * i) for i in range(3)]
        WT, UU = M, Pl
        S = area(6, 1024).rearrange("p (h v) -> p h v", v=P)
        VN = area(6, 1024, 1024).rearrange("p (h v) -> p h v", v=P)
        conv = [area(6).rearrange("p (k t) -> p k t", t=T), area(4).rearrange("p (k t) -> p k t", t=T)]
        sroot = area(3).rearrange("p (k t) -> p k t", t=T)
        gated = sroot
        stok = small[:, 0:256].rearrange("p (a f) -> p a f", f=P)
        sm = lambda o, n: small[:, 256 + o:256 + o + n]
        beta, gneg, y0, y1, y2, gate = sm(0, 16), sm(16, 8), sm(24, 16), sm(40, 16), sm(56, 16), sm(72, 16)
        graw, gexp, bexp, iw = sm(88, 64), sm(152, 64), sm(216, 16), sm(232, 16)
        mx = sm(248, 6).rearrange("p (a b) -> p a b", b=2)
        smx = sm(254, 6).rearrange("p (a b) -> p a b", b=2)
        m8 = sm(264, 8)
        C = W[:, 0:24 * T].rearrange("p (k t) -> p k t", t=T)
        att_p = W[:, 6144:6144 + 3 * 1024].rearrange("p (r s k) -> p r s k", r=3, s=2)
        att_t = W[:, 9216:9216 + 3 * 512].rearrange("p (r k) -> p r k", r=3)
        vtok = W[:, 10752:12800].rearrange("p (a n) -> p a n", a=2)
        merged = W[:, 12800:14848].rearrange("p (k t) -> p k t", t=T)
        memn = merged
        ixk = W[:, 0:256]
        score = W[:, 256:512]
        relu = W[:, 512:1536].rearrange("p (r s k) -> p r s k", r=2, s=2)
        work = W[:, 1536:1792]
        negm = W[:, 1792:2304].rearrange("p (a k) -> p a k", a=2)
        ropet = W[:, 2304:3328].rearrange("p (r s k) -> p r s k", r=2, s=2)
        silu = W[:, 0:512].rearrange("p (a t) -> p a t", a=2)
        hidden = W[:, 512:1024].rearrange("p (a t) -> p a t", a=2)
        mtmp = W[:, 0:512].rearrange("p (a t) -> p a t", a=2)
        P_of = lambda u: att_p[:, u % 3]
        PT_of = lambda u: att_t[:, u % 3]

        T2 = 2 * T
        def room(at, tiles, cols):
            return arena[:, at:at + tiles * cols].rearrange("p (k t) -> p k t", t=cols)
        H, hn2, sq2 = room(0, KT, T2), room(4096, KT, T2), room(8192, KT, T2)
        Z = room(12288, 20, T2)
        att_p2 = arena[:, 22528:25600].rearrange("p (r s k) -> p r s k", r=3, s=2)
        att_t2 = arena[:, 25600:27136].rearrange("p (r k) -> p r k", r=3)
        vtok2 = arena[:, 27136:30208].rearrange("p (a n) -> p a n", a=4)
        pools = [arena[:, 30208 + 1088 * i:30208 + 1088 * (i + 1)].rearrange("p (s e t) -> p s e t", s=2, e=2) for i in range(3)]
        hidden2 = room(12288, FT, T2)
        silu2 = room(23552, 3, T2)
        Zo, cqn, ckvn = room(12288, 7, T2), room(15872, 4, T), room(16896, 2, T2)
        QN, KV = room(17920, 12, T), room(20992, 16, T2)
        att_p3 = arena[:, 4096:7168].rearrange("p (r s k) -> p r s k", r=3, s=2)
        att_t3 = arena[:, 29184:30720].rearrange("p (r k) -> p r k", r=3)
        vtok3 = arena[:, 8192:12288].rearrange("p (a n) -> p a n", a=4)
        expert_w = squares[:, :].rearrange("p (e t) -> p e t", t=T)
        cos2, sin2 = rope[:, 0, :], rope[:, 1, :]
        o2 = CAT["strict"][0]
        rot_ax, pool_w = consts[:, o2:o2 + P], consts[:, o2 + P:o2 + 3 * P]
        gains = small[:, 0:64].rearrange("p (n k) -> p n k", k=KT)
        lamb = small[:, 64:72]
        rout = small[:, 80:240]
        mx2 = small[:, 504:510].rearrange("p (a b) -> p a b", b=2)
        smx2 = small[:, 510:516].rearrange("p (a b) -> p a b", b=2)
        mod = lambda l, n, s: mods[:, l, 8 * n:8 * n + 8, s]
        both = lambda a, s: slice(0, T) if s == 0 else slice(T, T2)

        def diff_units():
            units = []
            for s in range(2):
                k0, nk = (0, T2) if s == 0 else (T, T)
                for p in range(NP2):
                    for h in range(DH):
                        q = slice(s * T + p * P, s * T + (p + 1) * P)
                        units.append(dict(
                            logits=[[(0, nk, [(Z[64 * j:64 * j + 64, 2 + h, q], Z[64 * j:64 * j + 64, 8 + h, k0:k0 + nk])])]
                                    for j in range(2)],
                            nk=nk, subs=2, mask=None, turn=[(0, kt) for kt in range(nk // P)],
                            out=lambda pt, h=h, nk=nk, k0=k0: [
                                (0, [(vtok2[:, k0 // P + kt, h * P:(h + 1) * P], pt[:, kt * P:(kt + 1) * P])
                                     for kt in range(nk // P)])],
                            dst=(Z[:, 2 + h, q], P)))
            return units

        def latent_units():
            units = []
            for p in range(NP2):
                for h in range(MH):
                    q, r = slice(p * P, (p + 1) * P), slice(64 * (h % 2), 64 * (h % 2) + 64)
                    units.append(dict(
                        logits=[[(0, T2, [(QN[:, h, q], KV[:, h, :]), (QN[r, 8 + h // 2, q], Zo[r, 6, :])])]],
                        nk=T2, subs=1, mask=None, turn=[(0, kt) for kt in range(4)],
                        out=lambda pt, h=h: [(0, [(vtok3[:, kt, h * P:(h + 1) * P], pt[:, kt * P:(kt + 1) * P])
                                                  for kt in range(4)])],
                        dst=(QN[:, h, q], P)))
            return units

        stream = Stream()
        for l in range(DEPTH):
            stream.add(f"dn{l}", dram["w_in"][l], 33)
            stream.add(f"sa{l}", dram["w_in"][l], 28, first=33)
            stream.add(f"mem{l}", dram["w_mem"][l], 16)
            stream.add(f"xq{l}", dram["w_in"][l], 8, first=61)
            stream.add(f"gates{l}", dram["w_in"][l], 24, first=69)
            stream.add(f"branch{l}", dram["w_branch"][l], 24)
            stream.add(f"out{l}", dram["w_out"][l], 8)
            stream.add(f"ffn{l}", dram["w_ffn"][l], 3 * FT)

        for l in range(DEPTH):
            stream.add(f"mod{l}", dram["mod_w"][l], 48)
        stream.add("even_in", dram["even_in"], 20)
        stream.add("even_out", dram["even_out"], 8)
        stream.add("even_ffn", dram["even_ffn"], 2 * FT)
        stream.add("even_down", dram["even_down"], 24)
        stream.add("odd_in", dram["odd_in"], 7)
        stream.add("uq", dram["w_uq"], 12, width=512)
        stream.add("ukv", dram["w_ukv"], 16, width=256)
        stream.add("odd_out", dram["odd_out"], 8)
        stream.add("moe", dram["moe"], 3 * FT * NE)

        def sa_units(l):
            units = []
            for p in range(NP2):
                for h in range(0, SAH, 2):
                    nk = P * (p + 1)
                    units.append(dict(
                        logits=[[((i * 256), nk, [(Bq[:, h + i, p * P:(p + 1) * P], Bq[:, SAH + h + i, 0:nk])])
                                 for i in range(2)]],
                        nk=nk, subs=2, mask=negm[:, p, 0:nk], turn=[(i, kt) for i in range(2) for kt in range(p + 1)],
                        out=lambda pt, h=h, p=p: [
                            (i * P, [(vtok[:, kt, (h + i) * P:(h + i + 1) * P],
                                      pt[:, (i * (p + 1) + kt) * P:(i * (p + 1) + kt + 1) * P])
                                     for kt in range(p + 1)]) for i in range(2)],
                        dst=(Bq[:, 2 * SAH + h:2 * SAH + h + 2, p * P:(p + 1) * P], 256)))
            return units

        def xa_units(l):
            units = []
            for p in range(NP2):
                for h in range(0, XAH, 2):
                    units.append(dict(
                        logits=[[(i * 256, T, [(C[:, 2 * (h + i) + d, p * P:(p + 1) * P], C[:, 8 + 2 * (h + i) + d, :])
                                               for d in range(2)]) for i in range(2)]],
                        nk=T, subs=2, mask=None, turn=[(i, kt) for i in range(2) for kt in range(2)],
                        out=lambda pt, h=h: [
                            ((2 * i + d) * P, [(vtok[:, kt, (2 * (h + i) + d) * P:(2 * (h + i) + d + 1) * P],
                                                pt[:, (2 * i + kt) * P:(2 * i + kt + 1) * P]) for kt in range(2)])
                            for i in range(2) for d in range(2)],
                        dst=(C[:, 2 * h:2 * h + 4, p * P:(p + 1) * P], 512)))
            return units

        block = ctx.enter_context(nc.Block())

        @block.sync
        def _(sync):
            sy = Engine(c, sync, "sync")
            sync.dma_start(consts[:, :], dram["consts"]).then_inc(*sy.count("const_loaded", "all", 16))
            sync.dma_start(vecs[:, :], dram["vecs"]).then_inc(*sy.count("vec_loaded", "all", 16))
            sync.dma_start(x[:, :, :], dram["x"]).then_inc(*sy.count("x_loaded", "all", 16))
            load_stream(sync, stream, ring, c)

        @block.gpsimd
        def _(pool):
            po = Engine(c, pool, "pool")
            pool.dma_start(root[:, 0:T].bitcast(I32), dram["pos"][0, :].partition_broadcast(P)).then_inc(*po.count("pos_loaded", "all", 16))
            for l in range(DEPTH):
                pool.wait_ge(*c.at("sparse_done", l))
                pool.dma_start(memn[:, :, :], dram["mem"]).then_inc(*po.count("mem_loaded", l, 16))
            pool.wait_ge(*c.at("x_new", (DEPTH - 1, "out")))
            for dst, name in ((H[:, :, T:T2], "ctx"), (rope[:, :, :].rearrange("p a t -> p (a t)"), "tables2"),
                              (rot_ax, "rot_ax"), (pool_w, "pool_w")):
                pool.dma_start(dst, dram[name]).then_inc(*po.count("second_loaded", "all", 16))
            pool.wait_ge(*c.at("result", "x"))
            pool.dma_start(dram["y"], x[:, :, :]).then_inc(*po.count("stored", "y", 16))
            pool.wait_ge(*c.at("stored", "y"))

        @block.tensor
        def _(pe):
            te = Tensor(c, pe)
            pe.wait_ge(*c.at("const_loaded", "all"))
            ident, mm = k["ident"], nc.tensor.matmul
            for l in range(DEPTH):
                norm_tensor(te, k, ("mix", l), sq8, KT, T)
                pe.wait_ge(*c.at("normed", ("mix", l)))
                gemm_tensor(te, stream, f"dn{l}", ring, l, lambda i: hn[:, i, :], T)
                gemm_tensor(te, stream, f"sa{l}", ring, l, lambda i: hn[:, i, :], T)
                pe.wait_ge(*c.empty((f"dn{l}", l, 32)))
                pe.wait_ge(*te.take(("narrow", l)))
                ps = te.bank
                for p in range(NP2):
                    last = nc.tensor.transpose(ps[:, p * P:(p + 1) * P], A[:, 32, p * P:(p + 1) * P], ident)
                last.then_inc(*te.filled(("narrow", l)))
                for g in range(2):
                    pe.wait_ge(*c.at("squared", ("l2", l, g)))
                    for j in range(4):
                        pe.wait_ge(*te.take(("l2", l, g, j)))
                        ps = te.bank
                        mm(ps[:, :], k["ones"], squares[:, j * 512:(j + 1) * 512], start=True, stop=True).then_inc(*te.filled(("l2", l, g, j)))
                pe.wait_ge(*c.at("decay_log", l))
                pe.wait_ge(*te.take(("sums", l)))
                ps = te.bank
                for j, m in enumerate(("upto", "after", "chunk0", "chunk1")):
                    last = mm(ps[:, 16 * j:16 * j + 16], k[m], gate, start=True, stop=True)
                last.then_inc(*te.filled(("sums", l)))
                pe.wait_ge(*c.at("unit", (l, 1)))
                pe.wait_ge(*c.at("conv_silu", (l, 2)))
                for g in range(4):
                    p, h0 = g // 2, 4 * (g % 2)
                    for name, at in (("ktok", 8), ("vtok", 16)):
                        pe.wait_ge(*te.take((name, l, g)))
                        ps = te.bank
                        for i in range(4):
                            last = nc.tensor.transpose(ps[:, i * P:(i + 1) * P], A[:, at + h0 + i, p * P:(p + 1) * P], ident)
                        last.then_inc(*te.filled((name, l, g)))
                pe.wait_ge(*c.at("unit", (l, 0)))
                for g in range(4):
                    p, h0 = g // 2, 4 * (g % 2)
                    pe.wait_ge(*te.take(("cum", l, g)))
                    ps = te.bank
                    for i in range(4):
                        last = mm(ps[:, i * P:(i + 1) * P], gate[:, p * 8 + h0 + i:p * 8 + h0 + i + 1].to_broadcast([P, P]),
                                  k["upto"], start=True, stop=True)
                    last.then_inc(*te.filled(("cum", l, g)))
                    for name, at in (("kk", 8), ("kq", 0)):
                        pe.wait_ge(*te.take((name, l, g)))
                        ps = te.bank
                        for i in range(4):
                            last = mm(ps[:, i * P:(i + 1) * P], A[:, 8 + h0 + i, p * P:(p + 1) * P],
                                      A[:, at + h0 + i, p * P:(p + 1) * P], start=True, stop=True)
                        last.then_inc(*te.filled((name, l, g)))
                for g in range(4):
                    pe.wait_ge(*c.at("inv0", (l, g)))
                    pe.wait_ge(*te.take(("x0", l, g)))
                    ps = te.bank
                    for i in range(4):
                        last = nc.tensor.transpose(ps[:, i * P:(i + 1) * P], Pl[:, 4 * g + i, :], ident)
                    last.then_inc(*te.filled(("x0", l, g)))
                for lev in range(1, 6):
                    for g in range(4):
                        pe.wait_ge(*c.at("merge_mask", (l, lev, g)))
                        if lev == 1:
                            pe.wait_ge(*c.empty(("x0", l, g)))
                        else:
                            pe.wait_ge(*c.at("inv", (l, lev - 1, g)))
                        pe.wait_ge(*te.take(("ny", l, lev, g)))
                        ps = te.bank
                        for i in range(4):
                            last = mm(ps[:, i * P:(i + 1) * P], MK[:, 4 * g + i, :], X[:, 4 * g + i, :], start=True, stop=True)
                        last.then_inc(*te.filled(("ny", l, lev, g)))
                    for g in range(4):
                        pe.wait_ge(*c.empty(("ny", l, lev, g)))
                        pe.wait_ge(*te.take(("nx", l, lev, g)))
                        ps = te.bank
                        for i in range(4):
                            last = mm(ps[:, i * P:(i + 1) * P], Pl[:, 4 * g + i, :], Y[:, 4 * g + i, :], start=True, stop=True)
                        last.then_inc(*te.filled(("nx", l, lev, g)))
                        if lev < 5:
                            pe.wait_ge(*te.take(("np", l, lev, g)))
                            ps = te.bank
                            for i in range(4):
                                last = mm(ps[:, i * P:(i + 1) * P], Y[:, 4 * g + i, :], Pl[:, 4 * g + i, :], start=True, stop=True)
                            last.then_inc(*te.filled(("np", l, lev, g)))
                pe.wait_ge(*c.at("toks", l))
                for g in range(4):
                    pe.wait_ge(*c.at("inv", (l, 5, g)))
                    pe.wait_ge(*te.take(("u", l, g)))
                    ps = te.bank
                    for i in range(4):
                        last = mm(ps[:, i * P:(i + 1) * P], X[:, 4 * g + i, :], VB[:, 4 * g + i, :], start=True, stop=True)
                    last.then_inc(*te.filled(("u", l, g)))
                    pe.wait_ge(*te.take(("w", l, g)))
                    ps = te.bank
                    for i in range(4):
                        last = mm(ps[:, i * P:(i + 1) * P], KB[:, 4 * g + i, :], X[:, 4 * g + i, :], start=True, stop=True)
                    last.then_inc(*te.filled(("w", l, g)))
                for ch in range(NCH):
                    p, r = ch // 2, 64 * (ch % 2)
                    rows = slice(r, r + 64)
                    for j in range(2):
                        pe.wait_ge(*c.empty(("u", l, 2 * p + j)))
                        pe.wait_ge(*c.empty(("w", l, 2 * p + j)))
                    pe.wait_ge(*c.at("state", (l, ch)))
                    for j in range(2):
                        pe.wait_ge(*te.take(("ws", l, ch, j)))
                        ps = te.bank
                        for i in range(4):
                            h = 4 * j + i
                            last = mm(ps[rows, i * P:(i + 1) * P], WT[:, 8 * p + h, rows], S[:, h, :], start=True, stop=True)
                        last.then_inc(*te.filled(("ws", l, ch, j)))
                    pe.wait_ge(*c.at("vnew", (l, ch)))
                    if ch == 0:
                        pe.wait_ge(*c.at("qdec", (l, 3)))
                    pe.wait_ge(*te.take(("o", l, ch)))
                    ps = te.bank
                    for h in range(DNH):
                        o = ps[:, h * 64:(h + 1) * 64]
                        mm(o, S[:, h, :], A[:, h, ch * 64:(ch + 1) * 64], start=True, stop=False)
                        last = mm(o, VN[rows, h, :], AT[rows, 8 * p + h, rows], start=False, stop=True)
                    last.then_inc(*te.filled(("o", l, ch)))
                    if ch < NCH - 1:
                        for j in range(2):
                            pe.wait_ge(*te.take(("su", l, ch, j)))
                            ps = te.bank
                            for i in range(4):
                                h = 4 * j + i
                                last = mm(ps[:, i * P:(i + 1) * P], KD[rows, 8 * p + h, :], VN[rows, h, :], start=True, stop=True)
                            last.then_inc(*te.filled(("su", l, ch, j)))
                pe.wait_ge(*c.at("squared", ("o2", l)))
                for j in range(4):
                    pe.wait_ge(*te.take(("o2", l, j)))
                    ps = te.bank
                    mm(ps[:, :], k["ones"], squares[:, j * 512:(j + 1) * 512], start=True, stop=True).then_inc(*te.filled(("o2", l, j)))
                pe.wait_ge(*c.at("dn_done", l))
                for j in range(8):
                    pe.wait_ge(*c.empty((f"sa{l}", l, 2 * j + 1)))
                    pe.wait_ge(*te.take(("rope", l, j)))
                    ps = te.bank
                    mm(ps[:, :], k["rot_sa"], Bq[:, 2 * j:2 * j + 2, :].rearrange("p a t -> p (a t)"), start=True, stop=True).then_inc(*te.filled(("rope", l, j)))
                for j in range(2):
                    pe.wait_ge(*c.empty((f"sa{l}", l, 25 + 2 * j)))
                    pe.wait_ge(*te.take(("ropei", l, j)))
                    ps = te.bank
                    mm(ps[:, :], k["rot_ix"], Bq[:, 24 + 2 * j:26 + 2 * j, :].rearrange("p a t -> p (a t)"), start=True, stop=True).then_inc(*te.filled(("ropei", l, j)))
                pe.wait_ge(*te.take(("ik", l)))
                ps = te.bank
                mm(ps[:, 0:T], k["dup"], A[:, 32, :], start=True, stop=True)
                mm(ps[:, T:2 * T], k["dup_rot"], A[:, 32, :], start=True, stop=True).then_inc(*te.filled(("ik", l)))
                for j in range(4):
                    kt, h0 = j // 2, 4 * (j % 2)
                    pe.wait_ge(*c.empty((f"sa{l}", l, 16 + h0 + 3)))
                    pe.wait_ge(*te.take(("svt", l, j)))
                    ps = te.bank
                    for i in range(4):
                        last = nc.tensor.transpose(ps[:, i * P:(i + 1) * P], Bq[:, 16 + h0 + i, kt * P:(kt + 1) * P], ident)
                    last.then_inc(*te.filled(("svt", l, j)))
                pe.wait_ge(*c.at("index_rope", l))
                for p in range(NP2):
                    for j in range(4):
                        pe.wait_ge(*te.take(("score", l, p, j)))
                        ps = te.bank
                        r = slice(64 * (j % 2), 64 * (j % 2) + 64)
                        for i in range(2):
                            last = mm(ps[:, i * T:i * T + P * (p + 1)], Bq[r, 24 + 2 * (j // 2) + i, p * P:(p + 1) * P], ixk[r, 0:P * (p + 1)], start=True, stop=True)
                        last.then_inc(*te.filled(("score", l, p, j)))
                pe.wait_ge(*c.at("roped", l))
                pe.wait_ge(*c.empty(("svt", l, 3)))
                att_tensor(te, k, ("sa", l), sa_units(l), P_of, PT_of, ident)
                pe.wait_ge(*c.at("sparse_done", l))
                norm_tensor(te, k, ("mem", l), sq8, KT, T)
                pe.wait_ge(*c.at("normed", ("mem", l)))
                gemm_tensor(te, stream, f"mem{l}", ring, l, lambda i: memn[:, i, :], T)
                gemm_tensor(te, stream, f"xq{l}", ring, l, lambda i: hn[:, i, :], T)
                for j in range(4):
                    kt, h0 = j // 2, 4 * (j % 2)
                    pe.wait_ge(*c.empty((f"mem{l}", l, 8 + h0 + 3)))
                    pe.wait_ge(*te.take(("mvt", l, j)))
                    ps = te.bank
                    for i in range(4):
                        last = nc.tensor.transpose(ps[:, i * P:(i + 1) * P], C[:, 16 + h0 + i, kt * P:(kt + 1) * P], ident)
                    last.then_inc(*te.filled(("mvt", l, j)))
                pe.wait_ge(*c.empty((f"xq{l}", l, 7)))
                pe.wait_ge(*c.empty(("mvt", l, 3)))
                att_tensor(te, k, ("xa", l), xa_units(l), P_of, PT_of, ident)
                gemm_tensor(te, stream, f"gates{l}", ring, l, lambda i: hn[:, i, :], T)
                pe.wait_ge(*c.empty((("xa", l), "mixed", 3)))
                _, g0, _, _, _ = stream.phases[f"branch{l}"]
                src = [A[:, 24:32, :], Bq[:, 16:24, :], C[:, 0:8, :]]
                for n in range(KT):
                    for b in range(3):
                        g = g0 + 3 * n + b
                        pe.wait_ge(c.sem(f"slab_loaded{g % RING}"), 16 * (g // RING + 1))
                        pe.wait_ge(*te.take(("branch", l, 3 * n + b), bank=g % RING))
                        ps = te.bank
                        for i in range(KT):
                            last = mm(ps[:, 0:T], ring[:, g % RING, i * P:(i + 1) * P], src[b][:, i, :], start=i == 0, stop=i == KT - 1)
                        last.then_inc(c.sem(f"slab_done{g % RING}"), 1)
                pe.wait_ge(*c.at("merged", (l, KT - 1)))
                gemm_tensor(te, stream, f"out{l}", ring, l, lambda i: merged[:, i, :], T)
                norm_tensor(te, k, ("ffn", l), sq8, KT, T)
                pe.wait_ge(*c.at("normed", ("ffn", l)))
                ffn_tensor(te, stream, f"ffn{l}", ring, l, (hn, hidden), FT)
            norm_tensor(te, k, "final", sq8, KT, T)
            pe.wait_ge(*c.at("cond_silu", "all"))
            for l in range(DEPTH):
                gemm_tensor(te, stream, f"mod{l}", ring, l, lambda i: cond[:, i, :], 2)
            pe.wait_ge(*c.at("lam_prod", "all"))
            pe.wait_ge(*te.take("lam"))
            ps = te.bank
            mm(ps[:, 0:2], k["ones"], lamb[:, 0:2], start=True, stop=True).then_inc(*te.filled("lam"))
            norm_tensor(te, k, "e1", sq2, KT, T2)
            pe.wait_ge(*c.at("normed", "e1"))
            gemm_tensor(te, stream, "even_in", ring, 0, lambda i: hn2[:, i, :], T2)
            pe.wait_ge(*c.at("second_loaded", "all"))
            for j in range(6):
                pe.wait_ge(*c.empty(("even_in", 0, 2 + 2 * j + 1)))
                pe.wait_ge(*te.take(("axial", j)))
                ps = te.bank
                mm(ps[:, :].rearrange("p (a t) -> p a t", a=2), rot_ax, Z[:, 2 + 2 * j:4 + 2 * j, 0:T], start=True, stop=True).then_inc(*te.filled(("axial", j)))
            for kt in range(4):
                for j in range(2):
                    pe.wait_ge(*c.empty(("even_in", 0, 19)))
                    pe.wait_ge(*te.take(("evt", kt, j)))
                    ps = te.bank
                    for i in range(3):
                        last = nc.tensor.transpose(ps[:, i * P:(i + 1) * P], Z[:, 14 + 3 * j + i, kt * P:(kt + 1) * P], ident)
                    last.then_inc(*te.filled(("evt", kt, j)))
            pe.wait_ge(*c.at("pooled", "all"))
            for j in range(2):
                pe.wait_ge(*te.take(("pool", j)))
                ps = te.bank
                mm(ps[:, :], pool_w[:, j * P:(j + 1) * P], Z[:, j, :], start=True, stop=True).then_inc(*te.filled(("pool", j)))
            pe.wait_ge(*c.at("axial_done", 5))
            pe.wait_ge(*c.empty(("evt", 3, 1)))
            att_tensor(te, k, "diff", diff_units(), lambda u: att_p2[:, u % 3], lambda u: att_t2[:, u % 3], ident)
            pe.wait_ge(*c.at("squared", "heads"))
            for h in range(DH):
                pe.wait_ge(*te.take(("heads", h)))
                ps = te.bank
                mm(ps[:, :], k["ones"], sq2[:, h, :], start=True, stop=True).then_inc(*te.filled(("heads", h)))
            pe.wait_ge(*c.at("heads_normed", "all"))
            gemm_tensor(te, stream, "even_out", ring, 0, lambda i: Z[:, i, :], T2)
            norm_tensor(te, k, "e2", sq2, KT, T2)
            pe.wait_ge(*c.at("normed", "e2"))
            gemm_tensor(te, stream, "even_ffn", ring, 0, lambda i: hn2[:, i, :], T2)
            pe.wait_ge(*c.empty(("even_ffn", 0, 2 * FT - 1)))
            _, g0, _, _, _ = stream.phases["even_down"]
            for n in range(KT):
                pe.wait_ge(*te.take(("even_down", n)))
                ps = te.bank
                for b in range(3):
                    g = g0 + 3 * n + b
                    pe.wait_ge(c.sem(f"slab_loaded{g % RING}"), 16 * (g // RING + 1))
                    tiles = (8, 8, 6)[b]
                    for i in range(tiles):
                        last = mm(ps[:, :], ring[:, g % RING, i * P:(i + 1) * P], hidden2[:, 8 * b + i, :],
                                  start=b == 0 and i == 0, stop=b == 2 and i == tiles - 1)
                    last.then_inc(c.sem(f"slab_done{g % RING}"), 1)
            norm_tensor(te, k, "o1", sq2, KT, T2)
            pe.wait_ge(*c.at("normed", "o1"))
            gemm_tensor(te, stream, "odd_in", ring, 0, lambda i: hn2[:, i, :], T2)
            norm_tensor(te, k, "cq", sq2, 4, T)
            norm_tensor(te, k, "ckv", sq2, 2, T2)
            pe.wait_ge(*c.at("normed", "cq"))
            gemm_tensor(te, stream, "uq", ring, 0, lambda i: cqn[:, i, :], T, tiles=4)
            pe.wait_ge(*c.at("normed", "ckv"))
            gemm_tensor(te, stream, "ukv", ring, 0, lambda i: ckvn[:, i, :], T2, tiles=2)
            for j in range(2):
                pe.wait_ge(*c.empty(("uq", 0, 11)))
                pe.wait_ge(*te.take(("axq", j)))
                ps = te.bank
                mm(ps[:, :], rot_ax, QN[:, 8 + 2 * j:10 + 2 * j, :].rearrange("p a t -> p (a t)"), start=True, stop=True).then_inc(*te.filled(("axq", j)))
            pe.wait_ge(*te.take("axk"))
            ps = te.bank
            mm(ps[:, 0:T], rot_ax, Zo[:, 6, 0:T], start=True, stop=True).then_inc(*te.filled("axk"))
            pe.wait_ge(*c.empty(("ukv", 0, 15)))
            for kt in range(4):
                for j in range(2):
                    pe.wait_ge(*te.take(("ovt", kt, j)))
                    ps = te.bank
                    for i in range(4):
                        last = nc.tensor.transpose(ps[:, i * P:(i + 1) * P], KV[:, 8 + 4 * j + i, kt * P:(kt + 1) * P], ident)
                    last.then_inc(*te.filled(("ovt", kt, j)))
            pe.wait_ge(*c.at("axial2_done", "all"))
            pe.wait_ge(*c.empty(("ovt", 3, 1)))
            att_tensor(te, k, "latent", latent_units(), lambda u: att_p3[:, u % 3], lambda u: att_t3[:, u % 3], ident)
            pe.wait_ge(*c.empty(("latent", "mixed", 15)))
            gemm_tensor(te, stream, "odd_out", ring, 0, lambda i: QN[:, i, :], T)
            norm_tensor(te, k, "o2", sq2, KT, T)
            pe.wait_ge(*c.at("normed", "o2"))
            pe.wait_ge(*te.take("router"))
            ps = te.bank
            for p in range(NP2):
                for i in range(KT):
                    last = mm(ps[:, 8 * p:8 * p + 8], hn[:, i, p * P:(p + 1) * P], v["router"][:, 8 * i:8 * i + 8], start=i == 0, stop=i == KT - 1)
            last.then_inc(*te.filled("router"))
            pe.wait_ge(*c.at("routed", "all"))
            for j in range(4):
                pe.wait_ge(*te.take(("spread", j)))
                ps = te.bank
                for i in range(2):
                    for p in range(NP2):
                        w = rout[:, 8 * p + 2 * j + i:8 * p + 2 * j + i + 1].to_broadcast([P, P])
                        last = mm(ps[:, (2 * i + p) * P:(2 * i + p + 1) * P], w, ident, start=True, stop=True)
                last.then_inc(*te.filled(("spread", j)))
            ffn_tensor(te, stream, "moe", ring, "moe", (hn, hidden), FT * NE)
            norm_tensor(te, k, "last", sq2, KT, T)

        @block.scalar
        def _(act):
            sc = Engine(c, act, "scalar")
            sc.last_norm, sc.eps = None, eps
            af = nc.scalar.activation
            act.wait_ge(*c.at("eps", "all"))
            for i in range(2):
                act.wait_ge(*c.at("angle", i))
                af(rope[:, 2 * i + 1, :], rope[:, 2 * i + 1, :], ACT.Sin).then_inc(*sc.count("sincos", (i, 1)))
                af(rope[:, 2 * i, :], rope[:, 2 * i, :], ACT.Sin).then_inc(*sc.count("sincos", (i, 0)))
            act.wait_ge(*c.at("x_loaded", "all"))
            act.wait_ge(*c.at("vec_loaded", "all"))
            for l in range(DEPTH):
                if l:
                    act.wait_ge(*c.at("x_new", (l - 1, "ffn")))
                norm_scalar(sc, ("mix", l), x[:, :, :], sq8, root, KT, T)
                gemm_read(sc, stream, f"dn{l}", l, lambda i, ps: af(tile_of(A, i), ps[:, 0:T], ACT.Copy))
                gemm_read(sc, stream, f"sa{l}", l, lambda i, ps: af(tile_of(Bq, i), ps[:, 0:T], ACT.Copy))
                act.wait_ge(*c.full(("narrow", l)))
                ps = c.bank(("narrow", l))
                af(stok.rearrange("p a f -> p (a f)"), ps[:, 0:256], ACT.Copy).then_inc(*sc.emptied(("narrow", l)))
                for g in range(3):
                    act.wait_ge(*c.at("conv", (l, g)))
                    af(A[:, 8 * g:8 * g + 8, :], conv[g % 2], ACT.Silu).then_inc(*sc.count("conv_silu", (l, g)))
                act.wait_ge(*c.at("const_loaded", "all"))
                act.wait_ge(*sc.last())
                af(A[:, 24:32, :], A[:, 24:32, :], ACT.Silu).then_inc(*sc.count("z_silu", l))
                af(beta.rearrange("p (a b) -> p a b", a=2), stok[:, :, 64:72], ACT.Sigmoid).then_inc(*sc.count("beta", l))
                for g in range(2):
                    if g:
                        for j in range(4):
                            act.wait_ge(*c.full(("l2", l, 0, j)))
                        act.wait_ge(*c.at("unit", (l, 0)))
                    else:
                        act.wait_ge(*c.full(("mix", l)))
                    af(sq8, A[:, 8 * g:8 * g + 8, :], ACT.Square).then_inc(*sc.count("squared", ("l2", l, g)))
                    for j in range(4):
                        act.wait_ge(*c.full(("l2", l, g, j)))
                        ps = c.bank(("l2", l, g, j))
                        af(sroot[:, 2 * j:2 * j + 2, :].rearrange("p a t -> p (a t)"), ps[:, :], ACT.Sqrt, bias=eps[:, 0:1]).then_inc(*sc.emptied(("l2", l, g, j)))
                af(gneg, v["a_log"][:, 8 * l:8 * l + 8], ACT.Exp).then_inc(*sc.count("a_exp", l))
                act.wait_ge(*c.at("decay_in", l))
                af(y1, y1, ACT.Exp).then_inc(*sc.count())
                act.wait_ge(*sc.last())
                af(y1, y1, ACT.Ln, bias=eps[:, 1:2]).then_inc(*sc.count("decay_ln", l))
                act.wait_ge(*c.at("sums_copied", l))
                af(gexp, graw, ACT.Exp).then_inc(*sc.count("sums_exp", l))
                for g in range(4):
                    act.wait_ge(*c.full(("cum", l, g)))
                    ps = c.bank(("cum", l, g))
                    if g:
                        act.wait_ge(*c.at("qdec", (l, g - 1)))
                    af(EGB, ps[:, :], ACT.Exp).then_inc(*sc.count("cum_exp", (l, g)))
                    act.wait_ge(*c.at("decay_diff", (l, g)))
                    af(DEC, DEC, ACT.Exp, scale=-1.0).then_inc(*sc.count())
                    af(DECT, DECT, ACT.Exp).then_inc(*sc.count("decay_exp", (l, g)))
                for g in range(4):
                    act.wait_ge(*c.full(("x0", l, g)))
                    ps = c.bank(("x0", l, g))
                    af(X[:, 4 * g:4 * g + 4, :], ps[:, :].rearrange("p (a b) -> p a b", b=P), ACT.Copy).then_inc(*sc.emptied(("x0", l, g)))
                for lev in range(1, 6):
                    for g in range(4):
                        act.wait_ge(*c.full(("ny", l, lev, g)))
                        ps = c.bank(("ny", l, lev, g))
                        if lev > 1:
                            act.wait_ge(*c.at("inv", (l, lev - 1, g)))
                        af(Y[:, 4 * g:4 * g + 4, :], ps[:, :].rearrange("p (a b) -> p a b", b=P), ACT.Copy).then_inc(*sc.emptied(("ny", l, lev, g)))
                for g in range(4):
                    for name, dst in (("u", UU), ("w", WT)):
                        act.wait_ge(*c.full((name, l, g)))
                        ps = c.bank((name, l, g))
                        af(dst[:, 4 * g:4 * g + 4, :], ps[:, :].rearrange("p (a b) -> p a b", b=P), ACT.Copy).then_inc(*sc.emptied((name, l, g)))
                for ch in range(NCH):
                    act.wait_ge(*c.full(("o", l, ch)))
                    ps = c.bank(("o", l, ch))
                    af(A[:, 16:24, ch * 64:(ch + 1) * 64], ps[:, :].rearrange("p (h t) -> p h t", t=64), ACT.Copy).then_inc(*sc.emptied(("o", l, ch)))
                act.wait_ge(*sc.last())
                af(sq8, A[:, 16:24, :], ACT.Square).then_inc(*sc.count("squared", ("o2", l)))
                for j in range(4):
                    act.wait_ge(*c.full(("o2", l, j)))
                    ps = c.bank(("o2", l, j))
                    af(gated[:, 2 * j:2 * j + 2, :].rearrange("p a t -> p (a t)"), ps[:, :], ACT.Sqrt, bias=eps[:, 0:1], scale=1.0 / P).then_inc(*sc.emptied(("o2", l, j)))
                act.wait_ge(*c.at("dn_done", l))
                for j in range(4):
                    kt, h0 = j // 2, 4 * (j % 2)
                    act.wait_ge(*c.full(("svt", l, j)))
                    ps = c.bank(("svt", l, j))
                    af(vtok[:, kt, h0 * P:(h0 + 4) * P], ps[:, :], ACT.Copy).then_inc(*sc.emptied(("svt", l, j)))
                for p in range(NP2):
                    for j in range(4):
                        n = 4 * p + j
                        act.wait_ge(*c.full(("score", l, p, j)))
                        ps = c.bank(("score", l, p, j))
                        if n >= 2:
                            act.wait_ge(*c.at("scored", (l, n - 2)))
                        nk = P * (p + 1)
                        src = ps[:, :].rearrange("p (s k) -> p s k", s=2)[:, :, 0:nk]
                        af(relu[:, n % 2, :, 0:nk], src, ACT.Relu).then_inc(*sc.emptied(("score", l, p, j)))
                att_scalar(sc, ("sa", l), sa_units(l), P_of, PT_of, mx, smx)
                act.wait_ge(*sc.last())
                af(tick[:, 6:7], eps[:, 0:1], ACT.Copy).then_inc(*sc.count("sparse_done", l))
                act.wait_ge(*c.at("mem_loaded", l))
                act.wait_ge(*c.full(("o2", l, 3)))
                norm_scalar(sc, ("mem", l), memn[:, :, :], sq8, root, KT, T)
                gemm_read(sc, stream, f"mem{l}", l, lambda i, ps: af(tile_of(C, 8 + i), ps[:, 0:T], ACT.Copy))
                gemm_read(sc, stream, f"xq{l}", l, lambda i, ps: af(tile_of(C, i), ps[:, 0:T], ACT.Copy))
                for j in range(4):
                    kt, h0 = j // 2, 4 * (j % 2)
                    act.wait_ge(*c.full(("mvt", l, j)))
                    ps = c.bank(("mvt", l, j))
                    af(vtok[:, kt, h0 * P:(h0 + 4) * P], ps[:, :], ACT.Copy).then_inc(*sc.emptied(("mvt", l, j)))
                att_scalar(sc, ("xa", l), xa_units(l), P_of, PT_of, mx, smx)
                gemm_read(sc, stream, f"gates{l}", l, lambda i, ps: af(tile_of(A, i), ps[:, 0:T], ACT.Sigmoid, bias=v["b_gate"][:, bass.ds(24 * l + i, 1)]))
                act.wait_ge(*c.at("x_new", (l, "out")))
                norm_scalar(sc, ("ffn", l), x[:, :, :], sq8, root, KT, T)
                ffn_scalar(sc, stream, f"ffn{l}", l, silu, FT)
            act.wait_ge(*c.at("x_new", (DEPTH - 1, "ffn")))
            norm_scalar(sc, "final", x[:, :, :], sq8, root, KT, T)
            af(cond[:, :, :].rearrange("p k s -> p (k s)"), v["cond"], ACT.Silu).then_inc(*sc.count("cond_silu", "all"))
            act.wait_ge(*c.full("lam"))
            ps = c.bank("lam")
            af(lamb[:, 2:4], ps[:, 0:2], ACT.Exp).then_inc(*sc.emptied("lam"))
            act.wait_ge(*c.at("normed", "final"))
            act.wait_ge(*c.at("second_loaded", "all"))
            norm_scalar(sc, "e1", H, sq2, root, KT, T2)
            gemm_read(sc, stream, "even_in", 0, lambda i, ps: af(tile_of(Z, i), ps[:, :], ACT.Copy))
            for kt in range(4):
                for j in range(2):
                    act.wait_ge(*c.full(("evt", kt, j)))
                    ps = c.bank(("evt", kt, j))
                    af(vtok2[:, kt, 384 * j:384 * (j + 1)], ps[:, 0:384], ACT.Copy).then_inc(*sc.emptied(("evt", kt, j)))
            att_scalar(sc, "diff", diff_units(), lambda u: att_p2[:, u % 3], lambda u: att_t2[:, u % 3], mx2, smx2)
            act.wait_ge(*sc.last())
            af(sq2[:, 0:DH, :], Z[:, 2:2 + DH, :], ACT.Square).then_inc(*sc.count("squared", "heads"))
            for h in range(DH):
                act.wait_ge(*c.full(("heads", h)))
                ps = c.bank(("heads", h))
                af(hn2[:, h, :], ps[:, :], ACT.Sqrt, bias=eps[:, 0:1], scale=1.0 / P).then_inc(*sc.emptied(("heads", h)))
            act.wait_ge(*c.at("h_new", "e1"))
            norm_scalar(sc, "e2", H, sq2, root, KT, T2)

            even_ffn_read(sc, stream, 0, lambda f, buf, ps: af(silu2[:, buf, :], ps[:, :], ACT.Silu))
            act.wait_ge(*c.at("h_new", "e2"))
            norm_scalar(sc, "o1", H, sq2, root, KT, T2)
            gemm_read(sc, stream, "odd_in", 0, lambda i, ps: af(tile_of(Zo, i), ps[:, :], ACT.Copy))
            act.wait_ge(*sc.last())
            norm_scalar(sc, "cq", Zo[:, 0:4, 0:T], sq2, root, 4, T)
            norm_scalar(sc, "ckv", Zo[:, 4:6, :], sq2, root, 2, T2)
            gemm_read(sc, stream, "uq", 0, lambda i, ps: af(tile_of(QN, i), ps[:, 0:T], ACT.Copy))
            gemm_read(sc, stream, "ukv", 0, lambda i, ps: af(tile_of(KV, i), ps[:, :], ACT.Copy))
            for kt in range(4):
                for j in range(2):
                    act.wait_ge(*c.full(("ovt", kt, j)))
                    ps = c.bank(("ovt", kt, j))
                    af(vtok3[:, kt, 512 * j:512 * (j + 1)], ps[:, :], ACT.Copy).then_inc(*sc.emptied(("ovt", kt, j)))
            att_scalar(sc, "latent", latent_units(), lambda u: att_p3[:, u % 3], lambda u: att_t3[:, u % 3], mx2, smx2)
            act.wait_ge(*c.at("h_new", "o1"))
            norm_scalar(sc, "o2", H[:, :, 0:T], sq2, root, KT, T)
            act.wait_ge(*c.at("router_max", "all"))
            for p in range(NP2):
                ins = af(rout[:, 16 + 8 * p:24 + 8 * p], rout[:, 16 + 8 * p:24 + 8 * p], ACT.Exp, bias=rout[:, 32 + p:33 + p],
                         accum_out=rout[:, 34 + p:35 + p])
            ins.then_inc(*sc.count("router_exp", "all"))
            for j in range(4):
                act.wait_ge(*c.full(("spread", j)))
                ps = c.bank(("spread", j))
                af(expert_w[:, 2 * j:2 * j + 2, :], ps[:, :].rearrange("p (a t) -> p a t", a=2), ACT.Copy).then_inc(*sc.emptied(("spread", j)))
            ffn_scalar(sc, stream, "moe", "moe", silu, FT * NE)
            act.wait_ge(*c.at("h_new", "moe"))
            norm_scalar(sc, "last", H[:, :, 0:T], sq2, root, KT, T)

        @block.vector
        def _(dve):
            ve = Engine(c, dve, "vector")
            tt, ts, stt, copy = nc.vector.tensor_tensor, nc.vector.tensor_scalar, nc.vector.scalar_tensor_tensor, nc.vector.tensor_copy
            for b in range(BANKS):
                nc.vector.memset(c.banks[b][:, :], 0.0).then_inc(c.sem(f"bank_read{b}"), 1)
            nc.vector.memset(eps[:, 0:1], EPS).then_inc(*ve.count())
            nc.vector.memset(eps[:, 1:2], 1.0).then_inc(*ve.count("eps", "all"))
            dve.wait_ge(*c.at("pos_loaded", "all"))
            dve.wait_ge(*c.at("const_loaded", "all"))
            copy(squares[:, 0:T], root[:, 0:T].bitcast(I32)).then_inc(*ve.count())
            dve.wait_ge(*ve.last())
            for i in range(2):
                ang, n, cs, sn = squares[:, 256:512], squares[:, 512:768], rope[:, 2 * i, :], rope[:, 2 * i + 1, :]
                ts(ang, squares[:, 0:T], k["invf"][:, i:i + 1], None, ALU.mult).then_inc(*ve.count())
                dve.wait_ge(*ve.last())
                ts(n, ang, 1.0 / (2 * math.pi), ROUND, ALU.mult, ALU.add).then_inc(*ve.count())
                dve.wait_ge(*ve.last())
                ts(n, n, -ROUND, None, ALU.add).then_inc(*ve.count())
                for part in TWO_PI_PARTS:
                    dve.wait_ge(*ve.last())
                    stt(out=ang, in0=n, scalar=-part, in1=ang, op0=ALU.mult, op1=ALU.add).then_inc(*ve.count())
                dve.wait_ge(*ve.last())
                ts(sn, ang, 3.14159, -3.14159, ALU.min, ALU.max).then_inc(*ve.count())
                dve.wait_ge(*ve.last())
                stt(out=cs, in0=sn, scalar=-1.0, in1=sn, op0=ALU.mult, op1=ALU.max).then_inc(*ve.count())
                dve.wait_ge(*ve.last())
                ts(cs, cs, -1.0, math.pi / 2, ALU.mult, ALU.add).then_inc(*ve.count("angle", i))
                dve.wait_ge(*ve.last())
            dve.wait_ge(*c.at("vec_loaded", "all"))
            for l in range(DEPTH):
                if l:
                    dve.wait_ge(*ve.last())
                norm_vector(ve, ("mix", l), x, v["norm_mix"][:, 8 * l:8 * l + 8], root, hn, KT, T)
                for g in range(3):
                    dve.wait_ge(*c.empty((f"dn{l}", l, 8 * g + 7)))
                    if g == 2:
                        dve.wait_ge(*c.at("conv_silu", (l, 0)))
                    acc = conv[g % 2]
                    for tap in range(4):
                        for i in range(8):
                            w = v["conv"][:, 96 * l + 4 * (8 * g + i) + 3 - tap:][:, 0:1]
                            if tap == 0:
                                ins = ts(acc[:, i, :], A[:, 8 * g + i, :], w, None, ALU.mult)
                            else:
                                ins = stt(out=acc[:, i, tap:], in0=A[:, 8 * g + i, 0:T - tap], scalar=w,
                                          in1=acc[:, i, tap:], op0=ALU.mult, op1=ALU.add)
                        if tap < 3:
                            ins.then_inc(*ve.count())
                            dve.wait_ge(*ve.last())
                    ins.then_inc(*ve.count("conv", (l, g)))
                dve.wait_ge(*c.empty(("narrow", l)))
                two = lambda a: a.rearrange("p (a b) -> p a b", a=2)
                tt(two(y0), stok[:, :, 72:80], v["dt_bias"][:, 8 * l:8 * l + 8].unsqueeze(1).to_broadcast([P, 2, 8]), ALU.add).then_inc(*ve.count())
                dve.wait_ge(*ve.last())
                ts(y2, y0, -1.0, None, ALU.mult).then_inc(*ve.count())
                dve.wait_ge(*ve.last())
                tt(y1, y0, y2, ALU.min).then_inc(*ve.count("decay_in", l))
                ts(iw.rearrange("p (a b) -> p a b", a=2), stok[:, :, 80:88], 8 ** -0.5 * 64 ** -0.5, None, ALU.mult).then_inc(*ve.count())
                for g in range(2):
                    for j in range(4):
                        dve.wait_ge(*c.empty(("l2", l, g, j)))
                    dve.wait_ge(*ve.last())
                    nc.vector.reciprocal(sroot, sroot).then_inc(*ve.count())
                    dve.wait_ge(*ve.last())
                    at = A[:, 8 * g:8 * g + 8, :]
                    stt(out=at, in0=at, scalar=(P ** -0.5 if g == 0 else 1.0), in1=sroot, op0=ALU.mult, op1=ALU.mult).then_inc(*ve.count("unit", (l, g)))
                dve.wait_ge(*c.at("decay_ln", l))
                stt(out=y2, in0=y0, scalar=0.0, in1=y1, op0=ALU.max, op1=ALU.add).then_inc(*ve.count())
                dve.wait_ge(*ve.last())
                stt(out=two(gate), in0=two(y2), scalar=-1.0, in1=gneg.unsqueeze(1).to_broadcast([P, 2, 8]), op0=ALU.mult, op1=ALU.mult).then_inc(*ve.count("decay_log", l))
                dve.wait_ge(*c.full(("sums", l)))
                ps = c.bank(("sums", l))
                copy(graw, ps[:, 0:64]).then_inc(*ve.emptied(("sums", l)))
                dve.wait_ge(*ve.last())
                nc.vector.memset(tick[:, 0:1], 0.0).then_inc(*ve.count("sums_copied", l))
                dve.wait_ge(*c.at("sums_exp", l))
                dve.wait_ge(*c.at("beta", l))
                tt(bexp, beta, gexp[:, 0:16], ALU.mult).then_inc(*ve.count())
                dve.wait_ge(*ve.last())
                four = lambda a: a.unsqueeze(2).to_broadcast([P, 4, P])
                per = lambda ps: ps[:, :].rearrange("p (a b) -> p a b", b=P)
                for g in range(4):
                    s4 = slice(4 * g, 4 * g + 4)
                    dve.wait_ge(*c.full(("ktok", l, g)))
                    ps = c.bank(("ktok", l, g))
                    tt(KB[:, s4, :], per(ps), four(bexp[:, s4]), ALU.mult).then_inc(*ve.count())
                    tt(KD[:, s4, :], per(ps), four(gexp[:, 16 + 4 * g:20 + 4 * g]), ALU.mult).then_inc(*ve.emptied(("ktok", l, g)))
                    dve.wait_ge(*c.full(("vtok", l, g)))
                    ps = c.bank(("vtok", l, g))
                    tt(VB[:, s4, :], per(ps), four(beta[:, s4]), ALU.mult).then_inc(*ve.emptied(("vtok", l, g)))
                dve.wait_ge(*ve.last())
                nc.vector.memset(tick[:, 0:1], 0.0).then_inc(*ve.count("toks", l))
                for g in range(4):
                    p, h0 = g // 2, 4 * (g % 2)
                    s4 = slice(4 * g, 4 * g + 4)
                    dve.wait_ge(*c.at("cum_exp", (l, g)))
                    dve.wait_ge(*c.full(("cum", l, g)))
                    ps = c.bank(("cum", l, g))
                    dec, dect, egb = per(DEC), per(DECT), per(EGB)
                    for i in range(4):
                        gc = graw[:, 4 * g + i:4 * g + i + 1]
                        ts(dec[:, i, :], per(ps)[:, i, :], gc, 0.0, ALU.subtract, ALU.max)
                        ins = ts(dect[:, i, :], per(ps)[:, i, :], gc, 0.0, ALU.subtract, ALU.min)
                    ins.then_inc(*ve.count("decay_diff", (l, g)))
                    dve.wait_ge(*c.at("decay_exp", (l, g)))
                    tt(dec, dec, k["strict"].unsqueeze(1).to_broadcast([P, 4, P]), ALU.mult).then_inc(*ve.emptied(("cum", l, g)))
                    tt(dect, dect, k["incl"].unsqueeze(1).to_broadcast([P, 4, P]), ALU.mult).then_inc(*ve.count())
                    dve.wait_ge(*ve.last())
                    dve.wait_ge(*c.full(("kk", l, g)))
                    ps = c.bank(("kk", l, g))
                    for i in range(4):
                        ins = stt(out=M[:, 4 * g + i, :], in0=per(ps)[:, i, :], scalar=beta[:, 4 * g + i:4 * g + i + 1], in1=dec[:, i, :], op0=ALU.mult, op1=ALU.mult)
                    ins.then_inc(*ve.emptied(("kk", l, g)))
                    dve.wait_ge(*c.full(("kq", l, g)))
                    ps = c.bank(("kq", l, g))
                    tt(AT[:, s4, :], per(ps), dect, ALU.mult).then_inc(*ve.emptied(("kq", l, g)))
                    q = A[:, h0:h0 + 4, p * P:(p + 1) * P]
                    tt(q, q, egb, ALU.mult).then_inc(*ve.count("qdec", (l, g)))
                    dve.wait_ge(*ve.last())
                    mk = MK[:, s4, :]
                    tt(mk, M[:, s4, :], k["merge0"].unsqueeze(1).to_broadcast([P, 4, P]), ALU.mult).then_inc(*ve.count())
                    dve.wait_ge(*ve.last())
                    tt(Pl[:, s4, :], k["ident"].unsqueeze(1).to_broadcast([P, 4, P]), mk, ALU.subtract).then_inc(*ve.count("inv0", (l, g)))
                dve.wait_ge(*ve.last())
                for lev in range(1, 6):
                    for g in range(4):
                        s4 = slice(4 * g, 4 * g + 4)
                        if lev > 1:
                            dve.wait_ge(*c.full(("ny", l, lev - 1, g)))
                        tt(MK[:, s4, :], M[:, s4, :], k[f"merge{lev}"].unsqueeze(1).to_broadcast([P, 4, P]), ALU.mult).then_inc(*ve.count("merge_mask", (l, lev, g)))
                    for g in range(4):
                        s4 = slice(4 * g, 4 * g + 4)
                        if lev == 1:
                            dve.wait_ge(*c.empty(("x0", l, g)))
                        dve.wait_ge(*c.full(("nx", l, lev, g)))
                        ps = c.bank(("nx", l, lev, g))
                        ins = tt(X[:, s4, :], X[:, s4, :], per(ps), ALU.subtract)
                        if lev < 5:
                            ins.then_inc(*ve.emptied(("nx", l, lev, g)))
                            dve.wait_ge(*c.full(("np", l, lev, g)))
                            ps = c.bank(("np", l, lev, g))
                            ins = tt(Pl[:, s4, :], Pl[:, s4, :], per(ps), ALU.subtract)
                            ins.then_inc(*ve.emptied(("np", l, lev, g)))
                        else:
                            ins.then_inc(*ve.emptied(("nx", l, lev, g)))
                        dve.wait_ge(*ve.last())
                        nc.vector.memset(tick[:, 0:1], 0.0).then_inc(*ve.count("inv", (l, lev, g)))
                nc.vector.memset(S, 0.0).then_inc(*ve.count("state", (l, 0)))
                for ch in range(NCH):
                    p, r = ch // 2, 64 * (ch % 2)
                    rows = slice(r, r + 64)
                    for j in range(2):
                        dve.wait_ge(*c.empty(("u", l, 2 * p + j)))
                        dve.wait_ge(*c.full(("ws", l, ch, j)))
                        ps = c.bank(("ws", l, ch, j))
                        hs = slice(4 * j, 4 * j + 4)
                        if ch >= 1:
                            dve.wait_ge(*c.full(("su", l, ch - 1, 1)))
                        tt(VN[rows, hs, :], UU[rows, 8 * p + 4 * j:8 * p + 4 * j + 4, :], per(ps)[rows], ALU.subtract).then_inc(*ve.emptied(("ws", l, ch, j)))
                    dve.wait_ge(*ve.last())
                    nc.vector.memset(tick[:, 0:1], 0.0).then_inc(*ve.count("vnew", (l, ch)))
                    if ch < NCH - 1:
                        dve.wait_ge(*c.full(("o", l, ch)))
                        for j in range(2):
                            dve.wait_ge(*c.full(("su", l, ch, j)))
                            ps = c.bank(("su", l, ch, j))
                            for i in range(4):
                                h = 4 * j + i
                                cd = gexp[:, 32 + 16 * (ch % 2) + 8 * p + h:][:, 0:1]
                                ins = stt(out=S[:, h, :], in0=S[:, h, :], scalar=cd, in1=per(ps)[:, i, :], op0=ALU.mult, op1=ALU.add)
                            ins.then_inc(*ve.emptied(("su", l, ch, j)))
                        dve.wait_ge(*ve.last())
                        nc.vector.memset(tick[:, 0:1], 0.0).then_inc(*ve.count("state", (l, ch + 1)))
                for j in range(4):
                    dve.wait_ge(*c.empty(("o2", l, j)))
                dve.wait_ge(*c.at("z_silu", l))
                dve.wait_ge(*ve.last())
                nc.vector.reciprocal(gated, gated).then_inc(*ve.count())
                dve.wait_ge(*ve.last())
                o = A[:, 16:24, :]
                stt(out=o, in0=o, scalar=v["dn_norm"][:, l:l + 1], in1=gated, op0=ALU.mult, op1=ALU.mult).then_inc(*ve.count())
                dve.wait_ge(*ve.last())
                tt(A[:, 24:32, :], A[:, 24:32, :], o, ALU.mult).then_inc(*ve.count("dn_done", l))
                dve.wait_ge(*ve.last())
                dve.wait_ge(*c.at("sincos", (1, 0)))
                for j in range(8):
                    dve.wait_ge(*c.full(("rope", l, j)))
                    ps = c.bank(("rope", l, j))
                    r32 = slice(0, 32)
                    t = ropet[r32, j % 2]
                    xx = Bq[r32, 2 * j:2 * j + 2, :]
                    tt(t, ps[r32, :].rearrange("p (a t) -> p a t", a=2), rope[r32, 1:2, :].to_broadcast([32, 2, T]), ALU.mult).then_inc(*ve.emptied(("rope", l, j)))
                    tt(xx, xx, rope[r32, 0:1, :].to_broadcast([32, 2, T]), ALU.mult).then_inc(*ve.count())
                    dve.wait_ge(*ve.last())
                    tt(xx, xx, t, ALU.add).then_inc(*ve.count("roped", (l, j)))
                c.found[("roped", l)] = c.counted["roped"]
                for j in range(2):
                    dve.wait_ge(*c.full(("ropei", l, j)))
                    ps = c.bank(("ropei", l, j))
                    t = ropet[:, j % 2]
                    xx = Bq[:, 24 + 2 * j:26 + 2 * j, :]
                    dve.wait_ge(*ve.last())
                    tt(t, ps[:, :].rearrange("p (a t) -> p a t", a=2), rope[:, 3:4, :].to_broadcast([P, 2, T]), ALU.mult).then_inc(*ve.emptied(("ropei", l, j)))
                    tt(xx, xx, rope[:, 2:3, :].to_broadcast([P, 2, T]), ALU.mult).then_inc(*ve.count())
                    dve.wait_ge(*ve.last())
                    tt(xx, xx, t, ALU.add).then_inc(*ve.count())
                dve.wait_ge(*c.full(("ik", l)))
                ps = c.bank(("ik", l))
                t = ropet[:, 0, 0]
                dve.wait_ge(*ve.last())
                tt(t, ps[:, T:2 * T], rope[:, 3, :], ALU.mult).then_inc(*ve.count())
                tt(ixk, ps[:, 0:T], rope[:, 2, :], ALU.mult).then_inc(*ve.emptied(("ik", l)))
                dve.wait_ge(*ve.last())
                tt(ixk, ixk, t, ALU.add).then_inc(*ve.count("index_rope", l))
                for p in range(NP2):
                    nk = P * (p + 1)
                    for j in range(4):
                        dve.wait_ge(*c.empty(("score", l, p, j)))
                        for i in range(2):
                            h = 2 * (2 * (j // 2) + i) + j % 2
                            prev = k["admit"][:, P * p:P * p + nk] if h == 0 else score[:, 0:nk]
                            dve.wait_ge(*ve.last())
                            stt(out=score[:, 0:nk], in0=relu[:, (4 * p + j) % 2, i, 0:nk], scalar=iw[:, 8 * p + h:8 * p + h + 1],
                                        in1=prev, op0=ALU.mult, op1=ALU.add).then_inc(*ve.count("scored", (l, 4 * p + j)))
                    for n in range(TOPK // 8):
                        src = score if n == 0 else work
                        dve.wait_ge(*ve.last())
                        nc.vector.max(m8, src[:, 0:nk]).then_inc(*ve.count())
                        dve.wait_ge(*ve.last())
                        nc.vector.match_replace(work[:, 0:nk], m8, src[:, 0:nk], TAKEN).then_inc(*ve.count())
                    dve.wait_ge(*ve.last())
                    ts(negm[:, p, 0:nk], work[:, 0:nk], 10 * NEG * 1e7, -NEG, ALU.is_le, ALU.mult).then_inc(*ve.count())
                    dve.wait_ge(*ve.last())
                    ts(negm[:, p, 0:nk], negm[:, p, 0:nk], NEG, None, ALU.add).then_inc(*ve.count())
                att_vector(ve, ("sa", l), sa_units(l), P_of, mx, smx, P ** -0.5)
                norm_vector(ve, ("mem", l), memn, v["norm_mem"][:, 8 * l:8 * l + 8], root, memn, KT, T)
                att_vector(ve, ("xa", l), xa_units(l), P_of, mx, smx, 1.0 / 16)
                _, g0, _, _, _ = stream.phases[f"branch{l}"]
                dve.wait_ge(*c.empty((f"gates{l}", l, 23)))
                for n in range(KT):
                    for b in range(3):
                        g = g0 + 3 * n + b
                        dve.wait_ge(c.sem(f"slab_done{g % RING}"), g // RING + 1)
                        ps = c.banks[g % RING]
                        dst = merged[:, n, :] if b == 0 else att_p[:, 0, b - 1, 0:T]
                        if b:
                            dve.wait_ge(*ve.last())
                        tt(dst, ps[:, 0:T], A[:, 8 * b + n, :], ALU.mult).then_inc(*ve.emptied(("branch", l, 3 * n + b)))
                    for b in range(2):
                        dve.wait_ge(*ve.last())
                        tt(merged[:, n, :], merged[:, n, :], att_p[:, 0, b, 0:T], ALU.add).then_inc(*ve.count("merged", (l, n)))
                def add_x(i, ps):
                    return tt(x[:, i, :], x[:, i, :], ps[:, 0:T], ALU.add)
                gemm_read(ve, stream, f"out{l}", l, add_x)
                dve.wait_ge(*ve.last())
                nc.vector.memset(tick[:, 0:1], 0.0).then_inc(*ve.count("x_new", (l, "out")))
                norm_vector(ve, ("ffn", l), x, v["norm_ffn"][:, 8 * l:8 * l + 8], root, hn, KT, T)
                ffn_vector(ve, stream, f"ffn{l}", l, silu, hidden, tick, FT)
                dve.wait_ge(*c.summed(l))
                for b in range(4):
                    xx = x[:, 2 * b:2 * b + 2, :]
                    tt(xx, xx, c.banks[b][:, :].rearrange("p (a t) -> p a t", a=2), ALU.add).then_inc(*ve.emptied((l, "ffn", b)))
                dve.wait_ge(*ve.last())
                nc.vector.memset(tick[:, 0:1], 0.0).then_inc(*ve.count("x_new", (l, "ffn")))
            norm_vector(ve, "final", x, v["norm_final"], root, H, KT, T)
            dve.wait_ge(*ve.last())
            tt(lamb[:, 0:1], v["lam"][:, 0:1], v["lam"][:, 1:2], ALU.mult).then_inc(*ve.count())
            tt(lamb[:, 1:2], v["lam"][:, 2:3], v["lam"][:, 3:4], ALU.mult).then_inc(*ve.count("lam_prod", "all"))
            for l in range(DEPTH):
                gemm_read(ve, stream, f"mod{l}", l, lambda i, ps: ts(
                    mods[:, l, bass.ds(i, 1), :].rearrange("p a s -> p (a s)"), ps[:, 0:2], v["mod_b"][:, bass.ds(48 * l + i, 1)], None, ALU.add))
            dve.wait_ge(*c.empty("lam"))
            dve.wait_ge(*ve.last())
            stt(out=lamb[:, 4:5], in0=lamb[:, 2:3], scalar=LAM_INIT, in1=lamb[:, 3:4], op0=ALU.add, op1=ALU.subtract).then_inc(*ve.count())
            for n, (l, at, g) in enumerate(((0, 1, "norm1"), (0, 4, "norm2"), (1, 1, "norm1"), (1, 4, "norm2"))):
                for s in range(2):
                    stt(out=gains[:, 2 * n + s, :], in0=mod(l, at, s), scalar=1.0, in1=v[g][:, 8 * l:8 * l + 8], op0=ALU.add, op1=ALU.mult).then_inc(*ve.count())
            dve.wait_ge(*ve.last())

            def streams(n, l, at):
                return [(slice(s * T, (s + 1) * T), gains[:, 2 * n + s, :], mod(l, at, s)) for s in range(2)]

            def gated_add(l, at, n, ps, ss=(0, 1)):
                for s in ss:
                    hh = H[:, n, s * T:(s + 1) * T]
                    ins = stt(out=hh, in0=ps[:, s * T:(s + 1) * T], scalar=mods[:, l, 8 * at + n, s:s + 1], in1=hh, op0=ALU.mult, op1=ALU.add)
                return ins
            norm_vector(ve, "e1", H, None, root, hn2, KT, T2, streams(0, 0, 0))
            for j in range(6):
                dve.wait_ge(*c.full(("axial", j)))
                ps = c.bank(("axial", j))
                t = att_p2[:, j % 3, 0, :].rearrange("p (a t) -> p a t", a=2)
                xx = Z[:, 2 + 2 * j:4 + 2 * j, 0:T]
                wide = lambda a: a.unsqueeze(1).to_broadcast([P, 2, T])
                tt(t, ps[:, :].rearrange("p (a t) -> p a t", a=2), wide(sin2), ALU.mult).then_inc(*ve.emptied(("axial", j)))
                tt(xx, xx, wide(cos2), ALU.mult).then_inc(*ve.count())
                dve.wait_ge(*ve.last())
                tt(xx, xx, t, ALU.add).then_inc(*ve.count("axial_done", j))
            u, sa, sb_ = pools
            for a in pools:
                ins = nc.vector.memset(a.rearrange("p s e t -> p (s e t)"), 0.0)
            ins.then_inc(*ve.count())
            dve.wait_ge(*ve.last())
            zz = Z[:, 0:2, :].rearrange("p s (e t) -> p s e t", e=2)
            for s in range(2):
                ins = copy(u[:, s, :, 8:264], zz[:, s])
            ins.then_inc(*ve.count())
            dve.wait_ge(*ve.last())
            two_rows = (slice(0, 64), slice(64, 128))
            for s in range(2):
                ins = tt(sa[:, s, :, 1:272], u[:, s, :, 0:271], u[:, s, :, 1:272], ALU.add)
            ins.then_inc(*ve.count())
            dve.wait_ge(*ve.last())
            for s in range(2):
                ins = tt(sb_[:, s, :, 2:271], sa[:, s, :, 1:270], sa[:, s, :, 3:272], ALU.add)
            ins.then_inc(*ve.count())
            dve.wait_ge(*ve.last())
            tt(sa[:, 1, :, 4:269], sb_[:, 1, :, 2:267], sb_[:, 1, :, 6:271], ALU.add).then_inc(*ve.count())
            dve.wait_ge(*ve.last())
            r = two_rows[1]
            tt(sb_[r, 1, :, 8:264], sa[r, 1, :, 4:260], sa[r, 1, :, 12:268], ALU.add).then_inc(*ve.count())
            dve.wait_ge(*ve.last())
            for s in range(2):
                for r, a in zip(two_rows, (sa, sb_)):
                    inv = rope[r, 2 + s:3 + s, :].to_broadcast([64, 2, T])
                    ins = tt(a[r, s, :, 8:264], a[r, s, :, 8:264], inv, ALU.mult)
            ins.then_inc(*ve.count())
            dve.wait_ge(*ve.last())
            for s in range(2):
                for r, a in zip(two_rows, (sa, sb_)):
                    ins = tt(zz[r, s], a[r, s, :, 8:264], zz[r, s], ALU.subtract)
            ins.then_inc(*ve.count("pooled", "all"))
            for j in range(2):
                dve.wait_ge(*c.full(("pool", j)))
                ps = c.bank(("pool", j))
                ts(Z[:, j, :], ps[:, :], v["pool_scale"][:, j:j + 1], None, ALU.mult).then_inc(*ve.emptied(("pool", j)))
            dve.wait_ge(*ve.last())
            att_vector(ve, "diff", diff_units(), lambda u: att_p2[:, u % 3], mx2, smx2, 64 ** -0.5, combine=lamb[:, 4:5])
            for h in range(DH):
                dve.wait_ge(*c.empty(("heads", h)))
                nc.vector.reciprocal(hn2[:, h, :], hn2[:, h, :]).then_inc(*ve.count())
                dve.wait_ge(*ve.last())
                stt(out=Z[:, 2 + h, :], in0=Z[:, 2 + h, :], scalar=1.0 - LAM_INIT, in1=hn2[:, h, :], op0=ALU.mult, op1=ALU.mult).then_inc(*ve.count("heads_normed", "all"))
            for i in range(KT):
                tag = ("even_out", 0, i)
                _, g0, _, _, _ = stream.phases["even_out"]
                g = g0 + i
                dve.wait_ge(c.sem(f"slab_done{g % RING}"), g // RING + 1)
                gated_add(0, 2, i, c.banks[g % RING]).then_inc(*ve.emptied(tag))
            dve.wait_ge(*ve.last())
            nc.vector.memset(tick[:, 0:1], 0.0).then_inc(*ve.count("h_new", "e1"))
            norm_vector(ve, "e2", H, None, root, hn2, KT, T2, streams(1, 0, 3))
            even_ffn_read(ve, stream, 1, lambda f, buf, ps: tt(tile_of(hidden2, f), silu2[:, buf, :], ps[:, :], ALU.mult))
            _, g0, _, _, _ = stream.phases["even_down"]
            for n in range(KT):
                g = g0 + 3 * n + 2
                dve.wait_ge(c.sem(f"slab_done{g % RING}"), g // RING + 1)
                ps = c.bank(("even_down", n))
                gated_add(0, 5, n, ps).then_inc(*ve.emptied(("even_down", n)))
            dve.wait_ge(*ve.last())
            nc.vector.memset(tick[:, 0:1], 0.0).then_inc(*ve.count("h_new", "e2"))
            norm_vector(ve, "o1", H, None, root, hn2, KT, T2, streams(2, 1, 0))
            norm_vector(ve, "cq", Zo, v["q_norm"], root, cqn, 4, T)
            norm_vector(ve, "ckv", Zo[:, 4:6, :], v["kv_norm"], root, ckvn, 2, T2)
            for j in range(2):
                dve.wait_ge(*c.full(("axq", j)))
                ps = c.bank(("axq", j))
                t = att_p3[:, j, 0, :].rearrange("p (a t) -> p a t", a=2)
                xx = QN[:, 8 + 2 * j:10 + 2 * j, :]
                tt(t, ps[:, :].rearrange("p (a t) -> p a t", a=2), wide(sin2), ALU.mult).then_inc(*ve.emptied(("axq", j)))
                tt(xx, xx, wide(cos2), ALU.mult).then_inc(*ve.count())
                dve.wait_ge(*ve.last())
                tt(xx, xx, t, ALU.add).then_inc(*ve.count())
            dve.wait_ge(*c.full("axk"))
            ps = c.bank("axk")
            t = att_p3[:, 2, 0, 0:T]
            tt(t, ps[:, 0:T], sin2, ALU.mult).then_inc(*ve.emptied("axk"))
            tt(Zo[:, 6, 0:T], Zo[:, 6, 0:T], cos2, ALU.mult).then_inc(*ve.count())
            dve.wait_ge(*ve.last())
            tt(Zo[:, 6, 0:T], Zo[:, 6, 0:T], t, ALU.add).then_inc(*ve.count("axial2_done", "all"))
            dve.wait_ge(*ve.last())
            att_vector(ve, "latent", latent_units(), lambda u: att_p3[:, u % 3], mx2, smx2, 192 ** -0.5)
            gemm_read(ve, stream, "odd_out", 0, lambda i, ps: gated_add(1, 2, i, ps, (0,)))
            dve.wait_ge(*ve.last())
            nc.vector.memset(tick[:, 0:1], 0.0).then_inc(*ve.count("h_new", "o1"))
            norm_vector(ve, "o2", H, None, root, hn, KT, T, streams(3, 1, 3)[0:1])
            dve.wait_ge(*c.full("router"))
            ps = c.bank("router")
            lg = rout[:, 16:32].rearrange("p (a e) -> p a e", a=2)
            copy(lg, ps[:, 0:16].rearrange("p (a e) -> p a e", a=2)).then_inc(*ve.emptied("router"))
            dve.wait_ge(*ve.last())
            nc.vector.tensor_reduce(rout[:, 32:34], lg, AXX, ALU.max).then_inc(*ve.count())
            dve.wait_ge(*ve.last())
            ts(rout[:, 32:34], rout[:, 32:34], -1.0, None, ALU.mult).then_inc(*ve.count("router_max", "all"))
            dve.wait_ge(*c.at("router_exp", "all"))
            nc.vector.reciprocal(rout[:, 34:36], rout[:, 34:36]).then_inc(*ve.count())
            dve.wait_ge(*ve.last())
            for p in range(NP2):
                ins = ts(lg[:, p, :], lg[:, p, :], rout[:, 34 + p:35 + p], None, ALU.mult)
            ins.then_inc(*ve.count())
            higher = rout[:, 40:56].rearrange("p (a e) -> p a e", a=2)
            nc.vector.memset(rout[:, 40:56], 0.0).then_inc(*ve.count())
            for j in range(NE):
                for p in range(NP2):
                    dve.wait_ge(*ve.last())
                    stt(out=higher[:, p, :], in0=lg[:, p, :], scalar=lg[:, p, j:j + 1], in1=higher[:, p, :], op0=ALU.is_lt, op1=ALU.add).then_inc(*ve.count())
                    if j < NE - 1:
                        dve.wait_ge(*ve.last())
                        stt(out=higher[:, p, j + 1:], in0=lg[:, p, j + 1:], scalar=lg[:, p, j:j + 1], in1=higher[:, p, j + 1:], op0=ALU.is_equal, op1=ALU.add).then_inc(*ve.count())
            dve.wait_ge(*ve.last())
            ww = rout[:, 0:16].rearrange("p (a e) -> p a e", a=2)
            stt(out=ww, in0=higher, scalar=2.0, in1=lg, op0=ALU.is_lt, op1=ALU.mult).then_inc(*ve.count())
            dve.wait_ge(*ve.last())
            nc.vector.tensor_reduce(rout[:, 36:38], ww, AXX, ALU.add).then_inc(*ve.count())
            dve.wait_ge(*ve.last())
            nc.vector.reciprocal(rout[:, 36:38], rout[:, 36:38]).then_inc(*ve.count())
            dve.wait_ge(*ve.last())
            for p in range(NP2):
                ins = ts(ww[:, p, :], ww[:, p, :], rout[:, 36 + p:37 + p], None, ALU.mult)
            ins.then_inc(*ve.count("routed", "all"))
            dve.wait_ge(*c.empty(("spread", 3)))
            ffn_vector(ve, stream, "moe", "moe", silu, hidden, tick, FT * NE, weight=lambda e: tile_of(expert_w, e))
            dve.wait_ge(*c.summed("moe"))
            for b in range(4):
                gated_add(1, 5, 2 * b, c.banks[b][:, 0:T], (0,))
                gated_add(1, 5, 2 * b + 1, c.banks[b][:, T:2 * T], (0,)).then_inc(*ve.emptied(("moe", "ffn", b)))
            dve.wait_ge(*ve.last())
            nc.vector.memset(tick[:, 0:1], 0.0).then_inc(*ve.count("h_new", "moe"))
            norm_vector(ve, "last", H, v["final_2"], root, x, KT, T)
            dve.wait_ge(*ve.last())
            nc.vector.memset(tick[:, 0:1], 0.0).then_inc(*ve.count("result", "x"))
    return c.found

def slabs(w, rows=None):
    kt, n = w.shape[0] // P, w.shape[1] // P
    return np.ascontiguousarray(w.reshape(kt, P, n, P).transpose(2, 1, 0, 3)).reshape(n, P, kt * P)


def features_first(a):
    return np.ascontiguousarray(np.asarray(a).T.reshape(-1, P, a.shape[0]).transpose(1, 0, 2))


def columns(a):
    return np.asarray(a).reshape(-1, P).T


def lay_out(i):
    sizes = (1024, 1024, 1024, 1024, 8, 8, 1024, 1024, 1024, 512, 64, 8, 1024, 3072)
    at = np.concatenate([[0], np.cumsum(sizes)])
    out = {}
    w_in = []
    for l in range(DEPTH):
        w = np.asarray(i["w_in"])[l]
        part = [w[:, at[n]:at[n + 1]] for n in range(len(sizes))]
        dq, dk, dv, dz, db, da, sq, sk, sv, iq, ik, iw, xq, gl = part
        narrow = np.zeros((D, P), np.float32)
        narrow[:, 0:64], narrow[:, 64:72], narrow[:, 72:80], narrow[:, 80:88] = ik, db, da, iw
        w_in.append(slabs(np.concatenate([dq, dk, dv, dz, narrow, sq, sk, sv, iq, xq, gl], axis=1)))
    out["w_in"] = np.stack(w_in)
    out["w_mem"] = np.stack([slabs(np.asarray(i["w_mem_kv"])[l]) for l in range(DEPTH)])
    wb = np.asarray(i["w_branch"])
    out["w_branch"] = np.stack([np.stack([slabs(wb[l, b]) for b in range(3)], axis=1).reshape(24, P, SLAB)
                                for l in range(DEPTH)])
    out["w_out"] = np.stack([slabs(np.asarray(i["w_out"])[l]) for l in range(DEPTH)])
    out["w_ffn"] = np.stack([ffn_slabs(np.asarray(i["w_ffn_in"])[l][:, :F_HID], np.asarray(i["w_ffn_in"])[l][:, F_HID:],
                                       np.asarray(i["w_ffn_out"])[l]) for l in range(DEPTH)])
    out["x"] = features_first(np.asarray(i["x"])[0])
    out["mem"] = features_first(np.asarray(i["mem"])[0])
    out["pos"] = np.asarray(i["positions"]).reshape(1, T)
    conv = np.asarray(i["conv_w"])
    per_layer = lambda a: np.concatenate([columns(np.asarray(a)[l]) for l in range(DEPTH)], axis=1)
    rows = lambda a: np.broadcast_to(np.asarray(a).reshape(1, -1), (P, 16))
    second = lambda n: np.asarray(i[n + "_2"])
    out["mod_w"] = np.stack([slabs(second("mod_w")[l]) for l in range(DEPTH)])
    out["even_in"] = slabs(second("even_w_in")[0])
    out["even_out"] = slabs(second("even_w_out")[0])
    out["even_ffn"] = np.stack([slabs(second("ffn_w_gate")[0]), slabs(second("ffn_w_up")[0])], axis=1).reshape(2 * FT, P, SLAB)
    down = np.zeros((3 * KT * P, D), np.float32)
    down[0:F_HID] = second("ffn_w_down")[0]
    out["even_down"] = slabs(down).reshape(KT, P, 3, SLAB).transpose(0, 2, 1, 3).reshape(3 * KT, P, SLAB)
    odd = second("odd_w_in")[0]
    out["odd_in"] = slabs(np.concatenate([odd[:, 0:832], odd[:, 768:832]], axis=1))
    uq = second("w_uq")[0].reshape(512, MH, 192)
    out["w_uq"] = slabs(np.concatenate([uq[:, :, 0:128].reshape(512, D), uq[:, :, 128:].reshape(512, 512)], axis=1))
    ukv = second("w_ukv")[0].reshape(256, MH, 256)
    out["w_ukv"] = slabs(np.concatenate([ukv[:, :, 0:128].reshape(256, D), ukv[:, :, 128:].reshape(256, D)], axis=1))
    out["odd_out"] = slabs(second("odd_w_out")[0])
    gate, up, down = (second(n)[0] for n in ("moe_w_gate", "moe_w_up", "moe_w_down"))
    out["moe"] = np.concatenate([ffn_slabs(gate[e], up[e], down[e]) for e in range(NE)])
    out["ctx"] = features_first(second("ctx")[0])
    out["tables2"], out["rot_ax"] = TABLES_2, ROT_AX
    pool = second("pool_w")[0]
    out["pool_w"] = np.zeros((P, 2 * P), np.float32)
    for g in range(4):
        r = 64 * (g % 2)
        out["pool_w"][r:r + 64, P * (g // 2) + r:P * (g // 2) + r + 64] = pool[g]
    lam = np.zeros((P, 4), np.float32)
    for j, n in enumerate(("lambda_q1", "lambda_k1", "lambda_q2", "lambda_k2")):
        lam[0:64, j] = second(n)[0]
    vec = dict(
        cond=np.stack([columns(second("c")[0]), columns(second("c_ctx"))], axis=2).reshape(P, 16),
        norm1=per_layer(i["norm1_g_2"]), norm2=per_layer(i["norm2_g_2"]), mod_b=per_layer(i["mod_b_2"]),
        pool_scale=columns(second("pool_scale")[0]), lam=lam, q_norm=columns(second("q_norm_g")[0]),
        kv_norm=columns(second("kv_norm_g")[0]), final_2=columns(second("final_norm_g")),
        router=second("router_w")[0].reshape(KT, P, NE).transpose(1, 0, 2).reshape(P, 64),
        norm_mix=per_layer(i["norm_mix"]), norm_mem=per_layer(i["norm_mem"]), norm_ffn=per_layer(i["norm_ffn"]),
        norm_final=columns(i["norm_final"]), dn_norm=per_layer(i["dn_norm"]),
        conv=np.concatenate([conv[l].reshape(4, 24, P).transpose(2, 1, 0).reshape(P, 96) for l in range(DEPTH)], axis=1),
        b_gate=per_layer(i["b_gate"]), a_log=rows(i["a_log"]), dt_bias=rows(i["dt_bias"]))
    out["vecs"] = np.ascontiguousarray(np.concatenate([vec[n] for n in VEC_WIDTHS], axis=1))
    out["consts"] = CONSTS
    return out


def ffn_slabs(gate, up, down):
    return np.stack([slabs(gate), slabs(up), down.reshape(FT, P, D)], axis=1).reshape(3 * FT, P, SLAB)


def declare(nc, shapes, y_shape=(P, KT, T)):
    dram = {n: nc.dram_tensor(f"in_{n}", s, mybir.dt.from_np(t), kind="ExternalInput").ap()
            for n, (s, t) in shapes.items()}
    dram["y"] = nc.dram_tensor("y", y_shape, F32, kind="ExternalOutput").ap()
    return dram


def kernel(**inputs):
    import concourse.bacc as _bacc
    from concourse.bass_utils import run_bass_kernel_spmd as _run

    arrays = lay_out(inputs)
    shapes = {n: (a.shape, a.dtype) for n, a in arrays.items()}
    known = {}
    for _ in range(2):
        nc = _bacc.Bacc("TRN2", target_bir_lowering=False, num_devices=1)
        known = program(nc, declare(nc, shapes), known)
    r = _run(nc, [{f"in_{n}": a for n, a in arrays.items()}], core_ids=[0])
    y = r.results[0]["y"]
    return y.transpose(1, 0, 2).reshape(D, T).T.reshape(1, T, D)
```

```python
import math
from contextlib import ExitStack

import numpy as np
import concourse.bass as bass
from concourse import mybir

F32 = mybir.dt.float32
I32 = mybir.dt.int32
F32R = mybir.dt.float32r
ACT = mybir.ActivationFunctionType
ALU = mybir.AluOpType
AXX = mybir.AxisListType.X

P = 128
D = 1024
KT = D // P
T = 256
NP2 = T // P
DEPTH = 2
CHUNK = 64
NCH = T // CHUNK
DNH = 8
SAH = 8
XAH = 4
TOPK = T // 4
F_HID = 2816
FT = F_HID // P
NE = 8
DH = 6
MH = 8
EPS = 1e-6
NEG = -1e30
TAKEN = -3e38
RING = 6
BANKS = 8
MODS = 6 * KT
SA_PARTS = (13, 16, 23)
MODS_AT = (1, 0, 2, 1, 1, 1, 0)
ROPE_AT = ((0, 1, 2), (3, 4, 5), (6, 7, 8), (9, 10))
SLAB = KT * P
TWO_PI_PARTS = (6.28125, 0.0019350051879882812, 3.019916e-07)
ROUND = 12582912.0
LAM_INIT = 0.8 - 0.6 * math.exp(0.0)


def rotation(pairs):
    r = np.zeros((P, P), np.float32)
    for out_row, in_row, sign in pairs:
        r[in_row, out_row] = sign
    return r


def make_consts():
    i = np.arange(P)
    same = (i[:, None] // CHUNK) == (i[None, :] // CHUNK)
    c = {}
    c["ident"] = np.eye(P, dtype=np.float32)
    c["ones"] = np.ones((P, P), np.float32)
    c["upto"] = ((i[:, None] <= i[None, :]) & same).astype(np.float32)
    c["after"] = ((i[:, None] > i[None, :]) & same).astype(np.float32)
    for n in range(2):
        c[f"chunk{n}"] = np.repeat((i // CHUNK == n).astype(np.float32)[:, None], P, 1)
    c["strict"] = ((i[:, None] > i[None, :]) & same).astype(np.float32)
    c["incl"] = ((i[:, None] <= i[None, :]) & same).astype(np.float32)
    for k in range(6):
        b = 1 << k
        c[f"merge{k}"] = ((i[:, None] // (2 * b) == i[None, :] // (2 * b))
                          & (i[:, None] % (2 * b) >= b) & (i[None, :] % (2 * b) < b)).astype(np.float32)
    c["rot_sa"] = rotation([(r, r + 16, -1.0) for r in range(16)] + [(r + 16, r, 1.0) for r in range(16)])
    ri = rotation([(b + r, b + r + 8, -1.0) for b in (0, 64) for r in range(8)]
                  + [(b + r + 8, b + r, 1.0) for b in (0, 64) for r in range(8)])
    c["rot_ix"] = ri
    dup = np.zeros((P, P), np.float32)
    for m in range(P):
        dup[m % 64, m] = 1.0
    c["dup"] = dup
    duprot = np.zeros((P, P), np.float32)
    for m in range(P):
        duprot[:64, m] = ri[:64, m % 64]
    c["dup_rot"] = duprot
    invf = np.zeros((P, 2), np.float32)
    for r in range(32):
        invf[r, 0] = 500000.0 ** (-((r % 16) * 2.0 / 32))
    for r in range(P):
        if r % 64 < 16:
            invf[r, 1] = 500000.0 ** (-(((r % 64) % 8) * 2.0 / 16))
    c["invf"] = invf
    adm = np.zeros((P, P + 2 * P), np.float32)
    for p in range(2):
        key = np.arange(P * (p + 1)) // CHUNK
        query = (P * p + i) // CHUNK
        adm[:, P * p:P * p + P * (p + 1)] = np.where(key[None, :] <= query[:, None], 0.0, NEG)
    c["admit"] = adm
    return c


def pack(parts):
    at, off = {}, 0
    for name, a in parts.items():
        at[name] = (off, a.shape[1])
        off += a.shape[1]
    return np.ascontiguousarray(np.concatenate(list(parts.values()), axis=1)), at


def make_consts_2():
    i, t = np.arange(P), np.arange(T)
    rot = rotation([(b + h + r, b + h + r + 16, -1.0) for b in (0, 64) for h in (0, 32) for r in range(16)]
                   + [(b + h + r + 16, b + h + r, 1.0) for b in (0, 64) for h in (0, 32) for r in range(16)])
    row, col = (t // 64).astype(np.float32), (t % 64).astype(np.float32)
    inv = (np.float32(10000.0) ** (-np.arange(16, dtype=np.float32) / 16)).astype(np.float32)
    ang = np.zeros((P, T), np.float32)
    for r in range(P):
        ang[r] = (row if r % 64 < 32 else col) * inv[r % 16]
    count = np.zeros((P, 2, T), np.float32)
    for r in range(P):
        for s in range(2):
            w = (2, 4, 8, 16)[2 * s + r // 64]
            count[r, s] = 1.0 / (np.clip(t + w // 2, 0, T) - np.clip(t - w // 2, 0, T))
    return rot, np.concatenate([np.cos(ang), np.sin(ang), count.reshape(P, 2 * T)], axis=1).astype(np.float32)


CONSTS, CAT = pack(make_consts())
ROT_AX, TABLES_2 = make_consts_2()
VEC_WIDTHS = dict(norm_mix=16, norm_mem=16, norm_ffn=16, norm_final=8, dn_norm=2, conv=192, b_gate=48,
                  a_log=16, dt_bias=16, cond=16, norm1=16, norm2=16, mod_b=96, pool_scale=2, lam=4,
                  q_norm=4, kv_norm=2, final_2=8, router=64)
VAT, _o = {}, 0
for _n, _w in VEC_WIDTHS.items():
    VAT[_n] = (_o, _w)
    _o += _w
VEC_W = _o


class Counts:

    def __init__(self, nc, ctx, known):
        self.nc, self.ctx, self.known, self.found = nc, ctx, known, {}
        self.sems, self.counted = {}, {}
        self.banks = [ctx.enter_context(nc.psum_tensor(f"bank{b}", [P, 512], F32)) for b in range(BANKS)]

    def sem(self, stage):
        if stage not in self.sems:
            self.sems[stage] = self.ctx.enter_context(self.nc.semaphore(stage))
            self.counted[stage] = 0
        return self.sems[stage]

    def advance(self, stage, n):
        self.sem(stage)
        self.counted[stage] += n
        return self.counted[stage]

    def value(self, stage, tag):
        return self.known.get((stage, tag), 1)

    def at(self, stage, tag):
        return self.sem(stage), self.value(stage, tag)

    def place(self, tag):
        return self.known.get(("bank", tag), (0, 1))

    def bank(self, tag):
        return self.banks[self.place(tag)[0]]

    def full(self, tag):
        return self.at(f"bank_full{self.place(tag)[0]}", tag)

    def empty(self, tag):
        b, n = self.place(tag)
        return self.sem(f"bank_read{b}"), n


class Engine:

    def __init__(self, counts, eng, name):
        self.c, self.eng, self.name = counts, eng, name
        self.latest = None

    def count(self, stage=None, tag=None, by=1):
        stage = stage or f"{self.name}_step"
        n = self.c.advance(stage, by)
        if tag is not None:
            self.c.found[(stage, tag)] = n
        self.latest = (stage, n)
        return self.c.sem(stage), by

    def emptied(self, tag):
        b, n = self.c.place(tag)
        self.latest = (f"bank_read{b}", n)
        return self.c.sem(f"bank_read{b}"), 1

    def last(self):
        stage, n = self.latest
        return self.c.sem(stage), n


class Tensor(Engine):

    def __init__(self, counts, eng):
        super().__init__(counts, eng, "tensor")
        self.fills, self.turn, self.bank = [1] * BANKS, 0, None
        self.in_turn = BANKS

    def take(self, tag, bank=None):
        if bank is None:
            bank, self.turn = self.turn, (self.turn + 1) % self.in_turn
        held = self.fills[bank]
        self.fills[bank] += 1
        self.c.found[("bank", tag)] = (bank, self.fills[bank])
        self.bank = self.c.banks[bank]
        return self.c.sem(f"bank_read{bank}"), held

    def filled(self, tag):
        return self.count(f"bank_full{self.c.found[('bank', tag)][0]}", tag)

class Stream:

    def __init__(self):
        self.phases, self.total = {}, 0
        self.split, self.split_total = {}, 0

    def add(self, name, source, n, width=SLAB, first=0, split=False):
        self.phases[name] = (source, self.total, n, width, first)
        self.total += n
        if split:
            self.split[name] = self.split_total
            self.split_total += n


def loops(n):
    turns = n // RING
    return (turns if turns >= 3 else 0)


def load_stream(sync, stream, ring, c):
    for source, g0, n, width, first in stream.phases.values():
        def load(i, slot, before):
            if before is not None:
                sync.wait_ge(c.sem(f"slab_done{slot}"), before)
            index = bass.ds(i, 1)
            sync.dma_start(ring[:, slot, 0:width], source[index].rearrange("a p n -> p (a n)"))\
                .then_inc(c.sem(f"slab_loaded{slot}"), 16)
        turns = loops(n)
        peeled = 1 if turns and g0 < RING else 0
        for i in range(peeled * RING):
            g = g0 + i
            load(first + i, g % RING, g // RING if g >= RING else None)
        if turns:
            with sync.Fori(peeled, turns) as turn:
                for u in range(RING):
                    g = g0 + u
                    load(turn * RING + (first + u), g % RING, turn + g // RING)
        for i in range(turns * RING, n):
            g = g0 + i
            load(first + i, g % RING, g // RING if g >= RING else None)


def gemm_tensor(te, stream, name, ring, tag, rhs, cols, tiles=KT):
    _, g0, n, _, _ = stream.phases[name]
    nc, c = te.c.nc, te.c

    def slab(slot, ps):
        for k in range(tiles):
            last = nc.tensor.matmul(ps[:, 0:cols], ring[:, slot, k * P:(k + 1) * P], rhs(k),
                                    start=k == 0, stop=k == tiles - 1)
        last.then_inc(c.sem(f"slab_done{slot}"), 1)

    turns = loops(n)
    if turns:
        base = list(te.fills)
        with te.eng.Fori(0, turns) as turn:
            for u in range(RING):
                slot = (g0 + u) % RING
                te.eng.wait_ge(c.sem(f"slab_loaded{slot}"), (turn + ((g0 + u) // RING + 1)) * 16)
                te.eng.wait_ge(c.sem(f"bank_read{slot}"), turn + base[slot])
                slab(slot, c.banks[slot])
        for u in range(RING):
            slot = (g0 + u) % RING
            for t in range(turns):
                c.found[("bank", (name, tag, t * RING + u))] = (slot, base[slot] + t + 1)
            te.fills[slot] += turns
    for i in range(turns * RING, n):
        g = g0 + i
        te.eng.wait_ge(c.sem(f"slab_loaded{g % RING}"), 16 * (g // RING + 1))
        te.eng.wait_ge(*te.take((name, tag, i), bank=g % RING))
        slab(g % RING, te.bank)


def gemm_read(rd, stream, name, tag, read):
    _, g0, n, _, _ = stream.phases[name]
    c = rd.c
    turns = loops(n)
    if turns:
        with rd.eng.Fori(0, turns) as turn:
            for u in range(RING):
                slot = (g0 + u) % RING
                rd.eng.wait_ge(c.sem(f"slab_done{slot}"), turn + ((g0 + u) // RING + 1))
                read(turn * RING + u, c.banks[slot]).then_inc(c.sem(f"bank_read{slot}"), 1)
        rd.emptied((name, tag, turns * RING - 1))
    for i in range(turns * RING, n):
        g = g0 + i
        rd.eng.wait_ge(c.sem(f"slab_done{g % RING}"), g // RING + 1)
        read(i, c.banks[g % RING]).then_inc(*rd.emptied((name, tag, i)))


def norm_tensor(te, k, tag, squares, tiles, cols):
    te.eng.wait_ge(*te.c.at("squared", tag))
    te.eng.wait_ge(*te.take(tag))
    ps = te.bank
    for i in range(tiles):
        last = te.c.nc.tensor.matmul(ps[:, 0:cols], k["ones"], squares[:, i, 0:cols],
                                     start=i == 0, stop=i == tiles - 1)
    last.then_inc(*te.filled(tag))


def norm_scalar(sc, tag, src, squares, root, tiles, cols):
    nc = sc.c.nc
    if sc.last_norm is not None:
        sc.eng.wait_ge(*sc.c.full(sc.last_norm))
        sc.eng.wait_ge(*sc.c.at("normed", sc.last_norm))
    nc.scalar.activation(squares[:, 0:tiles, 0:cols], src, ACT.Square).then_inc(*sc.count("squared", tag))
    sc.eng.wait_ge(*sc.c.full(tag))
    ps = sc.c.bank(tag)
    nc.scalar.activation(root[:, 0:cols], ps[:, 0:cols], ACT.Sqrt, bias=sc.eps[:, 0:1], scale=1.0 / (tiles * P)).then_inc(*sc.emptied(tag))
    sc.last_norm = tag


def norm_vector(ve, tag, src, gain, root, out, tiles, cols, streams=None):
    nc = ve.c.nc
    ve.eng.wait_ge(*ve.c.empty(tag))
    nc.vector.reciprocal(root[:, 0:cols], root[:, 0:cols]).then_inc(*ve.count())
    ve.eng.wait_ge(*ve.last())
    parts = [(slice(0, cols), gain, None)] if streams is None else streams
    for at, g, _ in parts:
        for i in range(tiles):
            ins = nc.vector.scalar_tensor_tensor(out=out[:, i, at], in0=src[:, i, at], scalar=g[:, i:i + 1],
                                                 in1=root[:, at], op0=ALU.mult, op1=ALU.mult)
    if streams is not None:
        ins.then_inc(*ve.count())
        ve.eng.wait_ge(*ve.last())
        for at, _, shift in parts:
            for i in range(tiles):
                ins = nc.vector.tensor_scalar(out[:, i, at], out[:, i, at], shift[:, i:i + 1], None, ALU.add)
    ins.then_inc(*ve.count("normed", tag))


def att_tensor(te, k, tag, units, P_of, PT_of, ident, beside=None):
    nc = te.c.nc
    n = len(units)

    def logits(u):
        x = units[u]
        for b, bank in enumerate(x["logits"]):
            te.eng.wait_ge(*te.take((tag, "logits", u, b)))
            ps = te.bank
            for col, width, pairs in bank:
                for j, (lhsT, rhs) in enumerate(pairs):
                    last = nc.tensor.matmul(ps[:, col:col + width], lhsT, rhs, start=j == 0,
                                            stop=j == len(pairs) - 1)
            last.then_inc(*te.filled((tag, "logits", u, b)))

    def turned(u):
        x = units[u]
        te.eng.wait_ge(*te.c.at("probs", (tag, u)))
        tiles = x["turn"]
        te.eng.wait_ge(*te.take((tag, "turned", u)))
        ps = te.bank
        for j, (sub, kt) in enumerate(tiles):
            last = nc.tensor.transpose(ps[:, j * P:(j + 1) * P], P_of(u)[:, sub, kt * P:(kt + 1) * P], ident)
        last.then_inc(*te.filled((tag, "turned", u)))

    def out(u):
        x = units[u]
        te.eng.wait_ge(*te.c.empty((tag, "turned", u)))
        te.eng.wait_ge(*te.take((tag, "mixed", u)))
        ps = te.bank
        for col, pairs in x["out"](PT_of(u)):
            for j, (lhsT, rhs) in enumerate(pairs):
                last = nc.tensor.matmul(ps[:, col:col + P], lhsT, rhs, start=j == 0, stop=j == len(pairs) - 1)
        last.then_inc(*te.filled((tag, "mixed", u)))

    for u in range(n + 3):
        if u < n:
            logits(u)
        if beside:
            beside()
        if 0 <= u - 2 < n:
            turned(u - 2)
        if 0 <= u - 3 < n:
            out(u - 3)


ATT_BUF = 3


def att_vector(ve, tag, units, P_of, mx, sm, scale, combine=None):
    nc = ve.c.nc
    n = len(units)

    def front(u):
        x = units[u]
        if u >= ATT_BUF:
            ve.eng.wait_ge(*ve.c.full((tag, "turned", u - ATT_BUF)))
        s, nk, subs = P_of(u), x["nk"], x["subs"]
        at = 0
        for b, bank in enumerate(x["logits"]):
            ve.eng.wait_ge(*ve.c.full((tag, "logits", u, b)))
            ps = ve.c.bank((tag, "logits", u, b))
            m = len(bank)
            src = ps[:, 0:512].rearrange("p (s k) -> p s k", s=m)[:, :, 0:nk]
            if x["mask"] is None:
                ins = nc.vector.tensor_scalar(s[:, at:at + m, 0:nk], src, scale, None, ALU.mult)
            else:
                ins = nc.vector.scalar_tensor_tensor(out=s[:, at:at + m, 0:nk], in0=src, scalar=scale,
                                                     in1=x["mask"].unsqueeze(1).to_broadcast([P, m, nk]),
                                                     op0=ALU.mult, op1=ALU.add)
            ins.then_inc(*ve.emptied((tag, "logits", u, b)))
            at += m
        ve.eng.wait_ge(*ve.last())
        nc.vector.tensor_reduce(mx[:, u % ATT_BUF, 0:subs], s[:, 0:subs, 0:nk], AXX, ALU.max).then_inc(*ve.count())
        ve.eng.wait_ge(*ve.last())
        nc.vector.tensor_scalar(mx[:, u % ATT_BUF, 0:subs], mx[:, u % ATT_BUF, 0:subs], -1.0, None,
                                        ALU.mult).then_inc(*ve.count("maxed", (tag, u)))

    def back(u):
        x = units[u]
        s, nk, subs = P_of(u), x["nk"], x["subs"]
        ve.eng.wait_ge(*ve.c.at("exped", (tag, u)))
        r = sm[:, u % ATT_BUF, 0:subs]
        nc.vector.reciprocal(r, r).then_inc(*ve.count())
        ve.eng.wait_ge(*ve.last())
        if combine is None:
            for j in range(subs):
                ins = nc.vector.tensor_scalar(s[:, j, 0:nk], s[:, j, 0:nk], r[:, j:j + 1], None, ALU.mult)
        else:
            nc.vector.tensor_scalar(r[:, 1:2], r[:, 1:2], combine, None, ALU.mult).then_inc(*ve.count())
            ve.eng.wait_ge(*ve.last())
            nc.vector.tensor_scalar(s[:, 1, 0:nk], s[:, 1, 0:nk], r[:, 1:2], None, ALU.mult).then_inc(*ve.count())
            ve.eng.wait_ge(*ve.last())
            ins = nc.vector.scalar_tensor_tensor(out=s[:, 0, 0:nk], in0=s[:, 0, 0:nk], scalar=r[:, 0:1],
                                                 in1=s[:, 1, 0:nk], op0=ALU.mult, op1=ALU.subtract)
        ins.then_inc(*ve.count("probs", (tag, u)))

    for u in range(n + 1):
        if u < n:
            front(u)
        if u >= 1:
            back(u - 1)


def att_scalar(sc, tag, units, P_of, PT_of, mx, sm):
    nc = sc.c.nc
    n = len(units)

    def exps(u):
        x = units[u]
        sc.eng.wait_ge(*sc.c.at("maxed", (tag, u)))
        for j in range(x["subs"]):
            ins = nc.scalar.activation(P_of(u)[:, j, 0:x["nk"]], P_of(u)[:, j, 0:x["nk"]], ACT.Exp,
                                       bias=mx[:, u % ATT_BUF, j:j + 1], accum_out=sm[:, u % ATT_BUF, j:j + 1])
        ins.then_inc(*sc.count("exped", (tag, u)))

    def turned(u):
        x = units[u]
        sc.eng.wait_ge(*sc.c.full((tag, "turned", u)))
        ps = sc.c.bank((tag, "turned", u))
        if u >= ATT_BUF:
            sc.eng.wait_ge(*sc.c.full((tag, "mixed", u - ATT_BUF)))
        w = len(x["turn"]) * P
        nc.scalar.activation(PT_of(u)[:, 0:w], ps[:, 0:w], ACT.Copy).then_inc(*sc.emptied((tag, "turned", u)))

    def out(u):
        sc.eng.wait_ge(*sc.c.full((tag, "mixed", u)))
        ps = sc.c.bank((tag, "mixed", u))
        dst, cols = units[u]["dst"]
        src = ps[:, 0:cols] if dst.ndim == 2 else ps[:, 0:cols].rearrange("p (a b) -> p a b", b=P)
        nc.scalar.activation(dst, src, ACT.Copy).then_inc(*sc.emptied((tag, "mixed", u)))

    for u in range(n + 3):
        if u < n:
            exps(u)
        if 0 <= u - 2 < n:
            turned(u - 2)
        if 0 <= u - 3 < n:
            out(u - 3)

def rounded_tensor(te, stream, name, rounded):
    _, g0, _, _, _ = stream.phases[name]
    s0 = stream.split[name]
    nc, c = te.c.nc, te.c
    high, low = rounded

    def products(q, turn, pairs):
        slot, g = (s0 + q) % 3, g0 + q
        te.eng.wait_ge(c.sem(f"slab_done{g % RING}"), turn + (g // RING + 1))
        for out, kk, xh, xl, start, stop in pairs:
            wh, wl = high[:, slot, kk * P:(kk + 1) * P], low[:, slot, kk * P:(kk + 1) * P]
            nc.tensor.matmul(out, wh, xh, start=start, stop=False, skip_group_check=True)
            nc.tensor.matmul(out, wl, xh, start=False, stop=False, skip_group_check=True)
            last = nc.tensor.matmul(out, wh, xl, start=False, stop=stop, skip_group_check=True)
        last.then_inc(c.sem("split_used"), 1)

    return products


def round_high(sc, stream, name, ring, high):
    _, g0, _, _, _ = stream.phases[name]
    s0 = stream.split[name]
    nc, c = sc.c.nc, sc.c

    def step(q, turn):
        g, s = g0 + q, s0 + q
        sc.eng.wait_ge(c.sem(f"slab_loaded{g % RING}"), (turn + (g // RING + 1)) * 16)
        if s >= 3:
            sc.eng.wait_ge(c.sem("split_used"), turn * RING + (s - 2))
        nc.scalar.activation(high[:, s % 3, :], ring[:, g % RING, :], ACT.Copy).then_inc(c.sem("high_ready"), 1)

    return step


def round_low(eng, stream, name, ring, rounded, subtract):
    _, g0, _, _, _ = stream.phases[name]
    s0 = stream.split[name]
    c = eng.c
    high, low = rounded

    def step(q, turn):
        g, s = g0 + q, s0 + q
        eng.eng.wait_ge(c.sem("high_ready"), turn * RING + (s + 1))
        subtract(low[:, s % 3, :], ring[:, g % RING, :], high[:, s % 3, :], ALU.subtract)\
            .then_inc(c.sem(f"slab_done{g % RING}"), 1)

    return step


def split_vector(ve, tag, src, high, low):
    nc = ve.c.nc
    ve.eng.wait_ge(*ve.last())
    nc.vector.tensor_copy(high, src).then_inc(*ve.count())
    ve.eng.wait_ge(*ve.last())
    nc.vector.tensor_tensor(low, src, high, ALU.subtract).then_inc(*ve.count("split", tag))


def split_gemm_tensor(te, stream, name, tag, rounded, x, cols=T, part=None):
    _, g0, n, _, _ = stream.phases[name]
    first, end = part or (0, n)
    c = te.c
    products = rounded_tensor(te, stream, name, rounded)

    def slab(q, turn, ps):
        products(q, turn, [(ps[:, 0:cols], kk, x[0][:, kk, 0:cols], x[1][:, kk, 0:cols], kk == 0, kk == KT - 1)
                           for kk in range(KT)])

    turns = loops(end) if first == 0 else 0
    if turns:
        base = list(te.fills)
        with te.eng.Fori(0, turns) as turn:
            for u in range(RING):
                slot = (g0 + u) % RING
                te.eng.wait_ge(c.sem(f"bank_read{slot}"), turn + base[slot])
                slab(u, turn, c.banks[slot])
        for u in range(RING):
            slot = (g0 + u) % RING
            for t in range(turns):
                c.found[("bank", (name, tag, t * RING + u))] = (slot, base[slot] + t + 1)
            te.fills[slot] += turns
    for i in range(max(first, turns * RING), end):
        te.eng.wait_ge(*te.take((name, tag, i), bank=(g0 + i) % RING))
        slab(i, 0, te.bank)


def split_gemm_read(rd, stream, name, tag, read, copy_slab=None, part=None):
    _, g0, n, _, _ = stream.phases[name]
    first, end = part or (0, n)
    s0 = stream.split[name]
    c = rd.c
    if copy_slab and first == 0:
        for q in range(3):
            copy_slab(q, 0)
    turns = loops(end) if first == 0 else 0
    turns -= 1 if turns and turns * RING > n - 3 and copy_slab else 0
    if turns:
        with rd.eng.Fori(0, turns) as turn:
            for u in range(RING):
                rd.eng.wait_ge(c.sem("split_used"), turn * RING + (s0 + u + 1))
                read(turn * RING + u, c.banks[(g0 + u) % RING]).then_inc(c.sem(f"bank_read{(g0 + u) % RING}"), 1)
                if copy_slab:
                    copy_slab(u + 3, turn)
        rd.emptied((name, tag, turns * RING - 1))
    for i in range(max(first, turns * RING), end):
        rd.eng.wait_ge(c.sem("split_used"), s0 + i + 1)
        read(i, c.banks[(g0 + i) % RING]).then_inc(*rd.emptied((name, tag, i)))
        if copy_slab and i + 3 < n:
            copy_slab(i + 3, 0)


def split_gemm_rest(eng, stream, name, ring, rounded, subtract):
    _, _, n, _, _ = stream.phases[name]
    rest_of_slab = round_low(eng, stream, name, ring, rounded, subtract)
    turns = loops(n)
    if turns:
        with eng.eng.Fori(0, turns) as turn:
            for u in range(RING):
                rest_of_slab(u, turn)
    for q in range(turns * RING, n):
        rest_of_slab(q, 0)


def ffn_tensor(te, stream, name, tag, rounded, x, hidden, steps):
    c = te.c
    products = rounded_tensor(te, stream, name, rounded)
    for b in range(6):
        te.eng.wait_ge(*te.take((tag, "ffn", b), bank=b))
    te.eng.wait_ge(*c.at("hidden_ready", ("cleared", tag)))
    h0 = c.value("hidden0", tag)

    def gate_up(q, turn, bank):
        for part in range(2):
            out = c.banks[bank][:, part * T:(part + 1) * T]
            products(q + part, turn, [(out, kk, x[0][:, kk, 0:T], x[1][:, kk, 0:T], kk == 0, kk == KT - 1)
                                      for kk in range(KT)])

    def down(q, turn, parity):
        products(q, turn, [(c.banks[m // 2][:, (m % 2) * T:(m % 2 + 1) * T], m, hidden[0][:, parity, :],
                            hidden[1][:, parity, :], False, True) for m in range(KT)])

    def period(f, turn):
        te.eng.wait_ge(c.sem("hidden_ready"), turn * 2 + (h0 + f))
        gate_up(2 + 3 * f, turn, 4 + (f + 1) % 2)
        te.eng.wait_ge(c.sem("hidden_ready"), turn * 2 + (h0 + f + 1))
        down(4 + 3 * f, turn, f % 2)

    gate_up(0, 0, 4)
    with te.eng.Fori(0, (steps - 2) // 2) as turn:
        period(0, turn)
        period(1, turn)
    period(steps - 2, 0)
    te.eng.wait_ge(c.sem("hidden_ready"), h0 + steps)
    down(3 * steps - 1, 0, (steps - 1) % 2)


def ffn_scalar(sc, stream, name, tag, ring, high, silu, steps):
    nc, c = sc.c.nc, sc.c
    u0 = stream.split[name]
    s0 = c.advance("silu_ready", 0)
    h0 = c.value("hidden0", tag)
    c.found[("silu0", tag)] = s0
    copy_slab = round_high(sc, stream, name, ring, high)

    def silu_of(f, turn):
        sc.eng.wait_ge(c.sem("split_used"), turn * RING + (u0 + max(3 * f + 1, 2)))
        if f >= 2:
            sc.eng.wait_ge(c.sem("hidden_ready"), turn * 2 + (h0 + f - 1))
        nc.scalar.activation(silu[:, f % 2, :], c.banks[4 + f % 2][:, 0:T], ACT.Silu)\
            .then_inc(c.sem("silu_ready"), 1)

    def period(f, turn):
        silu_of(f, turn)
        for q in range(3 * f + 3, 3 * f + 6):
            copy_slab(q, turn)

    for q in range(3):
        copy_slab(q, 0)
    period(0, 0)
    period(1, 0)
    with sc.eng.Fori(0, (steps - 4) // 2) as turn:
        period(2, turn)
        period(3, turn)
    period(steps - 2, 0)
    silu_of(steps - 1, 0)
    c.advance("silu_ready", steps)
    sc.latest = ("silu_ready", s0 + steps)


def ffn_vector(ve, stream, name, tag, ring, rounded, silu, exact, hidden, tick, steps, weight=None):
    nc, c = ve.c.nc, ve.c
    s0 = c.value("silu0", tag)
    for b in range(4):
        n_before = c.place((tag, "ffn", b))[1]
        ve.eng.wait_ge(c.sem(f"bank_read{b}"), n_before - 1)
        ins = nc.vector.memset(c.banks[b][:, :], 0.0)
    ins.then_inc(*ve.count("hidden_ready", ("cleared", tag)))
    h0 = c.advance("hidden_ready", 0)
    c.found[("hidden0", tag)] = h0
    w0 = c.advance("weighed", 0)
    rest_of_slab = round_low(ve, stream, name, ring, rounded, nc.vector.tensor_tensor)

    def hidden_of(f, turn, expert):
        ve.eng.wait_ge(c.sem("silu_ready"), turn * 2 + (s0 + f + 1))
        s, h = silu[:, f % 2, :], exact[:, f % 2, :]
        up = c.banks[4 + f % 2][:, T:2 * T]
        hh, hl = hidden[0][:, f % 2, :], hidden[1][:, f % 2, :]
        if weight is None:
            nc.vector.memset(tick[:, 1:2], 0.0).then_inc(c.sem("weighed"), 1)
        else:
            nc.vector.tensor_tensor(s, s, weight(expert), ALU.mult).then_inc(c.sem("weighed"), 1)
        ve.eng.wait_ge(c.sem("weighed"), turn * 6 + (w0 + 3 * f + 1))
        nc.vector.tensor_tensor(h, s, up, ALU.mult).then_inc(c.sem("weighed"), 1)
        ve.eng.wait_ge(c.sem("weighed"), turn * 6 + (w0 + 3 * f + 2))
        nc.vector.tensor_copy(hh, h).then_inc(c.sem("weighed"), 1)
        ve.eng.wait_ge(c.sem("weighed"), turn * 6 + (w0 + 3 * f + 3))
        nc.vector.tensor_tensor(hl, h, hh, ALU.subtract).then_inc(c.sem("hidden_ready"), 1)

    def period(f, turn, expert=0):
        hidden_of(f, turn, expert)
        for q in range(3 * f + 3, 3 * f + 6):
            rest_of_slab(q, turn)

    for q in range(3):
        rest_of_slab(q, 0)
    period(0, 0)
    period(1, 0)
    experts = steps // FT
    with ve.eng.Fori(0, FT // 2 - (1 if experts > 1 else 2)) as turn:
        period(2, turn)
        period(3, turn)
    if experts > 1:
        with ve.eng.Fori(0, experts - 2) as e:
            with ve.eng.Fori(0, FT // 2) as turn:
                for u in range(2):
                    period(FT + u, turn + e * (FT // 2), e + 1)
        with ve.eng.Fori(0, FT // 2 - 1) as turn:
            for u in range(2):
                period(steps - FT + u, turn, experts - 1)
    period(steps - 2, 0, experts - 1)
    hidden_of(steps - 1, 0, experts - 1)
    c.advance("weighed", 3 * steps)
    c.advance("hidden_ready", steps)
    ve.latest = ("hidden_ready", h0 + steps)
    ve.eng.wait_ge(*ve.last())
    for b in (4, 5):
        nc.vector.memset(tick[:, b:b + 1], 0.0).then_inc(*ve.emptied((tag, "ffn", b)))

def tile_of(a, i):
    return a[:, bass.ds(i, 1), :].rearrange("p a t -> p (a t)")


def program(nc, dram, known):
    ctx = ExitStack()
    c = Counts(nc, ctx, known)

    with ctx:

        def sb(name, shape, dt=F32):
            return ctx.enter_context(nc.sbuf_tensor(name, shape, dt))

        ring = sb("ring", [P, RING, SLAB])
        consts = sb("consts", [P, CONSTS.shape[1]])
        vecs = sb("vecs", [P, VEC_W])
        x = sb("x", [P, KT, T])
        hn = sb("hn", [P, KT, T])
        squares = sb("squares", [P, KT * T])
        root = sb("root", [P, 512])
        rope = sb("rope", [P, 4, T])
        small = sb("small", [P, 640])
        tick = sb("tick", [P, 8])
        eps = sb("eps", [P, 4])
        mods = sb("mods", [P, DEPTH, 48, 2])
        cond = sb("cond", [P, KT, 2])
        arena_at = nc.sbuf_base
        arena = sb("arena", [P, 33 * T + 28 * T + 8 * 2048 + 1536])
        A = arena[:, 0:33 * T].rearrange("p (k t) -> p k t", t=T)
        Bq = arena[:, 33 * T:61 * T].rearrange("p (k t) -> p k t", t=T)
        W = arena[:, 61 * T:]

        k = {n: consts[:, o:o + w] for n, (o, w) in CAT.items()}
        v = {n: vecs[:, o:o + w] for n, (o, w) in VAT.items()}

        def area(i, n=2048, off=0):
            return W[:, i * 2048 + off:i * 2048 + off + n]

        sq8 = squares[:, :].rearrange("p (k t) -> p k t", t=T)
        KB, KD, VB, M, X, Pl, Y, AT = [area(i).rearrange("p (a b) -> p a b", b=P) for i in range(8)]
        MK = squares[:, :].rearrange("p (a b) -> p a b", b=P)
        DEC, DECT, EGB = [area(8, 512, 512 * i) for i in range(3)]
        WT, UU = M, Pl
        S = area(6, 1024).rearrange("p (h v) -> p h v", v=P)
        VN = area(6, 1024, 1024).rearrange("p (h v) -> p h v", v=P)
        conv = [area(6).rearrange("p (k t) -> p k t", t=T), area(4).rearrange("p (k t) -> p k t", t=T), sq8]
        sroot = area(5).rearrange("p (k t) -> p k t", t=T)
        gated = area(3).rearrange("p (k t) -> p k t", t=T)
        stok = small[:, 0:256].rearrange("p (a f) -> p a f", f=P)
        sm = lambda o, n: small[:, 256 + o:256 + o + n]
        beta, gneg, y0, y1, y2, gate = sm(0, 16), sm(16, 8), sm(24, 16), sm(40, 16), sm(56, 16), sm(72, 16)
        graw, gexp, bexp, iw = sm(88, 64), sm(152, 64), sm(216, 16), sm(232, 16)
        mx = sm(248, 6).rearrange("p (a b) -> p a b", b=2)
        smx = sm(254, 6).rearrange("p (a b) -> p a b", b=2)
        m8 = sm(264, 8)
        C = W[:, 0:24 * T].rearrange("p (k t) -> p k t", t=T)
        att_p = W[:, 6144:6144 + 3 * 1024].rearrange("p (r s k) -> p r s k", r=3, s=2)
        att_t = W[:, 9216:9216 + 3 * 512].rearrange("p (r k) -> p r k", r=3)
        vtok = W[:, 10752:12800].rearrange("p (a n) -> p a n", a=2)
        merged = W[:, 12800:14848].rearrange("p (k t) -> p k t", t=T)
        memn = merged
        ixk = W[:, 0:256]
        score = [A[:, 32, 0:P], W[:, 256:512]]
        relu = W[:, 512:1536].rearrange("p (r s k) -> p r s k", r=2, s=2)
        work = W[:, 1536:1792]
        negm = [A[:, 32, P:T], W[:, 1792:2048]]
        ropet = W[:, 16896:17920].rearrange("p (r s k) -> p r s k", r=2, s=2)
        def rounded(name, at, *shape):
            return nc.alloc_sbuf_tensor_at(name, [P, *shape], F32R, offset=arena_at + 4 * at)
        ffn_w = (rounded("ffn_w_high", 12288, 3, SLAB), rounded("ffn_w_low", 15360, 3, SLAB))
        w_at = 61 * T
        first_w = (rounded("first_w_high", w_at + 4096, 3, SLAB), rounded("first_w_low", w_at + 14336, 3, SLAB))
        first_x = (rounded("first_x_high", w_at, KT, T), rounded("first_x_low", w_at + 2048, KT, T))
        mem_w = (rounded("mem_w_high", 0, 3, SLAB), rounded("mem_w_low", 3072, 3, SLAB))
        mem_x = (rounded("mem_x_high", w_at + 14848, KT, T), rounded("mem_x_low", w_at + 12800, KT, T))
        late_x = (rounded("late_x_high", w_at + 14848, KT, T), rounded("late_x_low", 8448, KT, T))
        branch_x = [(rounded("delta_high", 12544 - 2048, KT, T), rounded("delta_low", 24 * T, KT, T)),
                    (rounded("sparse_high", w_at + 8192, KT, T), rounded("sparse_low", 49 * T, KT, T)),
                    (rounded("memory_high", w_at + 10240, KT, T), rounded("memory_low", w_at, KT, T))]
        even_w = (rounded("even_w_high", 22528, 3, SLAB), rounded("even_w_low", 25600, 3, SLAB))
        even_x = (rounded("even_x_high", 8192, KT, 2 * T), rounded("even_x_low", 4096, KT, 2 * T))
        merged_x = (rounded("merged_high", w_at + 14848, KT, T), rounded("merged_low", w_at + 12800, KT, T))
        branch_tmp = W[:, 12288:12800].rearrange("p (a t) -> p a t", a=2)
        gates_w = (rounded("gates_w_high", w_at + 2048, 3, SLAB), rounded("gates_w_low", w_at + 5120, 3, SLAB))
        hidden = (rounded("hidden_high", 18432, 2, T), rounded("hidden_low", 18944, 2, T))
        ffn_x = [(rounded(f"ffn_x_high{s}", at, KT, T), rounded(f"ffn_x_low{s}", at + 2048, KT, T))
                 for s, at in enumerate((19456, 24576))]
        silu = arena[:, 23552:24064].rearrange("p (a t) -> p a t", a=2)
        exact = arena[:, 24064:24576].rearrange("p (a t) -> p a t", a=2)
        mtmp = W[:, 0:512].rearrange("p (a t) -> p a t", a=2)
        P_of = lambda u: att_p[:, u % 3]
        PT_of = lambda u: att_t[:, u % 3]

        T2 = 2 * T
        def room(at, tiles, cols):
            return arena[:, at:at + tiles * cols].rearrange("p (k t) -> p k t", t=cols)
        H, hn2, sq2 = room(0, KT, T2), room(4096, KT, T2), room(8192, KT, T2)
        Z = room(12288, 20, T2)
        att_p2 = arena[:, 22528:25600].rearrange("p (r s k) -> p r s k", r=3, s=2)
        att_t2 = arena[:, 25600:27136].rearrange("p (r k) -> p r k", r=3)
        vtok2 = arena[:, 27136:30208].rearrange("p (a n) -> p a n", a=4)
        pools = [arena[:, 30208 + 1088 * i:30208 + 1088 * (i + 1)].rearrange("p (s e t) -> p s e t", s=2, e=2) for i in range(3)]
        Zo, cqn, ckvn = room(12288, 7, T2), room(15872, 4, T), room(16896, 2, T2)
        QN, KV = room(17920, 12, T), room(20992, 16, T2)
        att_p3 = arena[:, 4096:7168].rearrange("p (r s k) -> p r s k", r=3, s=2)
        att_t3 = arena[:, 29184:30720].rearrange("p (r k) -> p r k", r=3)
        vtok3 = arena[:, 8192:12288].rearrange("p (a n) -> p a n", a=4)
        expert_w = squares[:, :].rearrange("p (e t) -> p e t", t=T)
        cos2, sin2 = rope[:, 0, :], rope[:, 1, :]
        o2 = CAT["strict"][0]
        rot_ax, pool_w = consts[:, o2:o2 + P], consts[:, o2 + P:o2 + 3 * P]
        gains = small[:, 0:64].rearrange("p (n k) -> p n k", k=KT)
        lamb = small[:, 64:72]
        rout = small[:, 80:240]
        mx2 = small[:, 504:510].rearrange("p (a b) -> p a b", b=2)
        smx2 = small[:, 510:516].rearrange("p (a b) -> p a b", b=2)
        mod = lambda l, n, s: mods[:, l, 8 * n:8 * n + 8, s]
        both = lambda a, s: slice(0, T) if s == 0 else slice(T, T2)

        def diff_units():
            units = []
            for s in range(2):
                k0, nk = (0, T2) if s == 0 else (T, T)
                for p in range(NP2):
                    for h in range(DH):
                        q = slice(s * T + p * P, s * T + (p + 1) * P)
                        units.append(dict(
                            logits=[[(0, nk, [(Z[64 * j:64 * j + 64, 2 + h, q], Z[64 * j:64 * j + 64, 8 + h, k0:k0 + nk])])]
                                    for j in range(2)],
                            nk=nk, subs=2, mask=None, turn=[(0, kt) for kt in range(nk // P)],
                            out=lambda pt, h=h, nk=nk, k0=k0: [
                                (0, [(vtok2[:, k0 // P + kt, h * P:(h + 1) * P], pt[:, kt * P:(kt + 1) * P])
                                     for kt in range(nk // P)])],
                            dst=(Z[:, 2 + h, q], P)))
            return units

        def latent_units():
            units = []
            for p in range(NP2):
                for h in range(MH):
                    q, r = slice(p * P, (p + 1) * P), slice(64 * (h % 2), 64 * (h % 2) + 64)
                    units.append(dict(
                        logits=[[(0, T2, [(QN[:, h, q], KV[:, h, :]), (QN[r, 8 + h // 2, q], Zo[r, 6, :])])]],
                        nk=T2, subs=1, mask=None, turn=[(0, kt) for kt in range(4)],
                        out=lambda pt, h=h: [(0, [(vtok3[:, kt, h * P:(h + 1) * P], pt[:, kt * P:(kt + 1) * P])
                                                  for kt in range(4)])],
                        dst=(QN[:, h, q], P)))
            return units

        stream = Stream()
        for l in range(DEPTH):
            stream.add(f"dn{l}", dram["w_in"][l], 33, split=True)
            stream.add(f"sa{l}", dram["w_in"][l], 28, first=33, split=True)
            stream.add(f"mod{l}0", dram["mod_w"][l], MODS - 18)
            stream.add(f"mem{l}", dram["w_mem"][l], 16, split=True)
            stream.add(f"mod{l}1", dram["mod_w"][l], 11, first=MODS - 18)
            stream.add(f"xq{l}", dram["w_in"][l], 8, first=61, split=True)
            stream.add(f"mod{l}2", dram["mod_w"][l], 7, first=MODS - 7)
            stream.add(f"gates{l}", dram["w_in"][l], 24, first=69, split=True)
            stream.add(f"branch{l}", dram["w_branch"][l], 24, split=True)
            stream.add(f"out{l}", dram["w_out"][l], 8, split=True)
            stream.add(f"ffn{l}", dram["w_ffn"][l], 3 * FT, split=True)
        stream.add("even_in", dram["even_in"], 20, split=True)
        stream.add("even_out", dram["even_out"], 8)
        for s in range(2):
            stream.add(f"even_ffn{s}", dram["even_ffn"], 3 * FT, split=True)
        stream.add("odd_in", dram["odd_in"], 7)
        stream.add("uq", dram["w_uq"], 12, width=512)
        stream.add("ukv", dram["w_ukv"], 16, width=256)
        stream.add("odd_out", dram["odd_out"], 8)
        stream.add("moe", dram["moe"], 3 * FT * NE, split=True)

        def sa_units(l):
            units = []
            for p in range(NP2):
                for h in range(0, SAH, 2):
                    nk = P * (p + 1)
                    units.append(dict(
                        logits=[[((i * 256), nk, [(Bq[:, h + i, p * P:(p + 1) * P], Bq[:, SAH + h + i, 0:nk])])
                                 for i in range(2)]],
                        nk=nk, subs=2, mask=negm[p][:, 0:nk], turn=[(i, kt) for i in range(2) for kt in range(p + 1)],
                        out=lambda pt, h=h, p=p: [
                            (i * P, [(vtok[:, kt, (h + i) * P:(h + i + 1) * P],
                                      pt[:, (i * (p + 1) + kt) * P:(i * (p + 1) + kt + 1) * P])
                                     for kt in range(p + 1)]) for i in range(2)],
                        dst=(Bq[:, 2 * SAH + h:2 * SAH + h + 2, p * P:(p + 1) * P], 256)))
            return units

        def xa_units(l):
            units = []
            for p in range(NP2):
                for h in range(0, XAH, 2):
                    units.append(dict(
                        logits=[[(i * 256, T, [(C[:, 2 * (h + i) + d, p * P:(p + 1) * P], C[:, 8 + 2 * (h + i) + d, :])
                                               for d in range(2)]) for i in range(2)]],
                        nk=T, subs=2, mask=None, turn=[(i, kt) for i in range(2) for kt in range(2)],
                        out=lambda pt, h=h: [
                            ((2 * i + d) * P, [(vtok[:, kt, (2 * (h + i) + d) * P:(2 * (h + i) + d + 1) * P],
                                                pt[:, (2 * i + kt) * P:(2 * i + kt + 1) * P]) for kt in range(2)])
                            for i in range(2) for d in range(2)],
                        dst=(C[:, 2 * h:2 * h + 4, p * P:(p + 1) * P], 512)))
            return units

        block = ctx.enter_context(nc.Block())

        @block.sync
        def _(sync):
            sy = Engine(c, sync, "sync")
            sync.dma_start(consts[:, :], dram["consts"]).then_inc(*sy.count("const_loaded", "all", 16))
            sync.dma_start(vecs[:, :], dram["vecs"]).then_inc(*sy.count("vec_loaded", "all", 16))
            sync.dma_start(x[:, :, :], dram["x"]).then_inc(*sy.count("x_loaded", "all", 16))
            load_stream(sync, stream, ring, c)

        @block.gpsimd
        def _(pool):
            po = Engine(c, pool, "pool")
            pool.dma_start(root[:, 0:T].bitcast(I32), dram["pos"][0, :].partition_broadcast(P)).then_inc(*po.count("pos_loaded", "all", 16))
            for l in range(DEPTH):
                split_gemm_rest(po, stream, f"sa{l}", ring, first_w, nc.gpsimd.tensor_tensor)
                pool.wait_ge(*c.full(("o", l, NCH - 1)))
                pool.dma_start(memn[:, :, :], dram["mem"]).then_inc(*po.count("mem_loaded", l, 16))
                pool.wait_ge(*c.at("dn_done", l))
                split_gemm_rest(po, stream, f"mem{l}", ring, mem_w, nc.gpsimd.tensor_tensor)
                for b, src in enumerate((A[:, 24:32, :], Bq[:, 16:24, :], C[:, 0:8, :])):
                    if b == 0:
                        pool.wait_ge(*c.at("sparse_done", l))
                    else:
                        pool.wait_ge(*c.empty((("xa", l), "mixed", 3)))
                    nc.gpsimd.tensor_copy(branch_x[b][0][:, :, :], src).then_inc(*po.count("branch_high", (l, b)))
                    pool.wait_ge(*c.at("branch_high", (l, b)))
                    nc.gpsimd.tensor_tensor(branch_x[b][1][:, :, :], src, branch_x[b][0][:, :, :], ALU.subtract)\
                        .then_inc(*po.count("branch_split", (l, b)))
            pool.wait_ge(*c.at("x_new", (DEPTH - 1, "out")))
            for dst, name in ((H[:, :, T:T2], "ctx"), (rope[:, :, :].rearrange("p a t -> p (a t)"), "tables2"),
                              (rot_ax, "rot_ax"), (pool_w, "pool_w")):
                pool.dma_start(dst, dram[name]).then_inc(*po.count("second_loaded", "all", 16))
            for a in pools:
                nc.gpsimd.memset(a.rearrange("p s e t -> p (s e t)"), 0.0).then_inc(*po.count("pools_cleared", "all"))
            pool.wait_ge(*c.at("result", "x"))
            pool.dma_start(dram["y"], x[:, :, :]).then_inc(*po.count("stored", "y", 16))
            pool.wait_ge(*c.at("stored", "y"))

        @block.tensor
        def _(pe):
            te = Tensor(c, pe)
            pe.wait_ge(*c.at("const_loaded", "all"))
            ident, mm = k["ident"], nc.tensor.matmul
            te.in_turn = BANKS - 1
            pe.wait_ge(*c.at("cond_silu", "all"))
            pe.wait_ge(*te.take("mods", bank=BANKS - 1))
            mod_bank, mod_next = te.bank, [0] * DEPTH

            def some_mods(l, count):
                for i in range(mod_next[l], mod_next[l] + count):
                    part = (i >= MODS - 18) + (i >= MODS - 7)
                    _, g0, _, _, first = stream.phases[f"mod{l}{part}"]
                    g = g0 + i - first
                    pe.wait_ge(c.sem(f"slab_loaded{g % RING}"), 16 * (g // RING + 1))
                    at = 2 * (MODS * l + i)
                    for j in range(KT):
                        last = mm(mod_bank[:, at:at + 2], ring[:, g % RING, j * P:(j + 1) * P], cond[:, j, :],
                                  start=j == 0, stop=j == KT - 1)
                    last.then_inc(c.sem(f"slab_done{g % RING}"), 1)
                mod_next[l] += count
            for l in range(DEPTH):
                norm_tensor(te, k, ("mix", l), sq8, KT, T)
                pe.wait_ge(*c.at("split", ("mix", l)))
                split_gemm_tensor(te, stream, f"dn{l}", l, first_w, first_x)
                sa_slabs = lambda *part: split_gemm_tensor(te, stream, f"sa{l}", l, first_w, first_x, part=part)
                sa_slabs(0, SA_PARTS[0])
                pe.wait_ge(*c.empty((f"dn{l}", l, 32)))
                pe.wait_ge(*te.take(("narrow", l)))
                ps = te.bank
                for p in range(NP2):
                    last = nc.tensor.transpose(ps[:, p * P:(p + 1) * P], A[:, 32, p * P:(p + 1) * P], ident)
                last.then_inc(*te.filled(("narrow", l)))
                for g in range(2):
                    sa_slabs(SA_PARTS[g], SA_PARTS[g + 1])
                    pe.wait_ge(*c.at("squared", ("l2", l, g)))
                    for j in range(4):
                        pe.wait_ge(*te.take(("l2", l, g, j), bank=(6, 3, 4, 5)[j]))
                        ps = te.bank
                        mm(ps[:, :], k["ones"], squares[:, j * 512:(j + 1) * 512], start=True, stop=True).then_inc(*te.filled(("l2", l, g, j)))
                sa_slabs(SA_PARTS[2], 28)
                some_mods(l, MODS_AT[0])
                pe.wait_ge(*c.at("decay_log", l))
                pe.wait_ge(*te.take(("sums", l)))
                ps = te.bank
                for j, m in enumerate(("upto", "after", "chunk0", "chunk1")):
                    last = mm(ps[:, 16 * j:16 * j + 16], k[m], gate, start=True, stop=True)
                last.then_inc(*te.filled(("sums", l)))
                pe.wait_ge(*c.at("unit", (l, 1)))
                pe.wait_ge(*c.at("conv_silu", (l, 2)))
                for g in range(4):
                    p, h0 = g // 2, 4 * (g % 2)
                    for name, at in (("ktok", 8), ("vtok", 16)):
                        pe.wait_ge(*te.take((name, l, g)))
                        ps = te.bank
                        for i in range(4):
                            last = nc.tensor.transpose(ps[:, i * P:(i + 1) * P], A[:, at + h0 + i, p * P:(p + 1) * P], ident)
                        last.then_inc(*te.filled((name, l, g)))
                pe.wait_ge(*c.at("unit", (l, 0)))
                for g in range(4):
                    some_mods(l, MODS_AT[2])
                    p, h0 = g // 2, 4 * (g % 2)
                    pe.wait_ge(*te.take(("cum", l, g)))
                    ps = te.bank
                    for i in range(4):
                        last = mm(ps[:, i * P:(i + 1) * P], gate[:, p * 8 + h0 + i:p * 8 + h0 + i + 1].to_broadcast([P, P]),
                                  k["upto"], start=True, stop=True)
                    last.then_inc(*te.filled(("cum", l, g)))
                    for name, at in (("kk", 8), ("kq", 0)):
                        pe.wait_ge(*te.take((name, l, g)))
                        ps = te.bank
                        for i in range(4):
                            last = mm(ps[:, i * P:(i + 1) * P], A[:, 8 + h0 + i, p * P:(p + 1) * P],
                                      A[:, at + h0 + i, p * P:(p + 1) * P], start=True, stop=True)
                        last.then_inc(*te.filled((name, l, g)))
                for g in range(4):
                    some_mods(l, MODS_AT[3])
                    pe.wait_ge(*c.at("inv0", (l, g)))
                    pe.wait_ge(*te.take(("x0", l, g)))
                    ps = te.bank
                    for i in range(4):
                        last = nc.tensor.transpose(ps[:, i * P:(i + 1) * P], Pl[:, 4 * g + i, :], ident)
                    last.then_inc(*te.filled(("x0", l, g)))
                for lev in range(1, 6):
                    some_mods(l, MODS_AT[4])
                    for g in range(4):
                        pe.wait_ge(*c.at("merge_mask", (l, lev, g)))
                        if lev == 1:
                            pe.wait_ge(*c.empty(("x0", l, g)))
                        else:
                            pe.wait_ge(*c.at("inv", (l, lev - 1, g)))
                        pe.wait_ge(*te.take(("ny", l, lev, g)))
                        ps = te.bank
                        for i in range(4):
                            last = mm(ps[:, i * P:(i + 1) * P], MK[:, 4 * g + i, :], X[:, 4 * g + i, :], start=True, stop=True)
                        last.then_inc(*te.filled(("ny", l, lev, g)))
                    for g in range(4):
                        pe.wait_ge(*c.empty(("ny", l, lev, g)))
                        pe.wait_ge(*te.take(("nx", l, lev, g)))
                        ps = te.bank
                        for i in range(4):
                            last = mm(ps[:, i * P:(i + 1) * P], Pl[:, 4 * g + i, :], Y[:, 4 * g + i, :], start=True, stop=True)
                        last.then_inc(*te.filled(("nx", l, lev, g)))
                        if lev < 5:
                            pe.wait_ge(*te.take(("np", l, lev, g)))
                            ps = te.bank
                            for i in range(4):
                                last = mm(ps[:, i * P:(i + 1) * P], Y[:, 4 * g + i, :], Pl[:, 4 * g + i, :], start=True, stop=True)
                            last.then_inc(*te.filled(("np", l, lev, g)))
                pe.wait_ge(*c.at("toks", l))
                for g in range(4):
                    pe.wait_ge(*c.at("inv", (l, 5, g)))
                    pe.wait_ge(*te.take(("u", l, g)))
                    ps = te.bank
                    for i in range(4):
                        last = mm(ps[:, i * P:(i + 1) * P], X[:, 4 * g + i, :], VB[:, 4 * g + i, :], start=True, stop=True)
                    last.then_inc(*te.filled(("u", l, g)))
                    pe.wait_ge(*te.take(("w", l, g)))
                    ps = te.bank
                    for i in range(4):
                        last = mm(ps[:, i * P:(i + 1) * P], KB[:, 4 * g + i, :], X[:, 4 * g + i, :], start=True, stop=True)
                    last.then_inc(*te.filled(("w", l, g)))
                def rope_product(j):
                    if j < 8:
                        pe.wait_ge(*c.empty((f"sa{l}", l, 2 * j + 1)))
                        src, mats = Bq[:, 2 * j:2 * j + 2, :], ("rot_sa",)
                    elif j < 10:
                        pe.wait_ge(*c.empty((f"sa{l}", l, 25 + 2 * (j - 8))))
                        src, mats = Bq[:, 24 + 2 * (j - 8):26 + 2 * (j - 8), :], ("rot_ix",)
                    else:
                        src, mats = A[:, 32:33, :], ("dup", "dup_rot")
                    pe.wait_ge(*te.take(("rope", l, j)))
                    ps = te.bank
                    for i, m in enumerate(mats):
                        w = 2 * T // len(mats)
                        last = mm(ps[:, i * w:(i + 1) * w], k[m], src.rearrange("p a t -> p (a t)"), start=True, stop=True)
                    last.then_inc(*te.filled(("rope", l, j)))

                for ch in range(NCH):
                    p, r = ch // 2, 64 * (ch % 2)
                    rows = slice(r, r + 64)
                    for j in range(2):
                        pe.wait_ge(*c.empty(("u", l, 2 * p + j)))
                        pe.wait_ge(*c.empty(("w", l, 2 * p + j)))
                    pe.wait_ge(*c.at("state", (l, ch)))
                    for j in range(2):
                        pe.wait_ge(*te.take(("ws", l, ch, j)))
                        ps = te.bank
                        for i in range(4):
                            h = 4 * j + i
                            last = mm(ps[rows, i * P:(i + 1) * P], WT[:, 8 * p + h, rows], S[:, h, :], start=True, stop=True)
                        last.then_inc(*te.filled(("ws", l, ch, j)))
                    for j in ROPE_AT[ch]:
                        rope_product(j)
                    some_mods(l, MODS_AT[5])
                    pe.wait_ge(*c.at("vnew", (l, ch)))
                    if ch == 0:
                        pe.wait_ge(*c.at("qdec", (l, 3)))
                    pe.wait_ge(*te.take(("o", l, ch)))
                    ps = te.bank
                    for h in range(DNH):
                        o = ps[:, h * 64:(h + 1) * 64]
                        mm(o, S[:, h, :], A[:, h, ch * 64:(ch + 1) * 64], start=True, stop=False)
                        last = mm(o, VN[rows, h, :], AT[rows, 8 * p + h, rows], start=False, stop=True)
                    last.then_inc(*te.filled(("o", l, ch)))
                    if ch < NCH - 1:
                        for j in range(2):
                            pe.wait_ge(*te.take(("su", l, ch, j)))
                            ps = te.bank
                            for i in range(4):
                                h = 4 * j + i
                                last = mm(ps[:, i * P:(i + 1) * P], KD[rows, 8 * p + h, :], VN[rows, h, :], start=True, stop=True)
                            last.then_inc(*te.filled(("su", l, ch, j)))
                pe.wait_ge(*c.at("squared", ("o2", l)))
                for j in range(4):
                    pe.wait_ge(*te.take(("o2", l, j)))
                    ps = te.bank
                    mm(ps[:, :], k["ones"], squares[:, j * 512:(j + 1) * 512], start=True, stop=True).then_inc(*te.filled(("o2", l, j)))
                for j in range(4):
                    kt, h0 = j // 2, 4 * (j % 2)
                    pe.wait_ge(*c.empty((f"sa{l}", l, 16 + h0 + 3)))
                    pe.wait_ge(*te.take(("svt", l, j)))
                    ps = te.bank
                    for i in range(4):
                        last = nc.tensor.transpose(ps[:, i * P:(i + 1) * P], Bq[:, 16 + h0 + i, kt * P:(kt + 1) * P], ident)
                    last.then_inc(*te.filled(("svt", l, j)))
                some_mods(l, MODS_AT[6])
                pe.wait_ge(*c.at("index_rope", l))
                for p in range(NP2):
                    for j in range(4):
                        pe.wait_ge(*te.take(("score", l, p, j)))
                        ps = te.bank
                        r = slice(64 * (j % 2), 64 * (j % 2) + 64)
                        for i in range(2):
                            last = mm(ps[:, i * T:i * T + P * (p + 1)], Bq[r, 24 + 2 * (j // 2) + i, p * P:(p + 1) * P], ixk[r, 0:P * (p + 1)], start=True, stop=True)
                        last.then_inc(*te.filled(("score", l, p, j)))
                some_mods(l, MODS - 18 - mod_next[l])
                norm_tensor(te, k, ("mem", l), sq8, KT, T)
                pe.wait_ge(*c.at("split", ("mem", l)))
                split_gemm_tensor(te, stream, f"mem{l}", l, mem_w, mem_x)
                pe.wait_ge(*c.at("roped", (l, 9)))
                pe.wait_ge(*c.empty(("svt", l, 3)))
                att_tensor(te, k, ("sa", l), sa_units(l), P_of, PT_of, ident, lambda: some_mods(l, 1))
                pe.wait_ge(*c.at("split", ("late", l)))
                split_gemm_tensor(te, stream, f"xq{l}", l, mem_w, late_x)
                for j in range(4):
                    kt, h0 = j // 2, 4 * (j % 2)
                    pe.wait_ge(*c.empty((f"mem{l}", l, 8 + h0 + 3)))
                    pe.wait_ge(*te.take(("mvt", l, j)))
                    ps = te.bank
                    for i in range(4):
                        last = nc.tensor.transpose(ps[:, i * P:(i + 1) * P], C[:, 16 + h0 + i, kt * P:(kt + 1) * P], ident)
                    last.then_inc(*te.filled(("mvt", l, j)))
                pe.wait_ge(*c.empty((f"xq{l}", l, 7)))
                pe.wait_ge(*c.empty(("mvt", l, 3)))
                att_tensor(te, k, ("xa", l), xa_units(l), P_of, PT_of, ident, lambda: some_mods(l, 1))
                split_gemm_tensor(te, stream, f"gates{l}", l, gates_w, late_x)
                _, g0, _, _, _ = stream.phases[f"branch{l}"]
                products = rounded_tensor(te, stream, f"branch{l}", gates_w)
                for b in range(3):
                    pe.wait_ge(*c.at("branch_split", (l, b)))
                for i in range(24):
                    xh, xl = branch_x[i % 3]
                    pe.wait_ge(*te.take(("branch", l, i), bank=(g0 + i) % RING))
                    products(i, 0, [(te.bank[:, 0:T], kk, xh[:, kk, :], xl[:, kk, :], kk == 0, kk == KT - 1) for kk in range(KT)])
                pe.wait_ge(*c.at("merged_split", (l, KT - 1)))
                split_gemm_tensor(te, stream, f"out{l}", l, gates_w, merged_x)
                norm_tensor(te, k, ("ffn", l), sq8, KT, T)
                pe.wait_ge(*c.at("split", ("ffn", l)))
                ffn_tensor(te, stream, f"ffn{l}", l, ffn_w, ffn_x[0], hidden, FT)
            norm_tensor(te, k, "final", sq8, KT, T)
            te.in_turn = BANKS
            pe.wait_ge(*c.at("lam_prod", "all"))
            pe.wait_ge(*te.take("lam"))
            ps = te.bank
            mm(ps[:, 0:2], k["ones"], lamb[:, 0:2], start=True, stop=True).then_inc(*te.filled("lam"))
            norm_tensor(te, k, "e1", sq2, KT, T2)
            pe.wait_ge(*c.at("split", "e1"))
            split_gemm_tensor(te, stream, "even_in", 0, even_w, even_x, T2)
            pe.wait_ge(*c.at("second_loaded", "all"))
            for j in range(6):
                pe.wait_ge(*c.empty(("even_in", 0, 2 + 2 * j + 1)))
                pe.wait_ge(*te.take(("axial", j)))
                ps = te.bank
                mm(ps[:, :].rearrange("p (a t) -> p a t", a=2), rot_ax, Z[:, 2 + 2 * j:4 + 2 * j, 0:T], start=True, stop=True).then_inc(*te.filled(("axial", j)))
            for kt in range(4):
                for j in range(2):
                    pe.wait_ge(*c.empty(("even_in", 0, 19)))
                    pe.wait_ge(*te.take(("evt", kt, j)))
                    ps = te.bank
                    for i in range(3):
                        last = nc.tensor.transpose(ps[:, i * P:(i + 1) * P], Z[:, 14 + 3 * j + i, kt * P:(kt + 1) * P], ident)
                    last.then_inc(*te.filled(("evt", kt, j)))
            pe.wait_ge(*c.at("pooled", "all"))
            for j in range(2):
                pe.wait_ge(*te.take(("pool", j)))
                ps = te.bank
                mm(ps[:, :], pool_w[:, j * P:(j + 1) * P], Z[:, j, :], start=True, stop=True).then_inc(*te.filled(("pool", j)))
            pe.wait_ge(*c.at("axial_done", 5))
            pe.wait_ge(*c.empty(("evt", 3, 1)))
            att_tensor(te, k, "diff", diff_units(), lambda u: att_p2[:, u % 3], lambda u: att_t2[:, u % 3], ident)
            pe.wait_ge(*c.at("squared", "heads"))
            for h in range(DH):
                pe.wait_ge(*te.take(("heads", h)))
                ps = te.bank
                mm(ps[:, :], k["ones"], sq2[:, h, :], start=True, stop=True).then_inc(*te.filled(("heads", h)))
            pe.wait_ge(*c.at("heads_normed", "all"))
            gemm_tensor(te, stream, "even_out", ring, 0, lambda i: Z[:, i, :], T2)
            norm_tensor(te, k, "e2", sq2, KT, T2)
            for n in range(2):
                pe.wait_ge(*c.at("split", ("e2", n)))
                ffn_tensor(te, stream, f"even_ffn{n}", ("even", n), ffn_w, ffn_x[n], hidden, FT)
            norm_tensor(te, k, "o1", sq2, KT, T2)
            pe.wait_ge(*c.at("normed", "o1"))
            gemm_tensor(te, stream, "odd_in", ring, 0, lambda i: hn2[:, i, :], T2)
            norm_tensor(te, k, "cq", sq2, 4, T)
            norm_tensor(te, k, "ckv", sq2, 2, T2)
            pe.wait_ge(*c.at("normed", "cq"))
            gemm_tensor(te, stream, "uq", ring, 0, lambda i: cqn[:, i, :], T, tiles=4)
            pe.wait_ge(*c.at("normed", "ckv"))
            gemm_tensor(te, stream, "ukv", ring, 0, lambda i: ckvn[:, i, :], T2, tiles=2)
            for j in range(2):
                pe.wait_ge(*c.empty(("uq", 0, 11)))
                pe.wait_ge(*te.take(("axq", j)))
                ps = te.bank
                mm(ps[:, :], rot_ax, QN[:, 8 + 2 * j:10 + 2 * j, :].rearrange("p a t -> p (a t)"), start=True, stop=True).then_inc(*te.filled(("axq", j)))
            pe.wait_ge(*te.take("axk"))
            ps = te.bank
            mm(ps[:, 0:T], rot_ax, Zo[:, 6, 0:T], start=True, stop=True).then_inc(*te.filled("axk"))
            pe.wait_ge(*c.empty(("ukv", 0, 15)))
            for kt in range(4):
                for j in range(2):
                    pe.wait_ge(*te.take(("ovt", kt, j)))
                    ps = te.bank
                    for i in range(4):
                        last = nc.tensor.transpose(ps[:, i * P:(i + 1) * P], KV[:, 8 + 4 * j + i, kt * P:(kt + 1) * P], ident)
                    last.then_inc(*te.filled(("ovt", kt, j)))
            pe.wait_ge(*c.at("axial2_done", "all"))
            pe.wait_ge(*c.empty(("ovt", 3, 1)))
            att_tensor(te, k, "latent", latent_units(), lambda u: att_p3[:, u % 3], lambda u: att_t3[:, u % 3], ident)
            pe.wait_ge(*c.empty(("latent", "mixed", 15)))
            gemm_tensor(te, stream, "odd_out", ring, 0, lambda i: QN[:, i, :], T)
            norm_tensor(te, k, "o2", sq2, KT, T)
            pe.wait_ge(*c.at("split", "o2"))
            pe.wait_ge(*te.take("router"))
            ps = te.bank
            for p in range(NP2):
                for i in range(KT):
                    last = mm(ps[:, 8 * p:8 * p + 8], hn[:, i, p * P:(p + 1) * P], v["router"][:, 8 * i:8 * i + 8], start=i == 0, stop=i == KT - 1)
            last.then_inc(*te.filled("router"))
            pe.wait_ge(*c.at("routed", "all"))
            for j in range(4):
                pe.wait_ge(*te.take(("spread", j)))
                ps = te.bank
                for i in range(2):
                    for p in range(NP2):
                        w = rout[:, 8 * p + 2 * j + i:8 * p + 2 * j + i + 1].to_broadcast([P, P])
                        last = mm(ps[:, (2 * i + p) * P:(2 * i + p + 1) * P], w, ident, start=True, stop=True)
                last.then_inc(*te.filled(("spread", j)))
            ffn_tensor(te, stream, "moe", "moe", ffn_w, ffn_x[0], hidden, FT * NE)
            norm_tensor(te, k, "last", sq2, KT, T)

        @block.scalar
        def _(act):
            sc = Engine(c, act, "scalar")
            sc.last_norm, sc.eps = None, eps
            af = nc.scalar.activation
            act.wait_ge(*c.at("eps", "all"))
            for i in range(2):
                act.wait_ge(*c.at("angle", i))
                af(rope[:, 2 * i + 1, :], rope[:, 2 * i + 1, :], ACT.Sin).then_inc(*sc.count("sincos", (i, 1)))
                af(rope[:, 2 * i, :], rope[:, 2 * i, :], ACT.Sin).then_inc(*sc.count("sincos", (i, 0)))
            act.wait_ge(*c.at("x_loaded", "all"))
            act.wait_ge(*c.at("vec_loaded", "all"))
            af(cond[:, :, :].rearrange("p k s -> p (k s)"), v["cond"], ACT.Silu).then_inc(*sc.count("cond_silu", "all"))
            for l in range(DEPTH):
                if l:
                    act.wait_ge(*c.at("x_new", (l - 1, "ffn")))
                norm_scalar(sc, ("mix", l), x[:, :, :], sq8, root, KT, T)
                split_gemm_read(sc, stream, f"dn{l}", l, lambda i, ps: af(tile_of(A, i), ps[:, 0:T], ACT.Copy),
                                round_high(sc, stream, f"dn{l}", ring, first_w[0]))
                copy_slab = round_high(sc, stream, f"sa{l}", ring, first_w[0])
                sa_slabs = lambda *part: split_gemm_read(sc, stream, f"sa{l}", l, lambda i, ps: af(tile_of(Bq, i), ps[:, 0:T], ACT.Copy), copy_slab, part)
                sa_slabs(0, SA_PARTS[0])
                act.wait_ge(*c.full(("narrow", l)))
                ps = c.bank(("narrow", l))
                af(stok.rearrange("p a f -> p (a f)"), ps[:, 0:256], ACT.Copy).then_inc(*sc.emptied(("narrow", l)))
                for g in range(3):
                    act.wait_ge(*c.at("conv", (l, g)))
                    af(A[:, 8 * g:8 * g + 8, :], conv[g], ACT.Silu).then_inc(*sc.count("conv_silu", (l, g)))
                act.wait_ge(*sc.last())
                af(sq8, A[:, 0:8, :], ACT.Square).then_inc(*sc.count("squared", ("l2", l, 0)))
                sa_slabs(SA_PARTS[0], SA_PARTS[1])
                for g in range(2):
                    if g:
                        act.wait_ge(*c.at("unit", (l, 0)))
                    for j in range(4):
                        act.wait_ge(*c.full(("l2", l, g, j)))
                        ps = c.bank(("l2", l, g, j))
                        af(sroot[:, 2 * j:2 * j + 2, :].rearrange("p a t -> p (a t)"), ps[:, :], ACT.Sqrt, bias=eps[:, 0:1]).then_inc(*sc.emptied(("l2", l, g, j)))
                    if g == 0:
                        af(sq8, A[:, 8:16, :], ACT.Square).then_inc(*sc.count("squared", ("l2", l, 1)))
                        sa_slabs(SA_PARTS[1], SA_PARTS[2])
                        act.wait_ge(*c.at("const_loaded", "all"))
                        af(A[:, 24:32, :], A[:, 24:32, :], ACT.Silu).then_inc(*sc.count("z_silu", l))
                        af(beta.rearrange("p (a b) -> p a b", a=2), stok[:, :, 64:72], ACT.Sigmoid).then_inc(*sc.count("beta", l))
                sa_slabs(SA_PARTS[2], 28)
                af(gneg, v["a_log"][:, 8 * l:8 * l + 8], ACT.Exp).then_inc(*sc.count("a_exp", l))
                act.wait_ge(*c.at("decay_in", l))
                af(y1, y1, ACT.Exp).then_inc(*sc.count())
                act.wait_ge(*sc.last())
                af(y1, y1, ACT.Ln, bias=eps[:, 1:2]).then_inc(*sc.count("decay_ln", l))
                act.wait_ge(*c.at("sums_copied", l))
                af(gexp, graw, ACT.Exp).then_inc(*sc.count("sums_exp", l))
                for g in range(4):
                    act.wait_ge(*c.full(("cum", l, g)))
                    ps = c.bank(("cum", l, g))
                    if g:
                        act.wait_ge(*c.at("qdec", (l, g - 1)))
                    af(EGB, ps[:, :], ACT.Exp).then_inc(*sc.count("cum_exp", (l, g)))
                    act.wait_ge(*c.at("decay_diff", (l, g)))
                    af(DEC, DEC, ACT.Exp, scale=-1.0).then_inc(*sc.count())
                    af(DECT, DECT, ACT.Exp).then_inc(*sc.count("decay_exp", (l, g)))
                for g in range(4):
                    act.wait_ge(*c.full(("x0", l, g)))
                    ps = c.bank(("x0", l, g))
                    af(X[:, 4 * g:4 * g + 4, :], ps[:, :].rearrange("p (a b) -> p a b", b=P), ACT.Copy).then_inc(*sc.emptied(("x0", l, g)))
                for lev in range(1, 6):
                    for g in range(4):
                        act.wait_ge(*c.full(("ny", l, lev, g)))
                        ps = c.bank(("ny", l, lev, g))
                        if lev > 1:
                            act.wait_ge(*c.at("inv", (l, lev - 1, g)))
                        af(Y[:, 4 * g:4 * g + 4, :], ps[:, :].rearrange("p (a b) -> p a b", b=P), ACT.Copy).then_inc(*sc.emptied(("ny", l, lev, g)))
                for g in range(4):
                    for name, dst in (("u", UU), ("w", WT)):
                        act.wait_ge(*c.full((name, l, g)))
                        ps = c.bank((name, l, g))
                        af(dst[:, 4 * g:4 * g + 4, :], ps[:, :].rearrange("p (a b) -> p a b", b=P), ACT.Copy).then_inc(*sc.emptied((name, l, g)))
                for ch in range(NCH):
                    act.wait_ge(*c.full(("o", l, ch)))
                    ps = c.bank(("o", l, ch))
                    af(A[:, 16:24, ch * 64:(ch + 1) * 64], ps[:, :].rearrange("p (h t) -> p h t", t=64), ACT.Copy).then_inc(*sc.emptied(("o", l, ch)))
                act.wait_ge(*sc.last())
                af(sq8, A[:, 16:24, :], ACT.Square).then_inc(*sc.count("squared", ("o2", l)))
                for j in range(4):
                    act.wait_ge(*c.full(("o2", l, j)))
                    ps = c.bank(("o2", l, j))
                    af(gated[:, 2 * j:2 * j + 2, :].rearrange("p a t -> p (a t)"), ps[:, :], ACT.Sqrt, bias=eps[:, 0:1], scale=1.0 / P).then_inc(*sc.emptied(("o2", l, j)))
                for j in range(4):
                    kt, h0 = j // 2, 4 * (j % 2)
                    act.wait_ge(*c.full(("svt", l, j)))
                    ps = c.bank(("svt", l, j))
                    af(vtok[:, kt, h0 * P:(h0 + 4) * P], ps[:, :], ACT.Copy).then_inc(*sc.emptied(("svt", l, j)))
                for p in range(NP2):
                    for j in range(4):
                        n = 4 * p + j
                        act.wait_ge(*c.full(("score", l, p, j)))
                        ps = c.bank(("score", l, p, j))
                        if n >= 2:
                            act.wait_ge(*c.at("scored", (l, n - 2)))
                        nk = P * (p + 1)
                        src = ps[:, :].rearrange("p (s k) -> p s k", s=2)[:, :, 0:nk]
                        af(relu[:, n % 2, :, 0:nk], src, ACT.Relu).then_inc(*sc.emptied(("score", l, p, j)))
                act.wait_ge(*c.at("mem_loaded", l))
                act.wait_ge(*c.full(("o2", l, 3)))
                norm_scalar(sc, ("mem", l), memn[:, :, :], sq8, root, KT, T)
                split_gemm_read(sc, stream, f"mem{l}", l, lambda i, ps: af(tile_of(C, 8 + i), ps[:, 0:T], ACT.Copy),
                                round_high(sc, stream, f"mem{l}", ring, mem_w[0]))
                att_scalar(sc, ("sa", l), sa_units(l), P_of, PT_of, mx, smx)
                act.wait_ge(*sc.last())
                af(tick[:, 6:7], eps[:, 0:1], ACT.Copy).then_inc(*sc.count("sparse_done", l))
                split_gemm_read(sc, stream, f"xq{l}", l, lambda i, ps: af(tile_of(C, i), ps[:, 0:T], ACT.Copy),
                                round_high(sc, stream, f"xq{l}", ring, mem_w[0]))
                for j in range(4):
                    kt, h0 = j // 2, 4 * (j % 2)
                    act.wait_ge(*c.full(("mvt", l, j)))
                    ps = c.bank(("mvt", l, j))
                    af(vtok[:, kt, h0 * P:(h0 + 4) * P], ps[:, :], ACT.Copy).then_inc(*sc.emptied(("mvt", l, j)))
                att_scalar(sc, ("xa", l), xa_units(l), P_of, PT_of, mx, smx)
                split_gemm_read(sc, stream, f"gates{l}", l, lambda i, ps: af(tile_of(A, i), ps[:, 0:T], ACT.Sigmoid, bias=v["b_gate"][:, bass.ds(24 * l + i, 1)]),
                                round_high(sc, stream, f"gates{l}", ring, gates_w[0]))
                for name, n in ((f"branch{l}", 3 * KT), (f"out{l}", KT)):
                    copy_slab = round_high(sc, stream, name, ring, gates_w[0])
                    for q in range(n):
                        copy_slab(q, 0)
                act.wait_ge(*c.at("x_new", (l, "out")))
                norm_scalar(sc, ("ffn", l), x[:, :, :], sq8, root, KT, T)
                ffn_scalar(sc, stream, f"ffn{l}", l, ring, ffn_w[0], silu, FT)
            act.wait_ge(*c.at("x_new", (DEPTH - 1, "ffn")))
            norm_scalar(sc, "final", x[:, :, :], sq8, root, KT, T)
            act.wait_ge(*c.full("lam"))
            ps = c.bank("lam")
            af(lamb[:, 2:4], ps[:, 0:2], ACT.Exp).then_inc(*sc.emptied("lam"))
            act.wait_ge(*c.at("normed", "final"))
            act.wait_ge(*c.at("second_loaded", "all"))
            norm_scalar(sc, "e1", H, sq2, root, KT, T2)
            split_gemm_read(sc, stream, "even_in", 0, lambda i, ps: af(tile_of(Z, i), ps[:, :], ACT.Copy),
                            round_high(sc, stream, "even_in", ring, even_w[0]))
            for kt in range(4):
                for j in range(2):
                    act.wait_ge(*c.full(("evt", kt, j)))
                    ps = c.bank(("evt", kt, j))
                    af(vtok2[:, kt, 384 * j:384 * (j + 1)], ps[:, 0:384], ACT.Copy).then_inc(*sc.emptied(("evt", kt, j)))
            att_scalar(sc, "diff", diff_units(), lambda u: att_p2[:, u % 3], lambda u: att_t2[:, u % 3], mx2, smx2)
            act.wait_ge(*sc.last())
            af(sq2[:, 0:DH, :], Z[:, 2:2 + DH, :], ACT.Square).then_inc(*sc.count("squared", "heads"))
            for h in range(DH):
                act.wait_ge(*c.full(("heads", h)))
                ps = c.bank(("heads", h))
                af(hn2[:, h, :], ps[:, :], ACT.Sqrt, bias=eps[:, 0:1], scale=1.0 / P).then_inc(*sc.emptied(("heads", h)))
            act.wait_ge(*c.at("h_new", "e1"))
            norm_scalar(sc, "e2", H, sq2, root, KT, T2)
            for n in range(2):
                ffn_scalar(sc, stream, f"even_ffn{n}", ("even", n), ring, ffn_w[0], silu, FT)
            act.wait_ge(*c.at("h_new", "e2"))
            norm_scalar(sc, "o1", H, sq2, root, KT, T2)
            gemm_read(sc, stream, "odd_in", 0, lambda i, ps: af(tile_of(Zo, i), ps[:, :], ACT.Copy))
            act.wait_ge(*sc.last())
            norm_scalar(sc, "cq", Zo[:, 0:4, 0:T], sq2, root, 4, T)
            norm_scalar(sc, "ckv", Zo[:, 4:6, :], sq2, root, 2, T2)
            gemm_read(sc, stream, "uq", 0, lambda i, ps: af(tile_of(QN, i), ps[:, 0:T], ACT.Copy))
            gemm_read(sc, stream, "ukv", 0, lambda i, ps: af(tile_of(KV, i), ps[:, :], ACT.Copy))
            for kt in range(4):
                for j in range(2):
                    act.wait_ge(*c.full(("ovt", kt, j)))
                    ps = c.bank(("ovt", kt, j))
                    af(vtok3[:, kt, 512 * j:512 * (j + 1)], ps[:, :], ACT.Copy).then_inc(*sc.emptied(("ovt", kt, j)))
            att_scalar(sc, "latent", latent_units(), lambda u: att_p3[:, u % 3], lambda u: att_t3[:, u % 3], mx2, smx2)
            act.wait_ge(*c.at("h_new", "o1"))
            norm_scalar(sc, "o2", H[:, :, 0:T], sq2, root, KT, T)
            act.wait_ge(*c.at("router_max", "all"))
            for p in range(NP2):
                ins = af(rout[:, 16 + 8 * p:24 + 8 * p], rout[:, 16 + 8 * p:24 + 8 * p], ACT.Exp, bias=rout[:, 32 + p:33 + p],
                         accum_out=rout[:, 34 + p:35 + p])
            ins.then_inc(*sc.count("router_exp", "all"))
            for j in range(4):
                act.wait_ge(*c.full(("spread", j)))
                ps = c.bank(("spread", j))
                af(expert_w[:, 2 * j:2 * j + 2, :], ps[:, :].rearrange("p (a t) -> p a t", a=2), ACT.Copy).then_inc(*sc.emptied(("spread", j)))
            ffn_scalar(sc, stream, "moe", "moe", ring, ffn_w[0], silu, FT * NE)
            act.wait_ge(*c.at("h_new", "moe"))
            norm_scalar(sc, "last", H[:, :, 0:T], sq2, root, KT, T)

        @block.vector
        def _(dve):
            ve = Engine(c, dve, "vector")

            def summed(name):
                return c.sem("split_used"), stream.split[name] + stream.phases[name][2]
            tt, ts, stt, copy = nc.vector.tensor_tensor, nc.vector.tensor_scalar, nc.vector.scalar_tensor_tensor, nc.vector.tensor_copy
            for b in range(BANKS):
                nc.vector.memset(c.banks[b][:, :], 0.0).then_inc(c.sem(f"bank_read{b}"), 1)
            nc.vector.memset(eps[:, 0:1], EPS).then_inc(*ve.count())
            nc.vector.memset(eps[:, 1:2], 1.0).then_inc(*ve.count("eps", "all"))
            dve.wait_ge(*c.at("pos_loaded", "all"))
            dve.wait_ge(*c.at("const_loaded", "all"))
            copy(squares[:, 0:T], root[:, 0:T].bitcast(I32)).then_inc(*ve.count())
            dve.wait_ge(*ve.last())
            for i in range(2):
                ang, n, cs, sn = squares[:, 256:512], squares[:, 512:768], rope[:, 2 * i, :], rope[:, 2 * i + 1, :]
                ts(ang, squares[:, 0:T], k["invf"][:, i:i + 1], None, ALU.mult).then_inc(*ve.count())
                dve.wait_ge(*ve.last())
                ts(n, ang, 1.0 / (2 * math.pi), ROUND, ALU.mult, ALU.add).then_inc(*ve.count())
                dve.wait_ge(*ve.last())
                ts(n, n, -ROUND, None, ALU.add).then_inc(*ve.count())
                for part in TWO_PI_PARTS:
                    dve.wait_ge(*ve.last())
                    stt(out=ang, in0=n, scalar=-part, in1=ang, op0=ALU.mult, op1=ALU.add).then_inc(*ve.count())
                dve.wait_ge(*ve.last())
                ts(sn, ang, 3.14159, -3.14159, ALU.min, ALU.max).then_inc(*ve.count())
                dve.wait_ge(*ve.last())
                stt(out=cs, in0=sn, scalar=-1.0, in1=sn, op0=ALU.mult, op1=ALU.max).then_inc(*ve.count())
                dve.wait_ge(*ve.last())
                ts(cs, cs, -1.0, math.pi / 2, ALU.mult, ALU.add).then_inc(*ve.count("angle", i))
                dve.wait_ge(*ve.last())
            dve.wait_ge(*c.at("vec_loaded", "all"))
            for l in range(DEPTH):
                if l:
                    dve.wait_ge(*ve.last())
                norm_vector(ve, ("mix", l), x, v["norm_mix"][:, 8 * l:8 * l + 8], root, hn, KT, T)
                split_vector(ve, ("mix", l), hn[:, :, :], first_x[0][:, :, :], first_x[1][:, :, :])
                split_gemm_rest(ve, stream, f"dn{l}", ring, first_w, tt)
                for g in range(3):
                    dve.wait_ge(*c.empty((f"dn{l}", l, 8 * g + 7)))
                    if g == 2:
                        dve.wait_ge(*c.full(("mix", l)))
                    acc = conv[g]
                    for tap in range(4):
                        for i in range(8):
                            w = v["conv"][:, 96 * l + 4 * (8 * g + i) + 3 - tap:][:, 0:1]
                            if tap == 0:
                                ins = ts(acc[:, i, :], A[:, 8 * g + i, :], w, None, ALU.mult)
                            else:
                                ins = stt(out=acc[:, i, tap:], in0=A[:, 8 * g + i, 0:T - tap], scalar=w,
                                          in1=acc[:, i, tap:], op0=ALU.mult, op1=ALU.add)
                        if tap < 3:
                            ins.then_inc(*ve.count())
                            dve.wait_ge(*ve.last())
                    ins.then_inc(*ve.count("conv", (l, g)))
                dve.wait_ge(*c.empty(("narrow", l)))
                two = lambda a: a.rearrange("p (a b) -> p a b", a=2)
                tt(two(y0), stok[:, :, 72:80], v["dt_bias"][:, 8 * l:8 * l + 8].unsqueeze(1).to_broadcast([P, 2, 8]), ALU.add).then_inc(*ve.count())
                dve.wait_ge(*ve.last())
                ts(y2, y0, -1.0, None, ALU.mult).then_inc(*ve.count())
                dve.wait_ge(*ve.last())
                tt(y1, y0, y2, ALU.min).then_inc(*ve.count("decay_in", l))
                ts(iw.rearrange("p (a b) -> p a b", a=2), stok[:, :, 80:88], 8 ** -0.5 * 64 ** -0.5, None, ALU.mult).then_inc(*ve.count())
                for g in range(2):
                    for j in range(4):
                        dve.wait_ge(*c.empty(("l2", l, g, j)))
                    dve.wait_ge(*ve.last())
                    nc.vector.reciprocal(sroot, sroot).then_inc(*ve.count())
                    dve.wait_ge(*ve.last())
                    at = A[:, 8 * g:8 * g + 8, :]
                    stt(out=at, in0=at, scalar=(P ** -0.5 if g == 0 else 1.0), in1=sroot, op0=ALU.mult, op1=ALU.mult).then_inc(*ve.count("unit", (l, g)))
                dve.wait_ge(*c.at("decay_ln", l))
                stt(out=y2, in0=y0, scalar=0.0, in1=y1, op0=ALU.max, op1=ALU.add).then_inc(*ve.count())
                dve.wait_ge(*ve.last())
                stt(out=two(gate), in0=two(y2), scalar=-1.0, in1=gneg.unsqueeze(1).to_broadcast([P, 2, 8]), op0=ALU.mult, op1=ALU.mult).then_inc(*ve.count("decay_log", l))
                dve.wait_ge(*c.full(("sums", l)))
                ps = c.bank(("sums", l))
                copy(graw, ps[:, 0:64]).then_inc(*ve.emptied(("sums", l)))
                dve.wait_ge(*ve.last())
                nc.vector.memset(tick[:, 0:1], 0.0).then_inc(*ve.count("sums_copied", l))
                dve.wait_ge(*c.at("sums_exp", l))
                dve.wait_ge(*c.at("beta", l))
                tt(bexp, beta, gexp[:, 0:16], ALU.mult).then_inc(*ve.count())
                dve.wait_ge(*ve.last())
                four = lambda a: a.unsqueeze(2).to_broadcast([P, 4, P])
                per = lambda ps: ps[:, :].rearrange("p (a b) -> p a b", b=P)
                for g in range(4):
                    s4 = slice(4 * g, 4 * g + 4)
                    dve.wait_ge(*c.full(("ktok", l, g)))
                    ps = c.bank(("ktok", l, g))
                    tt(KB[:, s4, :], per(ps), four(bexp[:, s4]), ALU.mult).then_inc(*ve.count())
                    tt(KD[:, s4, :], per(ps), four(gexp[:, 16 + 4 * g:20 + 4 * g]), ALU.mult).then_inc(*ve.emptied(("ktok", l, g)))
                    dve.wait_ge(*c.full(("vtok", l, g)))
                    ps = c.bank(("vtok", l, g))
                    tt(VB[:, s4, :], per(ps), four(beta[:, s4]), ALU.mult).then_inc(*ve.emptied(("vtok", l, g)))
                dve.wait_ge(*ve.last())
                nc.vector.memset(tick[:, 0:1], 0.0).then_inc(*ve.count("toks", l))
                for g in range(4):
                    p, h0 = g // 2, 4 * (g % 2)
                    s4 = slice(4 * g, 4 * g + 4)
                    dve.wait_ge(*c.at("cum_exp", (l, g)))
                    dve.wait_ge(*c.full(("cum", l, g)))
                    ps = c.bank(("cum", l, g))
                    dec, dect, egb = per(DEC), per(DECT), per(EGB)
                    for i in range(4):
                        gc = graw[:, 4 * g + i:4 * g + i + 1]
                        ts(dec[:, i, :], per(ps)[:, i, :], gc, 0.0, ALU.subtract, ALU.max)
                        ins = ts(dect[:, i, :], per(ps)[:, i, :], gc, 0.0, ALU.subtract, ALU.min)
                    ins.then_inc(*ve.count("decay_diff", (l, g)))
                    dve.wait_ge(*c.at("decay_exp", (l, g)))
                    tt(dec, dec, k["strict"].unsqueeze(1).to_broadcast([P, 4, P]), ALU.mult).then_inc(*ve.emptied(("cum", l, g)))
                    tt(dect, dect, k["incl"].unsqueeze(1).to_broadcast([P, 4, P]), ALU.mult).then_inc(*ve.count())
                    dve.wait_ge(*ve.last())
                    dve.wait_ge(*c.full(("kk", l, g)))
                    ps = c.bank(("kk", l, g))
                    for i in range(4):
                        ins = stt(out=M[:, 4 * g + i, :], in0=per(ps)[:, i, :], scalar=beta[:, 4 * g + i:4 * g + i + 1], in1=dec[:, i, :], op0=ALU.mult, op1=ALU.mult)
                    ins.then_inc(*ve.emptied(("kk", l, g)))
                    dve.wait_ge(*c.full(("kq", l, g)))
                    ps = c.bank(("kq", l, g))
                    tt(AT[:, s4, :], per(ps), dect, ALU.mult).then_inc(*ve.emptied(("kq", l, g)))
                    q = A[:, h0:h0 + 4, p * P:(p + 1) * P]
                    tt(q, q, egb, ALU.mult).then_inc(*ve.count("qdec", (l, g)))
                    dve.wait_ge(*ve.last())
                    mk = MK[:, s4, :]
                    tt(mk, M[:, s4, :], k["merge0"].unsqueeze(1).to_broadcast([P, 4, P]), ALU.mult).then_inc(*ve.count())
                    dve.wait_ge(*ve.last())
                    tt(Pl[:, s4, :], k["ident"].unsqueeze(1).to_broadcast([P, 4, P]), mk, ALU.subtract).then_inc(*ve.count("inv0", (l, g)))
                dve.wait_ge(*ve.last())
                for lev in range(1, 6):
                    for g in range(4):
                        s4 = slice(4 * g, 4 * g + 4)
                        if lev > 1:
                            dve.wait_ge(*c.full(("ny", l, lev - 1, g)))
                        tt(MK[:, s4, :], M[:, s4, :], k[f"merge{lev}"].unsqueeze(1).to_broadcast([P, 4, P]), ALU.mult).then_inc(*ve.count("merge_mask", (l, lev, g)))
                    for g in range(4):
                        s4 = slice(4 * g, 4 * g + 4)
                        if lev == 1:
                            dve.wait_ge(*c.empty(("x0", l, g)))
                        dve.wait_ge(*c.full(("nx", l, lev, g)))
                        ps = c.bank(("nx", l, lev, g))
                        ins = tt(X[:, s4, :], X[:, s4, :], per(ps), ALU.subtract)
                        if lev < 5:
                            ins.then_inc(*ve.emptied(("nx", l, lev, g)))
                            dve.wait_ge(*c.full(("np", l, lev, g)))
                            ps = c.bank(("np", l, lev, g))
                            ins = tt(Pl[:, s4, :], Pl[:, s4, :], per(ps), ALU.subtract)
                            ins.then_inc(*ve.emptied(("np", l, lev, g)))
                        else:
                            ins.then_inc(*ve.emptied(("nx", l, lev, g)))
                        dve.wait_ge(*ve.last())
                        nc.vector.memset(tick[:, 0:1], 0.0).then_inc(*ve.count("inv", (l, lev, g)))
                nc.vector.memset(S, 0.0).then_inc(*ve.count("state", (l, 0)))
                dve.wait_ge(*c.at("sincos", (1, 0)))

                def rope_step(j):
                    dve.wait_ge(*c.full(("rope", l, j)))
                    ps = c.bank(("rope", l, j))
                    r = slice(0, 32) if j < 8 else slice(0, P)
                    cs, sn = (rope[r, 0:1, :], rope[r, 1:2, :]) if j < 8 else (rope[:, 2:3, :], rope[:, 3:4, :])
                    if j < 10:
                        t = ropet[r, j % 2]
                        at = 2 * j if j < 8 else 24 + 2 * (j - 8)
                        xx = Bq[r, at:at + 2, :]
                        wide = lambda a: a.to_broadcast([a.shape[0], 2, T])
                        tt(t, ps[r, :].rearrange("p (a t) -> p a t", a=2), wide(sn), ALU.mult).then_inc(*ve.emptied(("rope", l, j)))
                        tt(xx, xx, wide(cs), ALU.mult).then_inc(*ve.count())
                        dve.wait_ge(*ve.last())
                        tt(xx, xx, t, ALU.add).then_inc(*ve.count("roped", (l, j)))
                    else:
                        t = ropet[:, 0, 0]
                        tt(t, ps[:, T:2 * T], rope[:, 3, :], ALU.mult).then_inc(*ve.count())
                        tt(ixk, ps[:, 0:T], rope[:, 2, :], ALU.mult).then_inc(*ve.emptied(("rope", l, j)))
                        dve.wait_ge(*ve.last())
                        tt(ixk, ixk, t, ALU.add).then_inc(*ve.count("index_rope", l))
                    dve.wait_ge(*ve.last())

                for ch in range(NCH):
                    p, r = ch // 2, 64 * (ch % 2)
                    rows = slice(r, r + 64)
                    for j in range(2):
                        dve.wait_ge(*c.empty(("u", l, 2 * p + j)))
                        dve.wait_ge(*c.full(("ws", l, ch, j)))
                        ps = c.bank(("ws", l, ch, j))
                        hs = slice(4 * j, 4 * j + 4)
                        if ch >= 1:
                            dve.wait_ge(*c.full(("su", l, ch - 1, 1)))
                        tt(VN[rows, hs, :], UU[rows, 8 * p + 4 * j:8 * p + 4 * j + 4, :], per(ps)[rows], ALU.subtract).then_inc(*ve.emptied(("ws", l, ch, j)))
                    dve.wait_ge(*ve.last())
                    nc.vector.memset(tick[:, 0:1], 0.0).then_inc(*ve.count("vnew", (l, ch)))
                    for j in ROPE_AT[ch]:
                        rope_step(j)
                    if ch < NCH - 1:
                        dve.wait_ge(*c.full(("o", l, ch)))
                        for j in range(2):
                            dve.wait_ge(*c.full(("su", l, ch, j)))
                            ps = c.bank(("su", l, ch, j))
                            for i in range(4):
                                h = 4 * j + i
                                cd = gexp[:, 32 + 16 * (ch % 2) + 8 * p + h:][:, 0:1]
                                ins = stt(out=S[:, h, :], in0=S[:, h, :], scalar=cd, in1=per(ps)[:, i, :], op0=ALU.mult, op1=ALU.add)
                            ins.then_inc(*ve.emptied(("su", l, ch, j)))
                        dve.wait_ge(*ve.last())
                        nc.vector.memset(tick[:, 0:1], 0.0).then_inc(*ve.count("state", (l, ch + 1)))
                for j in range(4):
                    dve.wait_ge(*c.empty(("o2", l, j)))
                dve.wait_ge(*c.at("z_silu", l))
                dve.wait_ge(*ve.last())
                nc.vector.reciprocal(gated, gated).then_inc(*ve.count())
                dve.wait_ge(*ve.last())
                o = A[:, 16:24, :]
                stt(out=o, in0=o, scalar=v["dn_norm"][:, l:l + 1], in1=gated, op0=ALU.mult, op1=ALU.mult).then_inc(*ve.count())
                dve.wait_ge(*ve.last())
                tt(A[:, 24:32, :], A[:, 24:32, :], o, ALU.mult).then_inc(*ve.count("dn_done", l))
                dve.wait_ge(*ve.last())
                for p in range(NP2):
                    nk = P * (p + 1)
                    for j in range(4):
                        dve.wait_ge(*c.empty(("score", l, p, j)))
                        for i in range(2):
                            h = 2 * (2 * (j // 2) + i) + j % 2
                            prev = k["admit"][:, P * p:P * p + nk] if h == 0 else score[p][:, 0:nk]
                            dve.wait_ge(*ve.last())
                            stt(out=score[p][:, 0:nk], in0=relu[:, (4 * p + j) % 2, i, 0:nk], scalar=iw[:, 8 * p + h:8 * p + h + 1],
                                        in1=prev, op0=ALU.mult, op1=ALU.add).then_inc(*ve.count("scored", (l, 4 * p + j)))
                norm_vector(ve, ("mem", l), memn, v["norm_mem"][:, 8 * l:8 * l + 8], root, memn, KT, T)
                split_vector(ve, ("mem", l), memn[:, :, :], mem_x[0][:, :, :], mem_x[1][:, :, :])
                for p in range(NP2):
                    nk = P * (p + 1)
                    for n in range(TOPK // 8):
                        src = score[p] if n == 0 else work
                        dve.wait_ge(*ve.last())
                        nc.vector.max(m8, src[:, 0:nk]).then_inc(*ve.count())
                        dve.wait_ge(*ve.last())
                        nc.vector.match_replace(work[:, 0:nk], m8, src[:, 0:nk], TAKEN).then_inc(*ve.count())
                    dve.wait_ge(*ve.last())
                    ts(negm[p][:, 0:nk], work[:, 0:nk], 10 * NEG * 1e7, -NEG, ALU.is_le, ALU.mult).then_inc(*ve.count())
                    dve.wait_ge(*ve.last())
                    ts(negm[p][:, 0:nk], negm[p][:, 0:nk], NEG, None, ALU.add).then_inc(*ve.count())
                att_vector(ve, ("sa", l), sa_units(l), P_of, mx, smx, P ** -0.5)
                dve.wait_ge(*c.at("sparse_done", l))
                split_vector(ve, ("late", l), hn[:, :, :], late_x[0][:, :, :], late_x[1][:, :, :])
                split_gemm_rest(ve, stream, f"xq{l}", ring, mem_w, tt)
                att_vector(ve, ("xa", l), xa_units(l), P_of, mx, smx, 1.0 / 16)
                split_gemm_rest(ve, stream, f"gates{l}", ring, gates_w, tt)
                s0 = stream.split[f"branch{l}"]
                _, g0, _, _, _ = stream.phases[f"branch{l}"]
                rest_of_slab = round_low(ve, stream, f"branch{l}", ring, gates_w, tt)
                for q in range(3):
                    rest_of_slab(q, 0)
                dve.wait_ge(*c.empty((f"gates{l}", l, 23)))
                for n in range(KT):
                    for b in range(3):
                        i = 3 * n + b
                        dve.wait_ge(c.sem("split_used"), s0 + i + 1)
                        dst = merged[:, n, :] if b == 0 else branch_tmp[:, b - 1, :]
                        if b:
                            dve.wait_ge(*ve.last())
                        tt(dst, c.banks[(g0 + i) % RING][:, 0:T], A[:, 8 * b + n, :], ALU.mult).then_inc(*ve.emptied(("branch", l, i)))
                        if i + 3 < 3 * KT:
                            rest_of_slab(i + 3, 0)
                    for b in range(2):
                        dve.wait_ge(*ve.last())
                        tt(merged[:, n, :], merged[:, n, :], branch_tmp[:, b, :], ALU.add).then_inc(*ve.count("merged", (l, n)))
                    dve.wait_ge(*ve.last())
                    copy(merged_x[0][:, n, :], merged[:, n, :]).then_inc(*ve.count())
                    dve.wait_ge(*ve.last())
                    tt(merged_x[1][:, n, :], merged[:, n, :], merged_x[0][:, n, :], ALU.subtract).then_inc(*ve.count("merged_split", (l, n)))
                def add_x(i, ps):
                    return tt(x[:, i, :], x[:, i, :], ps[:, 0:T], ALU.add)
                split_gemm_rest(ve, stream, f"out{l}", ring, gates_w, tt)
                split_gemm_read(ve, stream, f"out{l}", l, add_x)
                dve.wait_ge(*ve.last())
                nc.vector.memset(tick[:, 0:1], 0.0).then_inc(*ve.count("x_new", (l, "out")))
                norm_vector(ve, ("ffn", l), x, v["norm_ffn"][:, 8 * l:8 * l + 8], root, hn, KT, T)
                split_vector(ve, ("ffn", l), hn[:, :, :], ffn_x[0][0][:, :, :], ffn_x[0][1][:, :, :])
                ffn_vector(ve, stream, f"ffn{l}", l, ring, ffn_w, silu, exact, hidden, tick, FT)
                dve.wait_ge(*summed(f"ffn{l}"))
                for b in range(4):
                    xx = x[:, 2 * b:2 * b + 2, :]
                    tt(xx, xx, c.banks[b][:, :].rearrange("p (a t) -> p a t", a=2), ALU.add).then_inc(*ve.emptied((l, "ffn", b)))
                dve.wait_ge(*ve.last())
                nc.vector.memset(tick[:, 0:1], 0.0).then_inc(*ve.count("x_new", (l, "ffn")))
            norm_vector(ve, "final", x, v["norm_final"], root, H, KT, T)
            dve.wait_ge(*ve.last())
            tt(lamb[:, 0:1], v["lam"][:, 0:1], v["lam"][:, 1:2], ALU.mult).then_inc(*ve.count())
            tt(lamb[:, 1:2], v["lam"][:, 2:3], v["lam"][:, 3:4], ALU.mult).then_inc(*ve.count("lam_prod", "all"))
            g = stream.phases[f"mod{DEPTH - 1}2"][1] + 6
            dve.wait_ge(c.sem(f"slab_done{g % RING}"), g // RING + 1)
            tt(mods[:, :, :, :].rearrange("p l n s -> p (l n) s"),
               c.banks[BANKS - 1][:, 0:2 * DEPTH * MODS].rearrange("p (n s) -> p n s", s=2),
               v["mod_b"].unsqueeze(2).to_broadcast([P, DEPTH * MODS, 2]), ALU.add).then_inc(*ve.emptied("mods"))
            dve.wait_ge(*c.empty("lam"))
            dve.wait_ge(*ve.last())
            stt(out=lamb[:, 4:5], in0=lamb[:, 2:3], scalar=LAM_INIT, in1=lamb[:, 3:4], op0=ALU.add, op1=ALU.subtract).then_inc(*ve.count())
            for n, (l, at, g) in enumerate(((0, 1, "norm1"), (0, 4, "norm2"), (1, 1, "norm1"), (1, 4, "norm2"))):
                for s in range(2):
                    stt(out=gains[:, 2 * n + s, :], in0=mod(l, at, s), scalar=1.0, in1=v[g][:, 8 * l:8 * l + 8], op0=ALU.add, op1=ALU.mult).then_inc(*ve.count())
            dve.wait_ge(*ve.last())

            def streams(n, l, at):
                return [(slice(s * T, (s + 1) * T), gains[:, 2 * n + s, :], mod(l, at, s)) for s in range(2)]

            def gated_add(l, at, n, ps, ss=(0, 1)):
                for s in ss:
                    hh = H[:, n, s * T:(s + 1) * T]
                    ins = stt(out=hh, in0=ps[:, s * T:(s + 1) * T], scalar=mods[:, l, 8 * at + n, s:s + 1], in1=hh, op0=ALU.mult, op1=ALU.add)
                return ins
            norm_vector(ve, "e1", H, None, root, hn2, KT, T2, streams(0, 0, 0))
            split_vector(ve, "e1", hn2, even_x[0][:, :, :], even_x[1][:, :, :])
            split_gemm_rest(ve, stream, "even_in", ring, even_w, tt)
            for j in range(6):
                dve.wait_ge(*c.full(("axial", j)))
                ps = c.bank(("axial", j))
                t = att_p2[:, j % 3, 0, :].rearrange("p (a t) -> p a t", a=2)
                xx = Z[:, 2 + 2 * j:4 + 2 * j, 0:T]
                wide = lambda a: a.unsqueeze(1).to_broadcast([P, 2, T])
                tt(t, ps[:, :].rearrange("p (a t) -> p a t", a=2), wide(sin2), ALU.mult).then_inc(*ve.emptied(("axial", j)))
                tt(xx, xx, wide(cos2), ALU.mult).then_inc(*ve.count())
                dve.wait_ge(*ve.last())
                tt(xx, xx, t, ALU.add).then_inc(*ve.count("axial_done", j))
            u, sa, sb_ = pools
            dve.wait_ge(*c.at("pools_cleared", "all"))
            zz = Z[:, 0:2, :].rearrange("p s (e t) -> p s e t", e=2)
            for s in range(2):
                ins = copy(u[:, s, :, 8:264], zz[:, s])
            ins.then_inc(*ve.count())
            dve.wait_ge(*ve.last())
            two_rows = (slice(0, 64), slice(64, 128))
            for s in range(2):
                ins = tt(sa[:, s, :, 1:272], u[:, s, :, 0:271], u[:, s, :, 1:272], ALU.add)
            ins.then_inc(*ve.count())
            dve.wait_ge(*ve.last())
            for s in range(2):
                ins = tt(sb_[:, s, :, 2:271], sa[:, s, :, 1:270], sa[:, s, :, 3:272], ALU.add)
            ins.then_inc(*ve.count())
            dve.wait_ge(*ve.last())
            tt(sa[:, 1, :, 4:269], sb_[:, 1, :, 2:267], sb_[:, 1, :, 6:271], ALU.add).then_inc(*ve.count())
            dve.wait_ge(*ve.last())
            r = two_rows[1]
            tt(sb_[r, 1, :, 8:264], sa[r, 1, :, 4:260], sa[r, 1, :, 12:268], ALU.add).then_inc(*ve.count())
            dve.wait_ge(*ve.last())
            for s in range(2):
                for r, a in zip(two_rows, (sa, sb_)):
                    inv = rope[r, 2 + s:3 + s, :].to_broadcast([64, 2, T])
                    ins = tt(a[r, s, :, 8:264], a[r, s, :, 8:264], inv, ALU.mult)
            ins.then_inc(*ve.count())
            dve.wait_ge(*ve.last())
            for s in range(2):
                for r, a in zip(two_rows, (sa, sb_)):
                    ins = tt(zz[r, s], a[r, s, :, 8:264], zz[r, s], ALU.subtract)
            ins.then_inc(*ve.count("pooled", "all"))
            for j in range(2):
                dve.wait_ge(*c.full(("pool", j)))
                ps = c.bank(("pool", j))
                ts(Z[:, j, :], ps[:, :], v["pool_scale"][:, j:j + 1], None, ALU.mult).then_inc(*ve.emptied(("pool", j)))
            dve.wait_ge(*ve.last())
            att_vector(ve, "diff", diff_units(), lambda u: att_p2[:, u % 3], mx2, smx2, 64 ** -0.5, combine=lamb[:, 4:5])
            for h in range(DH):
                dve.wait_ge(*c.empty(("heads", h)))
                nc.vector.reciprocal(hn2[:, h, :], hn2[:, h, :]).then_inc(*ve.count())
                dve.wait_ge(*ve.last())
                stt(out=Z[:, 2 + h, :], in0=Z[:, 2 + h, :], scalar=1.0 - LAM_INIT, in1=hn2[:, h, :], op0=ALU.mult, op1=ALU.mult).then_inc(*ve.count("heads_normed", "all"))
            for i in range(KT):
                tag = ("even_out", 0, i)
                _, g0, _, _, _ = stream.phases["even_out"]
                g = g0 + i
                dve.wait_ge(c.sem(f"slab_done{g % RING}"), g // RING + 1)
                gated_add(0, 2, i, c.banks[g % RING]).then_inc(*ve.emptied(tag))
            dve.wait_ge(*ve.last())
            nc.vector.memset(tick[:, 0:1], 0.0).then_inc(*ve.count("h_new", "e1"))
            norm_vector(ve, "e2", H, None, root, hn2, KT, T2, streams(1, 0, 3))
            for n in range(2):
                split_vector(ve, ("e2", n), hn2[:, :, n * T:(n + 1) * T], ffn_x[n][0][:, :, :], ffn_x[n][1][:, :, :])
            for n in range(2):
                ffn_vector(ve, stream, f"even_ffn{n}", ("even", n), ring, ffn_w, silu, exact, hidden, tick, FT)
                dve.wait_ge(*summed(f"even_ffn{n}"))
                for b in range(4):
                    for j in range(2):
                        hh = H[:, 2 * b + j, n * T:(n + 1) * T]
                        ins = stt(out=hh, in0=c.banks[b][:, j * T:(j + 1) * T], scalar=mods[:, 0, 40 + 2 * b + j, n:n + 1], in1=hh, op0=ALU.mult, op1=ALU.add)
                    ins.then_inc(*ve.emptied((("even", n), "ffn", b)))
            dve.wait_ge(*ve.last())
            nc.vector.memset(tick[:, 0:1], 0.0).then_inc(*ve.count("h_new", "e2"))
            norm_vector(ve, "o1", H, None, root, hn2, KT, T2, streams(2, 1, 0))
            norm_vector(ve, "cq", Zo, v["q_norm"], root, cqn, 4, T)
            norm_vector(ve, "ckv", Zo[:, 4:6, :], v["kv_norm"], root, ckvn, 2, T2)
            for j in range(2):
                dve.wait_ge(*c.full(("axq", j)))
                ps = c.bank(("axq", j))
                t = att_p3[:, j, 0, :].rearrange("p (a t) -> p a t", a=2)
                xx = QN[:, 8 + 2 * j:10 + 2 * j, :]
                tt(t, ps[:, :].rearrange("p (a t) -> p a t", a=2), wide(sin2), ALU.mult).then_inc(*ve.emptied(("axq", j)))
                tt(xx, xx, wide(cos2), ALU.mult).then_inc(*ve.count())
                dve.wait_ge(*ve.last())
                tt(xx, xx, t, ALU.add).then_inc(*ve.count())
            dve.wait_ge(*c.full("axk"))
            ps = c.bank("axk")
            t = att_p3[:, 2, 0, 0:T]
            tt(t, ps[:, 0:T], sin2, ALU.mult).then_inc(*ve.emptied("axk"))
            tt(Zo[:, 6, 0:T], Zo[:, 6, 0:T], cos2, ALU.mult).then_inc(*ve.count())
            dve.wait_ge(*ve.last())
            tt(Zo[:, 6, 0:T], Zo[:, 6, 0:T], t, ALU.add).then_inc(*ve.count("axial2_done", "all"))
            dve.wait_ge(*ve.last())
            att_vector(ve, "latent", latent_units(), lambda u: att_p3[:, u % 3], mx2, smx2, 192 ** -0.5)
            gemm_read(ve, stream, "odd_out", 0, lambda i, ps: gated_add(1, 2, i, ps, (0,)))
            dve.wait_ge(*ve.last())
            nc.vector.memset(tick[:, 0:1], 0.0).then_inc(*ve.count("h_new", "o1"))
            norm_vector(ve, "o2", H, None, root, hn, KT, T, streams(3, 1, 3)[0:1])
            split_vector(ve, "o2", hn[:, :, :], ffn_x[0][0][:, :, :], ffn_x[0][1][:, :, :])
            dve.wait_ge(*c.full("router"))
            ps = c.bank("router")
            lg = rout[:, 16:32].rearrange("p (a e) -> p a e", a=2)
            copy(lg, ps[:, 0:16].rearrange("p (a e) -> p a e", a=2)).then_inc(*ve.emptied("router"))
            dve.wait_ge(*ve.last())
            nc.vector.tensor_reduce(rout[:, 32:34], lg, AXX, ALU.max).then_inc(*ve.count())
            dve.wait_ge(*ve.last())
            ts(rout[:, 32:34], rout[:, 32:34], -1.0, None, ALU.mult).then_inc(*ve.count("router_max", "all"))
            dve.wait_ge(*c.at("router_exp", "all"))
            nc.vector.reciprocal(rout[:, 34:36], rout[:, 34:36]).then_inc(*ve.count())
            dve.wait_ge(*ve.last())
            for p in range(NP2):
                ins = ts(lg[:, p, :], lg[:, p, :], rout[:, 34 + p:35 + p], None, ALU.mult)
            ins.then_inc(*ve.count())
            higher = rout[:, 40:56].rearrange("p (a e) -> p a e", a=2)
            nc.vector.memset(rout[:, 40:56], 0.0).then_inc(*ve.count())
            for j in range(NE):
                for p in range(NP2):
                    dve.wait_ge(*ve.last())
                    stt(out=higher[:, p, :], in0=lg[:, p, :], scalar=lg[:, p, j:j + 1], in1=higher[:, p, :], op0=ALU.is_lt, op1=ALU.add).then_inc(*ve.count())
                    if j < NE - 1:
                        dve.wait_ge(*ve.last())
                        stt(out=higher[:, p, j + 1:], in0=lg[:, p, j + 1:], scalar=lg[:, p, j:j + 1], in1=higher[:, p, j + 1:], op0=ALU.is_equal, op1=ALU.add).then_inc(*ve.count())
            dve.wait_ge(*ve.last())
            ww = rout[:, 0:16].rearrange("p (a e) -> p a e", a=2)
            stt(out=ww, in0=higher, scalar=2.0, in1=lg, op0=ALU.is_lt, op1=ALU.mult).then_inc(*ve.count())
            dve.wait_ge(*ve.last())
            nc.vector.tensor_reduce(rout[:, 36:38], ww, AXX, ALU.add).then_inc(*ve.count())
            dve.wait_ge(*ve.last())
            nc.vector.reciprocal(rout[:, 36:38], rout[:, 36:38]).then_inc(*ve.count())
            dve.wait_ge(*ve.last())
            for p in range(NP2):
                ins = ts(ww[:, p, :], ww[:, p, :], rout[:, 36 + p:37 + p], None, ALU.mult)
            ins.then_inc(*ve.count("routed", "all"))
            dve.wait_ge(*c.empty(("spread", 3)))
            ffn_vector(ve, stream, "moe", "moe", ring, ffn_w, silu, exact, hidden, tick, FT * NE, weight=lambda e: tile_of(expert_w, e))
            dve.wait_ge(*summed("moe"))
            for b in range(4):
                gated_add(1, 5, 2 * b, c.banks[b][:, 0:T], (0,))
                gated_add(1, 5, 2 * b + 1, c.banks[b][:, T:2 * T], (0,)).then_inc(*ve.emptied(("moe", "ffn", b)))
            dve.wait_ge(*ve.last())
            nc.vector.memset(tick[:, 0:1], 0.0).then_inc(*ve.count("h_new", "moe"))
            norm_vector(ve, "last", H, v["final_2"], root, x, KT, T)
            dve.wait_ge(*ve.last())
            nc.vector.memset(tick[:, 0:1], 0.0).then_inc(*ve.count("result", "x"))
    return c.found

def slabs(w, rows=None):
    kt, n = w.shape[0] // P, w.shape[1] // P
    return np.ascontiguousarray(w.reshape(kt, P, n, P).transpose(2, 1, 0, 3)).reshape(n, P, kt * P)


def features_first(a):
    return np.ascontiguousarray(np.asarray(a).T.reshape(-1, P, a.shape[0]).transpose(1, 0, 2))


def columns(a):
    return np.asarray(a).reshape(-1, P).T


def lay_out(i):
    sizes = (1024, 1024, 1024, 1024, 8, 8, 1024, 1024, 1024, 512, 64, 8, 1024, 3072)
    at = np.concatenate([[0], np.cumsum(sizes)])
    out = {}
    w_in = []
    for l in range(DEPTH):
        w = np.asarray(i["w_in"])[l]
        part = [w[:, at[n]:at[n + 1]] for n in range(len(sizes))]
        dq, dk, dv, dz, db, da, sq, sk, sv, iq, ik, iw, xq, gl = part
        narrow = np.zeros((D, P), np.float32)
        narrow[:, 0:64], narrow[:, 64:72], narrow[:, 72:80], narrow[:, 80:88] = ik, db, da, iw
        w_in.append(slabs(np.concatenate([dq, dk, dv, dz, narrow, sq, sk, sv, iq, xq, gl], axis=1)))
    out["w_in"] = np.stack(w_in)
    out["w_mem"] = np.stack([slabs(np.asarray(i["w_mem_kv"])[l]) for l in range(DEPTH)])
    wb = np.asarray(i["w_branch"])
    out["w_branch"] = np.stack([np.stack([slabs(wb[l, b]) for b in range(3)], axis=1).reshape(24, P, SLAB)
                                for l in range(DEPTH)])
    out["w_out"] = np.stack([slabs(np.asarray(i["w_out"])[l]) for l in range(DEPTH)])
    out["w_ffn"] = np.stack([ffn_slabs([np.asarray(i["w_ffn_in"])[l][:, :F_HID]], [np.asarray(i["w_ffn_in"])[l][:, F_HID:]],
                                       [np.asarray(i["w_ffn_out"])[l]]) for l in range(DEPTH)])
    out["x"] = features_first(np.asarray(i["x"])[0])
    out["mem"] = features_first(np.asarray(i["mem"])[0])
    out["pos"] = np.asarray(i["positions"]).reshape(1, T)
    conv = np.asarray(i["conv_w"])
    per_layer = lambda a: np.concatenate([columns(np.asarray(a)[l]) for l in range(DEPTH)], axis=1)
    rows = lambda a: np.broadcast_to(np.asarray(a).reshape(1, -1), (P, 16))
    second = lambda n: np.asarray(i[n + "_2"])
    out["mod_w"] = np.stack([slabs(second("mod_w")[l]) for l in range(DEPTH)])
    out["even_in"] = slabs(second("even_w_in")[0])
    out["even_out"] = slabs(second("even_w_out")[0])
    out["even_ffn"] = ffn_slabs(*([second(n)[0]] for n in ("ffn_w_gate", "ffn_w_up", "ffn_w_down")))
    odd = second("odd_w_in")[0]
    out["odd_in"] = slabs(np.concatenate([odd[:, 0:832], odd[:, 768:832]], axis=1))
    uq = second("w_uq")[0].reshape(512, MH, 192)
    out["w_uq"] = slabs(np.concatenate([uq[:, :, 0:128].reshape(512, D), uq[:, :, 128:].reshape(512, 512)], axis=1))
    ukv = second("w_ukv")[0].reshape(256, MH, 256)
    out["w_ukv"] = slabs(np.concatenate([ukv[:, :, 0:128].reshape(256, D), ukv[:, :, 128:].reshape(256, D)], axis=1))
    out["odd_out"] = slabs(second("odd_w_out")[0])
    gate, up, down = (second(n)[0] for n in ("moe_w_gate", "moe_w_up", "moe_w_down"))
    out["moe"] = ffn_slabs(gate, up, down)
    out["ctx"] = features_first(second("ctx")[0])
    out["tables2"], out["rot_ax"] = TABLES_2, ROT_AX
    pool = second("pool_w")[0]
    out["pool_w"] = np.zeros((P, 2 * P), np.float32)
    for g in range(4):
        r = 64 * (g % 2)
        out["pool_w"][r:r + 64, P * (g // 2) + r:P * (g // 2) + r + 64] = pool[g]
    lam = np.zeros((P, 4), np.float32)
    for j, n in enumerate(("lambda_q1", "lambda_k1", "lambda_q2", "lambda_k2")):
        lam[0:64, j] = second(n)[0]
    vec = dict(
        cond=np.stack([columns(second("c")[0]), columns(second("c_ctx"))], axis=2).reshape(P, 16),
        norm1=per_layer(i["norm1_g_2"]), norm2=per_layer(i["norm2_g_2"]), mod_b=per_layer(i["mod_b_2"]),
        pool_scale=columns(second("pool_scale")[0]), lam=lam, q_norm=columns(second("q_norm_g")[0]),
        kv_norm=columns(second("kv_norm_g")[0]), final_2=columns(second("final_norm_g")),
        router=second("router_w")[0].reshape(KT, P, NE).transpose(1, 0, 2).reshape(P, 64),
        norm_mix=per_layer(i["norm_mix"]), norm_mem=per_layer(i["norm_mem"]), norm_ffn=per_layer(i["norm_ffn"]),
        norm_final=columns(i["norm_final"]), dn_norm=per_layer(i["dn_norm"]),
        conv=np.concatenate([conv[l].reshape(4, 24, P).transpose(2, 1, 0).reshape(P, 96) for l in range(DEPTH)], axis=1),
        b_gate=per_layer(i["b_gate"]), a_log=rows(i["a_log"]), dt_bias=rows(i["dt_bias"]))
    out["vecs"] = np.ascontiguousarray(np.concatenate([vec[n] for n in VEC_WIDTHS], axis=1))
    out["consts"] = CONSTS
    return out


def ffn_slabs(gate, up, down):
    gate, up = [np.concatenate([slabs(w) for w in ws]) for ws in (gate, up)]
    down = np.concatenate([w.reshape(FT, P, D) for w in down])
    tiles = np.stack([gate[1:], up[1:], down[:-1]], axis=1).reshape(-1, P, SLAB)
    return np.concatenate([gate[:1], up[:1], tiles, down[-1:]])


def declare(nc, shapes, y_shape=(P, KT, T)):
    dram = {n: nc.dram_tensor(f"in_{n}", s, mybir.dt.from_np(t), kind="ExternalInput").ap()
            for n, (s, t) in shapes.items()}
    dram["y"] = nc.dram_tensor("y", y_shape, F32, kind="ExternalOutput").ap()
    return dram


def kernel(**inputs):
    import concourse.bacc as _bacc
    from concourse.bass_utils import run_bass_kernel_spmd as _run

    arrays = lay_out(inputs)
    shapes = {n: (a.shape, a.dtype) for n, a in arrays.items()}
    known = {}
    for _ in range(2):
        nc = _bacc.Bacc("TRN2", target_bir_lowering=False, num_devices=1)
        known = program(nc, declare(nc, shapes), known)
    r = _run(nc, [{f"in_{n}": a for n, a in arrays.items()}], core_ids=[0])
    y = r.results[0]["y"]
    return y.transpose(1, 0, 2).reshape(D, T).T.reshape(1, T, D)
```
